# Optimizing a Trainium2 kernel written in Bass

```python
import math
import jax, jax.numpy as jnp
from jax import lax
import numpy as np

D_MODEL = 1024
BATCH = 1
SEQ = 1024
DEPTH = 1
DEC_BATCH = 1
DEC_SEQ = 1024
PAST_LEN = 128

GRID_W = 64
N_ATTN_HEADS = 8
ATTN_HEAD_DIM = 64
D_ATTN = N_ATTN_HEADS * ATTN_HEAD_DIM
WIN_ROWS_MAX = 8
WIN_COLS = 16
D_SSD = D_MODEL
SSD_HEAD_DIM = 64
N_SSD_HEADS = D_SSD // SSD_HEAD_DIM
SSD_GROUPS = 2
SSD_HEADS_PER_GROUP = N_SSD_HEADS // SSD_GROUPS
SSD_STATE = 128
SSD_CONV_W = 5
SSD_CHUNK = 128
D_XBC = D_SSD + 2 * SSD_GROUPS * SSD_STATE
DT_MIN = 1e-3
DT_MAX = 1e-1
D_MIX = D_ATTN + D_SSD
D_IN = 3 * D_ATTN + D_SSD + D_XBC + 2 * N_SSD_HEADS
D_FF = 2816
FFN_CONV_W = 3
EPS = 1e-6

kernel_name = 'hybrid_natten_ssd_encoder'

def rms_norm(x, g):
    xf = x.astype(jnp.float32)
    y = xf * lax.rsqrt(jnp.mean(xf * xf, axis=-1, keepdims=True) + EPS)
    return (y * g.astype(jnp.float32)).astype(x.dtype)

def depthwise_conv(x, w, b):
    pad = w.shape[0] // 2
    y = lax.conv_general_dilated(x, w[:, None, :].astype(x.dtype), window_strides=(1,),
                                 padding=[(pad, pad)], dimension_numbers=('NWC', 'WIO', 'NWC'),
                                 feature_group_count=x.shape[-1])
    return y + b.astype(x.dtype)

def neighbourhood_attention(q, k, v, rpb):
    b, l, h, dh = q.shape
    rows = l // GRID_W
    kr = min(WIN_ROWS_MAX, rows)
    qg = q.reshape(b, rows, GRID_W, h, dh)
    kg = k.reshape(b, rows, GRID_W, h, dh)
    vg = v.reshape(b, rows, GRID_W, h, dh)
    cols = np.arange(GRID_W)
    col_start = np.clip(cols - WIN_COLS // 2, 0, GRID_W - WIN_COLS)
    col_idx = col_start[:, None] + np.arange(WIN_COLS)[None, :]
    col_off = col_idx - cols[:, None]
    bias_cols = rpb[:, :, col_off + WIN_COLS - 1]
    scale = dh ** -0.5

    def row_block(r):
        rs = jnp.clip(r - kr // 2, 0, rows - kr)
        kb = lax.dynamic_slice_in_dim(kg, rs, kr, axis=1)[:, :, col_idx]
        vb = lax.dynamic_slice_in_dim(vg, rs, kr, axis=1)[:, :, col_idx]
        qr = lax.dynamic_index_in_dim(qg, r, axis=1, keepdims=False)
        row_off = rs + jnp.arange(kr) - r
        bias = jnp.take(bias_cols, row_off + WIN_ROWS_MAX - 1, axis=1)
        bias = bias.transpose(0, 2, 1, 3).astype(jnp.float32)
        s = jnp.einsum('bqhd,brqjhd->bhqrj', qr, kb).astype(jnp.float32) * scale + bias[None]
        p = jax.nn.softmax(s.reshape(b, h, GRID_W, kr * WIN_COLS), axis=-1)
        p = p.reshape(b, h, GRID_W, kr, WIN_COLS).astype(v.dtype)
        return jnp.einsum('bhqrj,brqjhd->bqhd', p, vb)

    out = lax.map(row_block, jnp.arange(rows))
    return out.transpose(1, 0, 2, 3, 4).reshape(b, l, h * dh)

def ssd_scan(x, dt, a, bmat, cmat):
    b, l, g, kh, p = x.shape
    n = bmat.shape[-1]
    q = SSD_CHUNK
    nc = l // q
    xdt = (x * dt[..., None]).reshape(b, nc, q, g, kh, p)
    da = (dt * a).astype(jnp.float32).reshape(b, nc, q, g, kh).transpose(0, 3, 4, 1, 2)
    bc = bmat.reshape(b, nc, q, g, n)
    cc = cmat.reshape(b, nc, q, g, n)
    a_cs = jnp.cumsum(da, axis=-1)
    idx = jnp.arange(q)
    lower = idx[:, None] >= idx[None, :]
    seg = a_cs[..., :, None] - a_cs[..., None, :]
    decay = jnp.exp(jnp.where(lower, seg, -jnp.inf))
    cb = jnp.einsum('bclgn,bcsgn->bgcls', cc, bc)
    y_diag = jnp.einsum('bgcls,bgkcls,bcsgkp->bclgkp', cb, decay, xdt)
    decay_states = jnp.exp(a_cs[..., -1:] - a_cs)
    states = jnp.einsum('bclgn,bgkcl,bclgkp->bcgkpn', bc, decay_states, xdt)
    states = jnp.concatenate([jnp.zeros_like(states[:, :1]), states], axis=1)
    chunk_cs = jnp.cumsum(jnp.pad(a_cs[..., -1], [(0, 0), (0, 0), (0, 0), (1, 0)]), axis=-1)
    zi = jnp.arange(nc + 1)
    seg_c = chunk_cs[..., :, None] - chunk_cs[..., None, :]
    decay_chunk = jnp.exp(jnp.where(zi[:, None] >= zi[None, :], seg_c, -jnp.inf))
    states = jnp.einsum('bgkzc,bcgkpn->bzgkpn', decay_chunk, states)[:, :-1]
    y_off = jnp.einsum('bclgn,bcgkpn,bgkcl->bclgkp', cc, states, jnp.exp(a_cs))
    return (y_diag + y_off).reshape(b, l, g, kh, p)

def ssd_mixer(z, xbc, dt_raw, conv_w, conv_b, dt_bias, a_log, d_skip, norm_g):
    b, l, _ = xbc.shape
    g, kh, p, n = SSD_GROUPS, SSD_HEADS_PER_GROUP, SSD_HEAD_DIM, SSD_STATE
    xbc = jax.nn.silu(depthwise_conv(xbc, conv_w, conv_b))
    xs = xbc[..., :D_SSD].reshape(b, l, g, kh, p)
    bm = xbc[..., D_SSD:D_SSD + g * n].reshape(b, l, g, n)
    cm = xbc[..., D_SSD + g * n:].reshape(b, l, g, n)
    dt = jax.nn.softplus(dt_raw.astype(jnp.float32).reshape(b, l, 2, g, kh)
                         + dt_bias.astype(jnp.float32).reshape(2, g, kh))
    a = -jnp.exp(a_log.astype(jnp.float32)).reshape(2, g, kh)
    flip = lambda t: jnp.flip(t, axis=1)
    y_fwd = ssd_scan(xs, dt[:, :, 0], a[0], bm, cm)
    y_bwd = flip(ssd_scan(flip(xs), flip(dt[:, :, 1]), a[1], flip(bm), flip(cm)))
    y = y_fwd + y_bwd + xs * d_skip.reshape(g, kh)[..., None]
    y = (y.reshape(b, l, D_SSD) * jax.nn.silu(z)).astype(z.dtype)
    y = rms_norm(y.reshape(b, l, g, D_SSD // g), norm_g.reshape(g, D_SSD // g))
    return y.reshape(b, l, D_SSD)

def encoder_layer(x, norm_mix_pre, norm_mix_post, w_in, attn_rpb, attn_out_norm,
                  ssd_conv_w, ssd_conv_b, ssd_dt_bias, ssd_a_log, ssd_d, ssd_norm, w_out,
                  norm_ffn_pre, norm_ffn_post, w_gate, w_up, ffn_conv_w, ffn_conv_b, w_down):
    b, l, _ = x.shape
    h = rms_norm(x, norm_mix_pre)
    proj = h @ w_in
    o = 0
    q = proj[..., o:o + D_ATTN]; o += D_ATTN
    k = proj[..., o:o + D_ATTN]; o += D_ATTN
    v = proj[..., o:o + D_ATTN]; o += D_ATTN
    z = proj[..., o:o + D_SSD]; o += D_SSD
    xbc = proj[..., o:o + D_XBC]; o += D_XBC
    dt_raw = proj[..., o:o + 2 * N_SSD_HEADS]
    hs = (b, l, N_ATTN_HEADS, ATTN_HEAD_DIM)
    attn = neighbourhood_attention(q.reshape(hs), k.reshape(hs), v.reshape(hs), attn_rpb)
    attn = rms_norm(attn, attn_out_norm)
    ssd = ssd_mixer(z, xbc, dt_raw, ssd_conv_w, ssd_conv_b, ssd_dt_bias, ssd_a_log, ssd_d, ssd_norm)
    mix = jnp.concatenate([attn, ssd], axis=-1) @ w_out
    x = x + rms_norm(mix, norm_mix_post)
    h = rms_norm(x, norm_ffn_pre)
    gate = depthwise_conv(h @ w_gate, ffn_conv_w, ffn_conv_b)
    f = (jax.nn.gelu(gate, approximate=True) * (h @ w_up)) @ w_down
    return x + rms_norm(f, norm_ffn_post)

def trunk(x, norm_mix_pre, norm_mix_post, w_in, attn_rpb, attn_out_norm,
          ssd_conv_w, ssd_conv_b, ssd_dt_bias, ssd_a_log, ssd_d, ssd_norm, w_out,
          norm_ffn_pre, norm_ffn_post, w_gate, w_up, ffn_conv_w, ffn_conv_b, w_down):
    for i in range(DEPTH):
        x = encoder_layer(x, norm_mix_pre[i], norm_mix_post[i], w_in[i], attn_rpb[i], attn_out_norm[i],
                          ssd_conv_w[i], ssd_conv_b[i], ssd_dt_bias[i], ssd_a_log[i], ssd_d[i], ssd_norm[i],
                          w_out[i], norm_ffn_pre[i], norm_ffn_post[i], w_gate[i], w_up[i],
                          ffn_conv_w[i], ffn_conv_b[i], w_down[i])
    return x

def setup_inputs(seed: int = 0) -> dict:
    key = jax.random.key(seed)
    ks = jax.random.split(key, 24)
    f32 = jnp.float32

    def nrm(k, shape, scale):
        return jax.random.normal(k, shape, f32) * scale

    def gain(k, shape):
        return 1.0 + 0.05 * jax.random.normal(k, shape, f32)

    dt0 = jnp.exp(jax.random.uniform(ks[12], (DEPTH, 2, N_SSD_HEADS), f32, math.log(DT_MIN), math.log(DT_MAX)))
    return {
        'x_prompt': nrm(ks[0], (BATCH, SEQ, D_MODEL), 1.0),
        'x_sample': nrm(ks[1], (DEC_BATCH, DEC_SEQ, D_MODEL), 1.0),
        'norm_mix_pre': gain(ks[2], (DEPTH, D_MODEL)),
        'norm_mix_post': gain(ks[3], (DEPTH, D_MODEL)),
        'w_in': nrm(ks[4], (DEPTH, D_MODEL, D_IN), D_MODEL ** -0.5),
        'attn_rpb': nrm(ks[5], (DEPTH, N_ATTN_HEADS, 2 * WIN_ROWS_MAX - 1, 2 * WIN_COLS - 1), 0.02),
        'attn_out_norm': gain(ks[6], (DEPTH, D_ATTN)),
        'ssd_conv_w': nrm(ks[7], (DEPTH, SSD_CONV_W, D_XBC), SSD_CONV_W ** -0.5),
        'ssd_conv_b': nrm(ks[8], (DEPTH, D_XBC), 0.02),
        'ssd_dt_bias': dt0 + jnp.log(-jnp.expm1(-dt0)),
        'ssd_a_log': jnp.log(jax.random.uniform(ks[9], (DEPTH, 2, N_SSD_HEADS), f32, 1.0, 16.0)),
        'ssd_d': gain(ks[10], (DEPTH, N_SSD_HEADS)),
        'ssd_norm': gain(ks[11], (DEPTH, D_SSD)),
        'w_out': nrm(ks[13], (DEPTH, D_MIX, D_MODEL), D_MIX ** -0.5),
        'norm_ffn_pre': gain(ks[14], (DEPTH, D_MODEL)),
        'norm_ffn_post': gain(ks[15], (DEPTH, D_MODEL)),
        'w_gate': nrm(ks[16], (DEPTH, D_MODEL, D_FF), D_MODEL ** -0.5),
        'w_up': nrm(ks[17], (DEPTH, D_MODEL, D_FF), D_MODEL ** -0.5),
        'ffn_conv_w': nrm(ks[18], (DEPTH, FFN_CONV_W, D_FF), FFN_CONV_W ** -0.5),
        'ffn_conv_b': nrm(ks[19], (DEPTH, D_FF), 0.02),
        'w_down': nrm(ks[20], (DEPTH, D_FF, D_MODEL), D_FF ** -0.5),
    }

def reference(x_prompt, x_sample, norm_mix_pre, norm_mix_post, w_in, attn_rpb, attn_out_norm,
              ssd_conv_w, ssd_conv_b, ssd_dt_bias, ssd_a_log, ssd_d, ssd_norm, w_out,
              norm_ffn_pre, norm_ffn_post, w_gate, w_up, ffn_conv_w, ffn_conv_b, w_down):
    y_prompt = trunk(x_prompt, norm_mix_pre, norm_mix_post, w_in, attn_rpb, attn_out_norm,
                     ssd_conv_w, ssd_conv_b, ssd_dt_bias, ssd_a_log, ssd_d, ssd_norm, w_out,
                     norm_ffn_pre, norm_ffn_post, w_gate, w_up, ffn_conv_w, ffn_conv_b, w_down)
    y_sample = trunk(x_sample, norm_mix_pre, norm_mix_post, w_in, attn_rpb, attn_out_norm,
                     ssd_conv_w, ssd_conv_b, ssd_dt_bias, ssd_a_log, ssd_d, ssd_norm, w_out,
                     norm_ffn_pre, norm_ffn_post, w_gate, w_up, ffn_conv_w, ffn_conv_b, w_down)
    return (y_prompt, y_sample)


_drawn_inputs = setup_inputs


def setup_inputs(seed=0):
    import zlib

    import numpy as np

    out = dict(_drawn_inputs(seed))
    spreads = {}
    factors = {'attn_rpb': 6.246, 'ssd_d': 3.333, 'ffn_conv_b': 5.063, 'ssd_conv_b': 3.192}
    for name, (base, spread) in spreads.items():
        noise = np.random.default_rng([zlib.crc32(name.encode()), seed]).standard_normal(out[name].shape)
        drawn = base * np.exp(spread * noise) if base else spread * noise
        out[name] = __import__('jax').numpy.asarray(drawn.astype(out[name].dtype))
    for name, factor in factors.items():
        out[name] = (out[name] * factor).astype(out[name].dtype)
    return out
```

```python
import concourse.bass as bass
from concourse import mybir
from contextlib import ExitStack

P = 128
SEQS = 2
T = 1024
D = 1024
KD = D // P
TT = T // P
HALF = 512
GRID_W, ROWS, KR, WIN_COLS = 64, 16, 8, 16
HEADS, DH = 8, 64
PAIRS = HEADS // 2
UNITS = PAIRS * ROWS
KEYS = KR * GRID_W
SH, SP_, GROUPS = 16, 64, 2
GH = SH // GROUPS
FF = 2816
FK = FF // P
EPS = 1e-6
MASKED = -1e30

PC = {}
_c = 0
for _name, _n in (("mix_pre", KD), ("mix_post", KD), ("attn", 4), ("ssd", KD), ("ffn_pre", KD), ("ffn_post", KD),
                  ("conv_w", 12 * 5), ("conv_b", 12), ("fconv_w", FK * 3), ("fconv_b", FK), ("dt_bias", 1), ("a_log", 1)):
    PC[_name] = _c
    _c += _n
NPARAM = _c

IN_BLOCKS, OUT_BLOCKS, GU_BLOCKS = 32, 8, 2 * FK
OUT_UNITS = (6, 6)
DOWN_UNITS = (8, 8, 6)
U_OUT = IN_BLOCKS
U_GU = U_OUT + OUT_BLOCKS * len(OUT_UNITS)
U_DOWN = U_GU + GU_BLOCKS
UNITS_W = U_DOWN + KD * len(DOWN_UNITS)
SLOTS = 4
LOADS = UNITS_W // SLOTS

STARTED = ('conv_done', 'diag_done', 'f_ready', 'gate_conv', 'gate_copied', 'gelu_done', 'in_copied', 'norm_applied', 'o_done', 'pt_done', 'rs_done', 's_done', 'silu_done', 'sq_used', 'st_done', 'sequence_saved', 'weights_used', 'yd_done', 'yo_copied', 'yo_t', 'yt_done')
H, XBC, Z, Q, K = 0, 8, 20, 28, 32
VT, VK = 16, 12
RAW = 8
B_T, C_T = XBC + 8, XBC + 10
BTOK, YBUF, SF = K, K + 2, K + 3
SB, XW = XBC, XBC + 7
FFN = XBC
ARENA = 36

NORMS = (8, 4, 4, 4, 8, 8, 8)
NSQ = sum(NORMS)
DVE_LINKS = 347


def uend(block):
    if block < 32:
        return block + 1
    if block < 40:
        return U_OUT + 2 * (block - 32) + 2
    if block < 84:
        return U_GU + block - 40 + 1
    return U_DOWN + 3 * (block - 84) + 3


def encoder(nc, x, w_in, w_dt, w_out, w_gu, w_down, params, skip, rpb, y):
    F = mybir.dt.float32
    ALU, ACT = mybir.AluOpType, mybir.ActivationFunctionType
    ctx = ExitStack()
    with ctx:
        def sb(name, shape):
            return ctx.enter_context(nc.sbuf_tensor(name, shape, F))

        def sem(name):
            return ctx.enter_context(nc.semaphore(name))

        arena = sb("arena", [P, ARENA, T])
        ring = sb("ring", [P, SLOTS, KD * P])
        tmp = sb("tmp", [P, 8 * 1028])
        rows = sb("rows", [P, T])
        scal = sb("scal", [P, TT, 96])
        wst = sb("wst", [P, TT, 32])
        ecs = sb("ecs", [P, TT, 32])
        dtot = sb("dtot", [P, TT, 32])
        ident = sb("ident", [P, P])
        ones = sb("ones", [P, P])
        upper = sb("upper", [P, P])
        lower = sb("lower", [P, P])
        last = ident[:, P - 1:P].broadcast_to([P, P])
        first = ident[:, 0:1].broadcast_to([P, P])
        prm = sb("prm", [P, NPARAM])
        hconv = sb("hconv", [P, 72])
        skp = sb("skp", [P, SH])
        wdt = sb("wdt", [P, KD * 32])
        acol = sb("acol", [P, 1])
        epsc = sb("epsc", [P, 1])
        srt = sb("srt", [P, 8])
        rst = sb("rst", [P, 8])
        mx = sb("mx", [P, 2])
        nmx = sb("nmx", [P, 2])
        rsum = sb("rsum", [P, 2])
        rinv = sb("rinv", [P, 2])
        G = ctx.enter_context(nc.psum_tensor("G", [P, 4, HALF], F))
        A = ctx.enter_context(nc.psum_tensor("A", [P, 4, HALF], F))

        qb = sb("qb", [P, 2, P])

        def t(i, n=T, o=0):
            return tmp[:, i * 1028 + o:i * 1028 + o + n]

        pbuf = t(0).rearrange("p (a n) -> p a n", a=2)
        ptbuf = t(1).rearrange("p (a n) -> p a n", a=2)
        v_even = t(6).rearrange("p (a n) -> p a n", a=8)
        v_odd = t(7, 7 * P).rearrange("p (a n) -> p a n", a=7)

        def bc(g, d):
            o = 4 * 1028 + (2 * g + d) * T
            return tmp[:, o:o + T].rearrange("p (h n) -> p h n", h=GH)

        table = t(5, 960)

        x_dram = nc.dram_tensor("x_by_channel", (P, KD, T), F, kind="Internal").ap()
        x1_dram = nc.dram_tensor("x1_by_channel", (P, KD, T), F, kind="Internal").ap()
        v_dram = nc.dram_tensor("v_by_token", (T, PAIRS * P), F, kind="Internal").ap()
        cs_dram = nc.dram_tensor("running_sums", (2, 32, T), F, kind="Internal").ap()
        pad_dram = nc.dram_tensor("padded_bias", (HEADS * 15, 127), F, kind="Internal").ap()
        bias_dram = nc.dram_tensor("bias_tables", (PAIRS, P, 960), F, kind="Internal").ap()

        names = """params_in w_ready0 w_ready1 w_ready2 w_ready3 weights_used x_in xt_done xt_out
            raw_saved h_ready sq_done sq_used srt_done diag_done rs_done norm_applied
            in_copied vt_done v_out v_saved v_in tb_in conv_done z_raw tanh_done silu_done
            dt_done dt_read exp_dt exp_dt_out rows_ready rows_saved q_ready s_done s_biased p_exp p_scaled
            pt_done pt_out o_done o_out qb_free xtok_done xtok_out scal_done scal_out tot_done tot_out
            coef_in coef_exp coef_out xw_ready st_done st_read sb_ready cb_done cb_out bc_in0 bc_in1 settled sp_settled e_ready e_exp m_ready yd_done yo_done
            y_ready yt_done yt_out sf_ready xd_ready out_copied x1_part x_back x1_ready x1_saved
            pads gate_copied gate_tap gate_conv gelu_done f_ready o2_copied x1_back y_norm yo_t yo_copied y_saved sequence_saved
            const started dve_chain scratch rpb_pad table_read table_masked table_saved"""
        S = {n: sem(n) for n in names.split()}
        w_ready = [S[f"w_ready{i}"] for i in range(4)]
        CONSTS = 14

        def start(name, k):
            assert k > 0 or name in STARTED, name
            return int(name in STARTED)

        class Chain:
            def __init__(self, eng, sm, s, total):
                self.eng, self.sm, self.s, self.total, self.n = eng, sm, s, total, 0

            def step(self, ins):
                self.n += 1
                return ins.then_inc(self.sm, 1)

            def wait(self):
                self.eng.wait_ge(self.sm, self.s * self.total + self.n)

            def link(self, ins):
                self.step(ins)
                self.wait()

        block = ctx.enter_context(nc.Block())

        @block.sync
        def _(sp):
            sp.dma_start(prm[:, :], params).then_inc(S["params_in"], 16)
            sp.dma_start(wdt[:, :], w_dt).then_inc(S["params_in"], 16)
            sp.wait_ge(S["started"], len(STARTED))
            with sp.Fori(0, SEQS) as s:
                def at(name, per, k):
                    sp.wait_ge(S[name], s * per + k + start(name, k))

                def unit(u, src, n):
                    at("weights_used", UNITS_W, max(0, u - SLOTS + 1))
                    sp.dma_start(ring[:, u % SLOTS, 0:n * P], src).then_inc(w_ready[u % SLOTS], 16)

                at("sequence_saved", 1, 0)
                sp.sem_inc(S["sp_settled"], 1)
                for i in range(TT):
                    sp.dma_start(arena[:, Z + i, :], x[bass.ds(s, 1), i * P:(i + 1) * P, :].rearrange("a p n -> (a p) n")
                                 ).then_inc(S["x_in"], 16)
                for u in range(IN_BLOCKS):
                    unit(u, w_in[u], KD)
                for b in range(OUT_BLOCKS):
                    for j, n in enumerate(OUT_UNITS):
                        unit(U_OUT + 2 * b + j, w_out[b, :, 6 * j * P:(6 * j + n) * P], n)
                for u in range(GU_BLOCKS):
                    unit(U_GU + u, w_gu[u], KD)
                for b in range(KD):
                    for j, n in enumerate(DOWN_UNITS):
                        unit(U_DOWN + 3 * b + j, w_down[b, :, 8 * j * P:(8 * j + n) * P], n)

        @block.tensor
        def _(pe):
            pe.wait_ge(S["const"], CONSTS)
            pe.wait_ge(S["params_in"], 32)
            with pe.Fori(0, SEQS) as s:
                def at(name, per, k):
                    pe.wait_ge(S[name], s * per + k + start(name, k))

                def gemm(b, units, rhs, parts=None):
                    kc, total = 0, sum(units)
                    for j, n in enumerate(units):
                        u = uend(b) - len(units) + j
                        pe.wait_ge(w_ready[u % SLOTS], (s * LOADS + u // SLOTS + 1) * 16)
                        for kk in range(n):
                            for h in range(2):
                                m = nc.tensor.matmul(G[:, 2 * (b % 2) + h, :], ring[:, u % SLOTS, kk * P:(kk + 1) * P],
                                                     rhs(kc, h), start=(kc == 0), stop=(kc == total - 1))
                            kc += 1
                        m.then_inc(S["weights_used"], 1)

                def cols(c, h):
                    return arena[:, c, h * HALF:(h + 1) * HALF]

                nsq = [0]
                nn = [0]

                def norm_pe(chunks):
                    at("norm_applied", NSQ, nsq[0])
                    for k in range(chunks):
                        nsq[0] += 1
                        at("sq_done", NSQ, nsq[0])
                        for i in range(TT):
                            m = nc.tensor.matmul(A[:, 3, i:i + 1], t(nsq[0] % 2, P, i * P), ones[:, 0:1],
                                                 start=(k == 0 and i == 0), stop=(k == chunks - 1), skip_group_check=True)
                        m.then_inc(S["sq_used"], 1)
                    nn[0] += 1
                    at("diag_done", len(NORMS), nn[0])
                    for i in range(TT):
                        m = nc.tensor.matmul(G[:, 2 + i // 4, (i % 4) * P:(i % 4 + 1) * P], ones[:, :], t(2, P, i * P),
                                             start=True, stop=True)
                    m.then_inc(S["rs_done"], 1)

                at("x_in", 16 * TT, 16 * TT)
                at("yo_copied", 16, 0)
                for i in range(16):
                    k, h = divmod(i, 2)
                    if i >= 3:
                        at("xt_out", 16, i - 2)
                    for j in range(4):
                        m = nc.tensor.transpose(A[:, i % 3, j * P:(j + 1) * P], arena[:, Z + 4 * h + j, k * P:(k + 1) * P], ident[:, :])
                    m.then_inc(S["xt_done"], 1)
                norm_pe(KD)
                at("norm_applied", NSQ, 8)
                for b in range(IN_BLOCKS // 2 - 4):
                    at("in_copied", IN_BLOCKS, max(0, b - 1))
                    gemm(b, (KD,), lambda k, h: cols(H + k, h))
                for k in range(KD):
                    for h in range(2):
                        m = nc.tensor.matmul(A[0:32, h, :], wdt[:, k * 32:(k + 1) * 32], cols(H + k, h),
                                             start=(k == 0), stop=(k == KD - 1))
                m.then_inc(S["dt_done"], 1)
                at("in_copied", IN_BLOCKS, 12)
                for i in range(TT):
                    if i >= 2:
                        at("v_out", TT, i - 1)
                    for j in range(4):
                        m = nc.tensor.transpose(A[:, 2 + i % 2, j * P:(j + 1) * P], arena[:, VT + j, i * P:(i + 1) * P], ident[:, :])
                    m.then_inc(S["vt_done"], 1)
                for b in range(12, 16):
                    at("in_copied", IN_BLOCKS, b - 1)
                    gemm(b, (KD,), lambda k, h: cols(H + k, h))
                at("v_out", TT, TT)
                at("dt_read", 1, 1)
                for st in range(UNITS + 2):
                    if st < UNITS:
                        rs = min(max(st % ROWS - KR // 2, 0), ROWS - KR)
                        at("q_ready", UNITS, st + 1)
                        if st >= 2:
                            at("s_biased", UNITS, st - 1)
                        nc.tensor.matmul(A[:, st % 2, :], qb[:, st % 2, :],
                                         arena[:, K + st // ROWS, rs * GRID_W:rs * GRID_W + KEYS],
                                         start=True, stop=True).then_inc(S["s_done"], 1)
                        b = 16 + st // 4
                        if st % 4 == 0:
                            at("in_copied", IN_BLOCKS, b - 1)
                            pe.wait_ge(w_ready[b % SLOTS], (s * LOADS + b // SLOTS + 1) * 16)
                        for kc in (2 * (st % 4), 2 * (st % 4) + 1):
                            for h in range(2):
                                m = nc.tensor.matmul(G[:, 2 * (b % 2) + h, :], ring[:, b % SLOTS, kc * P:(kc + 1) * P],
                                                     cols(H + kc, h), start=(kc == 0), stop=(kc == KD - 1))
                        if st % 4 == 3:
                            m.then_inc(S["weights_used"], 1)
                    if 1 <= st <= UNITS:
                        u = st - 1
                        at("p_scaled", UNITS, u + 1)
                        if u >= 1:
                            at("pt_out", UNITS, u)
                        for j in range(4):
                            m = nc.tensor.transpose(A[:, 2, j * P:(j + 1) * P], pbuf[:, u % 2, j * P:(j + 1) * P], ident[:, :])
                        m.then_inc(S["pt_done"], 1)
                    if st >= 2:
                        u = st - 2
                        rs = min(max(u % ROWS - KR // 2, 0), ROWS - KR)
                        at("pt_out", UNITS, u + 1)
                        at("v_in", 32 * PAIRS, 32 * (u // ROWS + 1))
                        if u >= 1:
                            at("o_out", UNITS, u)
                        for j in range(4):
                            vv = (v_even if rs % 2 == 0 else v_odd)[:, rs // 2 + j, :]
                            m = nc.tensor.matmul(A[:, 3, 0:P], vv, ptbuf[:, u % 2, j * P:(j + 1) * P], start=(j == 0), stop=(j == 3))
                        m.then_inc(S["o_done"], 1)
                at("silu_done", 20, 20)
                at("rows_ready", 1, 1)
                at("in_copied", IN_BLOCKS, 32)
                at("o_out", UNITS, UNITS)
                for c in range(TT):
                    for part in range(3):
                        i = 3 * c + part
                        if i >= 4:
                            at("xtok_out", 3 * TT, i - 3)
                        n = 4 if part < 2 else 2
                        for j in range(n):
                            m = nc.tensor.transpose(A[:, i % 4, j * P:(j + 1) * P],
                                                    arena[:, XBC + 4 * part + j, c * P:(c + 1) * P], ident[:, :])
                        if part == 2:
                            m = nc.tensor.transpose(A[:, i % 4, 2 * P:2 * P + 96], rows[0:96, c * P:(c + 1) * P], ident[0:96, 0:96])
                        m.then_inc(S["xtok_done"], 1)
                at("xtok_out", 3 * TT, 3 * TT)
                nc.tensor.matmul(G[:, 0, 0:TT * 32], last, scal[:, :, 32:64], start=True, stop=True)
                nc.tensor.matmul(G[:, 1, 0:TT * 32], first, scal[:, :, 64:96], start=True, stop=True).then_inc(S["tot_done"], 1)
                for i, c in enumerate(range(TT - 1, 0, -1)):
                    at("xw_ready", 14, i + 1)
                    at("coef_out", 1, 1)
                    if i:
                        at("st_read", 7 + 14, i)
                    for g in range(GROUPS):
                        m = nc.tensor.matmul(G[:, g, :], arena[:, BTOK + c // 4, (c % 4) * 256 + g * P:(c % 4) * 256 + (g + 1) * P],
                                             arena[:, XW, g * HALF:(g + 1) * HALF], start=True, stop=True)
                    m.then_inc(S["st_done"], 1)
                for c in range(TT):
                    if c == 0:
                        at("st_read", 7 + 14, 7)
                    if c:
                        at("cb_out", TT, c)
                        at("st_read", 7 + 14, 7 + 2 * c)
                    for g in range(GROUPS):
                        m = nc.tensor.matmul(A[:, 0, g * P:(g + 1) * P], arena[:, B_T + g, c * P:(c + 1) * P],
                                             arena[:, C_T + g, c * P:(c + 1) * P], start=True, stop=True)
                    m.then_inc(S["cb_done"], 1)
                    if c:
                        at("y_ready", TT, c)
                    if c < TT - 1:
                        at("st_read", 7 + 14, 7)
                        for g in range(GROUPS):
                            m = nc.tensor.matmul(A[:, 1 + g, :], arena[:, C_T + g, c * P:(c + 1) * P],
                                                 arena[:, SB + c, g * HALF:(g + 1) * HALF], start=True, stop=True)
                    if c:
                        at("st_read", 7 + 14, 7 + 2 * c)
                        for g in range(GROUPS):
                            m = nc.tensor.matmul(G[:, 2 + g, :], arena[:, C_T + g, c * P:(c + 1) * P],
                                                 arena[:, SF, g * HALF:(g + 1) * HALF], start=True, stop=True)
                    m.then_inc(S["yo_done"], 1)
                    if c < TT - 1:
                        at("xw_ready", 14, 7 + c + 1)
                        for g in range(GROUPS):
                            if g:
                                at("st_read", 7 + 14, 7 + 2 * c + 1)
                            nc.tensor.matmul(A[:, 3, :], arena[:, BTOK + c // 4, (c % 4) * 256 + g * P:(c % 4) * 256 + (g + 1) * P],
                                             arena[:, XW, g * HALF:(g + 1) * HALF], start=True, stop=True).then_inc(S["st_done"], 1)
                    if c:
                        at("yt_out", 2 * TT, 2 * c)
                    for g in range(GROUPS):
                        at("m_ready", 2 * TT, 2 * c + g + 1)
                        for hd in range(GH):
                            m = nc.tensor.matmul(G[:, g, hd * SP_:(hd + 1) * SP_], t(2 * g, P, hd * P),
                                                 arena[:, H + c, g * HALF + hd * SP_:g * HALF + (hd + 1) * SP_],
                                                 start=True, stop=True)
                        m.then_inc(S["yd_done"], 1)
                    at("y_ready", TT, c + 1)
                    for g in range(GROUPS):
                        for j in range(4):
                            m = nc.tensor.transpose(G[:, g, j * P:(j + 1) * P],
                                                    arena[:, YBUF, (4 * g + j) * P:(4 * g + j + 1) * P], ident[:, :])
                        m.then_inc(S["yt_done"], 1)
                at("yt_out", 2 * TT, 2 * TT)
                norm_pe(4)
                norm_pe(4)
                norm_pe(4)
                at("norm_applied", NSQ, 20)
                for b in range(32, 40):
                    if b >= 34:
                        at("out_copied", OUT_BLOCKS, b - 33)
                    gemm(b, OUT_UNITS, lambda k, h: cols(Q + k if k < 4 else Z + k - 4, h))
                at("out_copied", OUT_BLOCKS, OUT_BLOCKS)
                norm_pe(KD)
                norm_pe(KD)
                at("norm_applied", NSQ, 36)
                for b in range(40, 84):
                    p = (b - 40) // 2
                    if b % 2 == 0:
                        at("gate_copied", FK, p)
                    else:
                        at("f_ready", FK, p)
                    gemm(b, (KD,), lambda k, h: cols(H + k, h))
                for b in range(84, 92):
                    if b == 84:
                        at("f_ready", FK, FK)
                    if b >= 86:
                        at("o2_copied", KD, b - 85)
                    gemm(b, DOWN_UNITS, lambda k, h: cols(FFN + k, h))
                at("o2_copied", KD, KD)
                norm_pe(KD)
                for i in range(16):
                    tile, g = divmod(i, 2)
                    if i == 0:
                        at("norm_applied", NSQ, NSQ)
                    if i >= 3:
                        at("yo_copied", 16, i - 2)
                    for j in range(4):
                        m = nc.tensor.transpose(A[:, i % 3, j * P:(j + 1) * P],
                                                arena[:, H + 4 * g + j, tile * P:(tile + 1) * P], ident[:, :])
                    m.then_inc(S["yo_t"], 1)


        @block.scalar
        def _(act):
            act.wait_ge(S["const"], CONSTS)
            act.wait_ge(S["params_in"], 32)
            nc.scalar.mul(hconv[:, :], prm[:, PC["conv_w"]:PC["conv_w"] + 72], 0.5)
            nc.scalar.activation(acol[0:32, :], prm[0:32, PC["a_log"]:PC["a_log"] + 1], ACT.Exp).then_inc(S["scratch"], 1)
            act.wait_ge(S["scratch"], 1)
            nc.scalar.mul(acol[0:32, :], acol[0:32, :], -1.0).then_inc(S["scratch"], 1)
            with act.Fori(0, SEQS) as s:
                def at(name, per, k):
                    act.wait_ge(S[name], s * per + k + start(name, k))

                nsq = [0]
                nn = [0]

                def norm_act(sources, width, ready=None):
                    for i, c in enumerate(sources):
                        if ready:
                            ready(i)
                        nsq[0] += 1
                        at("sq_used", NSQ, max(0, nsq[0] - 2))
                        nc.scalar.activation(t(nsq[0] % 2), arena[:, c, :], ACT.Square).then_inc(S["sq_done"], 1)
                    at("sq_used", NSQ, nsq[0])
                    at("diag_done", 7, nn[0])
                    nn[0] += 1
                    nc.scalar.activation(srt[:, :], A[:, 3, 0:8], ACT.Sqrt, bias=epsc[:, :], scale=1.0 / width).then_inc(S["srt_done"], 1)

                at("norm_applied", NSQ, 0)
                for i in range(16):
                    k, h = divmod(i, 2)
                    at("xt_done", 16, i + 1)
                    nc.scalar.copy(arena[:, RAW + k, h * HALF:(h + 1) * HALF], A[:, i % 3, :]).then_inc(S["xt_out"], 1)
                norm_act(range(RAW, RAW + KD), D, lambda i: at("xt_out", 16, 2 * i + 2))

                def used(b):
                    at("weights_used", UNITS_W, uend(b))

                def psum(b):
                    return G[:, 2 * (b % 2):2 * (b % 2) + 2, :].rearrange("p a n -> p (a n)")

                for b in range(12):
                    used(b)
                    to = (Q, K, VT)[b // 4] + b % 4
                    if b < 4:
                        nc.scalar.mul(arena[:, to, :], psum(b), DH ** -0.5).then_inc(S["in_copied"], 1)
                    else:
                        nc.scalar.copy(arena[:, to, :], psum(b)).then_inc(S["in_copied"], 1)
                used(12)
                nc.scalar.copy(arena[:, Z, :], psum(12)).then_inc(S["in_copied"], 1)
                at("exp_dt", 1, 1)
                nc.scalar.activation(t(1)[0:32], t(1)[0:32], ACT.Exp, scale=-1.0).then_inc(S["exp_dt_out"], 1)
                for b in range(13, 16):
                    used(b)
                    nc.scalar.copy(arena[:, Z + b - 12, :], psum(b)).then_inc(S["in_copied"], 1)

                def tanh_half(i, c, scale):
                    at("silu_done", 20, i)
                    nc.scalar.activation(t(4), arena[:, c, :], ACT.Tanh, scale=scale).then_inc(S["tanh_done"], 1)

                for i in range(4):
                    at("in_copied", IN_BLOCKS, 13 + i)
                    tanh_half(i, Z + i, 0.5)
                at("pads", 2, 1)
                for st in range(UNITS + 10):
                    if st < UNITS:
                        at("s_biased", UNITS, st + 1)
                        nc.scalar.activation(pbuf[:, st % 2, :], pbuf[:, st % 2, :], ACT.Exp, bias=nmx[:, st % 2:st % 2 + 1],
                                             accum_out=rsum[:, st % 2:st % 2 + 1]).then_inc(S["p_exp"], 1)
                    if 1 <= st <= UNITS:
                        u = st - 1
                        at("pt_done", UNITS, u + 1)
                        at("o_done", UNITS, max(0, u - 1))
                        nc.scalar.copy(ptbuf[:, u % 2, :], A[:, 2, :]).then_inc(S["pt_out"], 1)
                    if 2 <= st < UNITS + 2:
                        u = st - 2
                        at("o_done", UNITS, u + 1)
                        r = u % ROWS
                        for hh in range(2):
                            o = nc.scalar.copy(arena[hh * 64:(hh + 1) * 64, Q + u // ROWS, r * 64:(r + 1) * 64],
                                               A[hh * 64:(hh + 1) * 64, 3, hh * 64:(hh + 1) * 64])
                        o.then_inc(S["o_out"], 1)
                    if st % 4 == 0 and 4 <= st <= UNITS:
                        m = st // 4 - 1
                        used(16 + m)
                        if m % 4 < 3:
                            j = 3 * (m // 4) + m % 4
                            at("conv_done", 12, max(0, j - 1))
                            nc.scalar.copy(t(2 + j % 2, T, 2), psum(16 + m)).then_inc(S["in_copied"], 1)
                        else:
                            nc.scalar.copy(arena[:, Z + 4 + m // 4, :], psum(16 + m)).then_inc(S["in_copied"], 1)
                    if st % 4 == 0 and 8 <= st and (st // 4 - 2) % 4 < 3 and st // 4 - 2 < 16:
                        m = st // 4 - 2
                        j = 3 * (m // 4) + m % 4
                        at("conv_done", 12, j + 1)
                        tanh_half(4 + m, XBC + j, 1.0)
                    if st % 4 == 1 and 4 < st and (st // 4 - 1) % 4 == 3 and st // 4 - 1 < 16:
                        m = st // 4 - 1
                        at("in_copied", IN_BLOCKS, 17 + m)
                        tanh_half(4 + m, Z + 4 + m // 4, 0.5)

                def broadcast_sums(c, g):
                    for d in range(2):
                        src = bass.AP(cs_dram.tensor, (d * 32 + d * SH + g * GH) * T + c * P, [[0, P], [T, GH], [1, P]])
                        act.dma_start(bc(g, d), src).then_inc(S[f"bc_in{g}"], 16)

                at("silu_done", 20, 20)
                at("o_done", UNITS, UNITS)
                at("rows_saved", 32, 32)
                for g in range(GROUPS):
                    broadcast_sums(0, g)
                for i in range(3 * TT):
                    c, part = divmod(i, 3)
                    at("xtok_done", 3 * TT, i + 1)
                    if part < 2:
                        nc.scalar.copy(arena[:, H + c, part * HALF:(part + 1) * HALF], A[:, i % 4, :]).then_inc(S["xtok_out"], 1)
                    else:
                        nc.scalar.copy(arena[:, BTOK + c // 4, (c % 4) * 256:(c % 4 + 1) * 256], A[:, i % 4, 0:256])
                        nc.scalar.copy(scal[:, c, :], A[:, i % 4, 256:352]).then_inc(S["xtok_out"], 1)
                at("coef_in", 1, 1)
                for d in range(2):
                    hs = slice(d * SH, (d + 1) * SH)
                    tot = G[:, d, 0:TT * 32].rearrange("p (c n) -> p c n", c=TT)[:, :, hs]
                    nc.scalar.activation(dtot[:, :, hs], tot, ACT.Exp)
                    nc.scalar.activation(ecs[:, :, hs], scal[:, :, 32 + d * 48:48 + d * 48], ACT.Exp)
                nc.scalar.activation(wst[:, :, :], wst[:, :, :], ACT.Exp).then_inc(S["coef_exp"], 1)
                for c in range(TT):
                    for g in range(GROUPS):
                        at("e_ready", 2 * TT, 2 * c + g + 1)
                        if c < TT - 1:
                            broadcast_sums(c + 1, g)
                        nc.scalar.activation(t(2 * g), t(2 * g), ACT.Exp).then_inc(S["e_exp"], 1)
                at("yt_out", 2 * TT, 2 * TT)
                norm_act(range(Q, Q + 4), 512)
                norm_act(range(Z, Z + 4), 512)
                norm_act(range(Z + 4, Z + 8), 512)
                for b in range(32, 40):
                    used(b)
                    nc.scalar.copy(arena[:, H + b - 32, :], psum(b)).then_inc(S["out_copied"], 1)
                norm_act(range(H, H + KD), D, lambda i: at("out_copied", 8, i + 1))
                norm_act(range(RAW, RAW + KD), D, lambda i: at("norm_applied", NSQ, 21 + i))
                at("pads", 2, 2)
                for p in range(FK):
                    used(40 + 2 * p)
                    at("gate_conv", FK, p)
                    nc.scalar.copy(t(2, T, 1), psum(40)).then_inc(S["gate_copied"], 1)
                    at("gate_conv", FK, p + 1)
                    at("f_ready", FK, p)
                    nc.scalar.activation(t(6), t(4), ACT.Gelu_apprx_tanh).then_inc(S["gelu_done"], 1)
                for b in range(84, 92):
                    used(b)
                    nc.scalar.copy(arena[:, H + b - 84, :], psum(b)).then_inc(S["o2_copied"], 1)
                norm_act(range(H, H + KD), D, lambda i: at("o2_copied", 8, i + 1))
                for i in range(16):
                    tile, g = divmod(i, 2)
                    at("yo_t", 16, i + 1)
                    nc.scalar.copy(arena[:, Z + tile, g * HALF:(g + 1) * HALF], A[:, i % 3, :]).then_inc(S["yo_copied"], 1)

        @block.vector
        def _(dve):
            dve.wait_ge(S["const"], CONSTS)
            dve.wait_ge(S["params_in"], 32)
            dve.wait_ge(S["scratch"], 2)
            with dve.Fori(0, SEQS) as s:
                def at(name, per, k):
                    dve.wait_ge(S[name], s * per + k + start(name, k))

                ch = Chain(dve, S["dve_chain"], s, DVE_LINKS)
                tt, ts, stt = nc.vector.tensor_tensor, nc.vector.tensor_scalar, nc.vector.scalar_tensor_tensor
                nn = [0]
                applied = [0]
                rs = G[:, 2:4, :].rearrange("p a n -> p (a n)")

                def col(name, k):
                    return prm[:, PC[name] + k:PC[name] + k + 1]

                def norm_dve(chunks, gain, g0, src, dst, add=None):
                    nn[0] += 1
                    at("srt_done", 7, nn[0])
                    at("rs_done", 7, nn[0] - 1)
                    ch.link(nc.vector.reciprocal(rst[:, :], srt[:, :]))
                    for i in range(TT):
                        m = ts(t(2, P, i * P), ident[:, :], rst[:, i:i + 1], None, ALU.mult)
                    m.then_inc(S["diag_done"], 1)
                    at("rs_done", 7, nn[0])
                    for k in range(chunks):
                        m = stt(arena[:, dst + k, :], arena[:, src + k, :], col(gain, g0 + k), rs, ALU.mult, ALU.mult)
                        if add is not None:
                            ch.link(m)
                            m = tt(arena[:, add[1] + k, :], arena[:, add[0] + k, :], arena[:, dst + k, :], ALU.add)
                        m.then_inc(S["norm_applied"], 1)
                        applied[0] += 1

                at("yo_t", 16, 0)
                norm_dve(KD, "mix_pre", 0, RAW, H)
                at("raw_saved", 16, 16)
                for i in range(TT):
                    at("vt_done", TT, i + 1)
                    nc.vector.tensor_copy(arena[:, VK + i // 2, (i % 2) * HALF:(i % 2 + 1) * HALF], A[:, 2 + i % 2, :]).then_inc(S["v_out"], 1)
                at("dt_done", 1, 1)
                x_, u_, z_, z2 = (t(i)[0:32] for i in (0, 1, 5, 6))
                ts(x_, A[0:32, 0:2, :].rearrange("p a n -> p (a n)"), prm[0:32, PC["dt_bias"]:PC["dt_bias"] + 1], None,
                   ALU.add).then_inc(S["dt_read"], 1)
                at("dt_read", 1, 1)
                stt(u_, x_, -1.0, x_, ALU.mult, ALU.max).then_inc(S["exp_dt"], 1)
                at("exp_dt_out", 1, 1)
                ch.link(ts(z_, u_, 2.0, None, ALU.add))
                ch.link(nc.vector.reciprocal(z_, z_))
                ch.link(tt(z_, z_, u_, ALU.mult))
                ch.link(tt(z2, z_, z_, ALU.mult))
                ch.link(ts(u_, z2, 1.0 / 17, None, ALU.mult))
                for n in range(7, 0, -1):
                    ch.link(stt(u_, u_, 1.0 / (2 * n + 1), z2, ALU.add, ALU.mult))
                ch.link(stt(z_, u_, 1.0, z_, ALU.add, ALU.mult))
                ch.link(ts(x_, x_, 0.0, None, ALU.max))
                ch.link(stt(rows[0:32, :], z_, 2.0, x_, ALU.mult, ALU.add))
                ch.link(ts(x_, rows[0:32, :], acol[0:32, :], None, ALU.mult))
                for c in range(TT):
                    da = x_[:, c * P:(c + 1) * P]
                    nc.vector.tensor_tensor_scan(rows[32:64, c * P:(c + 1) * P], ones[0:32, :], da, 0.0, ALU.mult, ALU.add)
                    m = nc.vector.tensor_tensor_scan(rows[64:96, c * P:(c + 1) * P][:, ::-1], ones[0:32, :], da[:, ::-1], 0.0,
                                                     ALU.mult, ALU.add)
                m.then_inc(S["rows_ready"], 1)

                def silu(i, c):
                    at("tanh_done", 20, i + 1)
                    stt(arena[:, c, :], t(4), 1.0, arena[:, c, :], ALU.add, ALU.mult).then_inc(S["silu_done"], 1)

                for i in range(4):
                    silu(i, Z + i)
                at("v_saved", 16, 16)
                for st in range(UNITS + 10):
                    if st < UNITS:
                        at("s_done", UNITS, st + 1)
                        at("tb_in", 16 * PAIRS, 16 * (st // ROWS + 1))
                        at("pt_done", UNITS, max(0, st - 1))
                        if st < 2:
                            at("rows_ready", 1, 1)
                        dve.sem_inc(S["settled"], 1)
                        rs0 = min(max(st % ROWS - KR // 2, 0), ROWS - KR)
                        ro = rs0 - st % ROWS + KR - 1
                        ch.link(nc.vector.tensor_tensor_reduce(
                            out=pbuf[:, st % 2, :], in0=A[:, st % 2, :], in1=table[:, ro * 64:ro * 64 + KEYS], scale=1.0,
                            scalar=-3e38, op0=ALU.add, op1=ALU.max, accum_out=mx[:, st % 2:st % 2 + 1]))
                        ts(nmx[:, st % 2:st % 2 + 1], mx[:, st % 2:st % 2 + 1], -1.0, None, ALU.mult).then_inc(S["s_biased"], 1)
                    m = st // 4 - 1
                    if 0 <= m < 16 and m % 4 < 3:
                        j = 3 * (m // 4) + m % 4
                        o, cv = arena[:, XBC + j, :], lambda i: t(2 + j % 2, T, i)
                        w = lambda i: hconv[:, 5 * j + i:5 * j + i + 1]
                        if st % 4 == 1:
                            at("in_copied", IN_BLOCKS, 17 + m)
                            ch.link(ts(o, cv(0), w(0), hconv[:, 60 + j:61 + j], ALU.mult, ALU.add))
                            ch.link(stt(o, cv(1), w(1), o, ALU.mult, ALU.add))
                        if st % 4 == 2:
                            ch.link(stt(o, cv(2), w(2), o, ALU.mult, ALU.add))
                            ch.link(stt(o, cv(3), w(3), o, ALU.mult, ALU.add))
                        if st % 4 == 3:
                            stt(o, cv(4), w(4), o, ALU.mult, ALU.add).then_inc(S["conv_done"], 1)
                    if 0 <= m < 16 and m % 4 == 3 and st % 4 == 2:
                        silu(4 + m, Z + 4 + m // 4)
                    if st % 4 == 0 and 0 <= m - 1 < 16 and (m - 1) % 4 < 3:
                        silu(4 + m - 1, XBC + 3 * ((m - 1) // 4) + (m - 1) % 4)
                    if st < UNITS:
                        at("p_exp", UNITS, st + 1)
                        ch.link(nc.vector.reciprocal(rinv[:, st % 2:st % 2 + 1], rsum[:, st % 2:st % 2 + 1]))
                        ts(pbuf[:, st % 2, :], pbuf[:, st % 2, :], rinv[:, st % 2:st % 2 + 1], None, ALU.mult).then_inc(S["p_scaled"], 1)
                at("tot_done", 1, 1)
                for d in range(2):
                    hs = slice(d * SH, (d + 1) * SH)
                    m = tt(wst[:, :, hs], G[:, d, 0:TT * 32].rearrange("p (c n) -> p c n", c=TT)[:, :, hs],
                           scal[:, :, 32 + d * 48:48 + d * 48], ALU.subtract)
                m.then_inc(S["coef_in"], 1)
                at("coef_exp", 1, 1)
                tt(wst[:, :, :], wst[:, :, :], scal[:, :, 0:32], ALU.mult).then_inc(S["coef_out"], 1)

                def per_head(coef, c, d):
                    return coef[:, c, d * SH:(d + 1) * SH].unsqueeze(2).broadcast_to([P, SH, SP_])

                def heads(ap):
                    return ap.rearrange("p (h n) -> p h n", h=SH)

                gg = G[:, 0:2, :].rearrange("p a n -> p (a n)")
                for i, c in enumerate(range(TT - 1, 0, -1)):
                    to = arena[:, SB + c - 1, :]
                    if i:
                        ch.link(tt(heads(to), heads(arena[:, SB + c, :]), per_head(dtot, c, 1), ALU.mult))
                    at("st_done", 21, i + 1)
                    if i:
                        m = tt(to, gg, to, ALU.add)
                    else:
                        m = nc.vector.tensor_copy(to, gg)
                    m.then_inc(S["st_read"], 1)
                    at("st_read", 21, i + 1)
                at("rows_saved", 32, 32)
                yb = arena[:, YBUF, :]
                for c in range(TT):
                    at("cb_done", TT, c + 1)
                    cbv = A[:, 0, 0:2 * P].rearrange("p (g n) -> p g n", g=2)
                    up, lo = rows[:, 0:256], rows[:, 256:512]
                    tt(up.rearrange("p (g n) -> p g n", g=2), cbv, upper[:, :].unsqueeze(1).broadcast_to([P, 2, P]), ALU.mult)
                    m = tt(lo.rearrange("p (g n) -> p g n", g=2), cbv, lower[:, :].unsqueeze(1).broadcast_to([P, 2, P]), ALU.mult)
                    m.then_inc(S["cb_out"], 1)
                    at("cb_out", TT, c + 1)
                    if c < TT - 1:
                        if c:
                            at("yo_done", TT, c + 1)
                            ch.link(tt(heads(arena[:, SF, :]), heads(arena[:, SF, :]), per_head(dtot, c, 0), ALU.mult))
                        for g in range(GROUPS):
                            sf = arena[:, SF, g * HALF:(g + 1) * HALF]
                            at("st_done", 21, 7 + 2 * c + g + 1)
                            if c:
                                m = tt(sf, A[:, 3, :], sf, ALU.add)
                            else:
                                m = nc.vector.tensor_copy(sf, A[:, 3, :])
                            m.then_inc(S["st_read"], 1)
                    for g in range(GROUPS):
                        at(f"bc_in{g}", 32 * TT, 32 * (c + 1))
                        at("yd_done", 2 * TT, max(0, 2 * c + g - 1))
                        E, W = t(2 * g), t(2 * g + 1)
                        for h in range(GH):
                            n = g * GH + h
                            m = ts(E[:, h * P:(h + 1) * P], bc(g, 0)[:, h, :], scal[:, c, 32 + n:33 + n], None, ALU.subtract)
                        ch.link(m)
                        for h in range(GH):
                            n = g * GH + h
                            eh = E[:, h * P:(h + 1) * P]
                            m = stt(eh, bc(g, 1)[:, h, :], scal[:, c, 80 + n:81 + n], eh, ALU.subtract, ALU.min)
                        m.then_inc(S["e_ready"], 1)
                        for h in range(GH):
                            n = g * GH + h
                            m = ts(W[:, h * P:(h + 1) * P], lo[:, g * P:(g + 1) * P], scal[:, c, 16 + n:17 + n], None, ALU.mult)
                        ch.link(m)
                        for h in range(GH):
                            n = g * GH + h
                            wh = W[:, h * P:(h + 1) * P]
                            m = stt(wh, up[:, g * P:(g + 1) * P], scal[:, c, n:n + 1], wh, ALU.mult, ALU.add)
                        ch.link(m)
                    for g in range(GROUPS):
                        at("e_exp", 2 * TT, 2 * c + g + 1)
                        tt(t(2 * g), t(2 * g), t(2 * g + 1), ALU.mult).then_inc(S["m_ready"], 1)
                    at("m_ready", 2 * TT, 2 * c + 2)
                    at("xd_ready", TT, c + 1)
                    at("yo_done", TT, c + 1)
                    if c:
                        ch.link(tt(heads(t(1)), heads(G[:, 2:4, :].rearrange("p a n -> p (a n)")), per_head(ecs, c, 0), ALU.mult))
                        ch.link(tt(yb, yb, t(1), ALU.add))
                    if c < TT - 1:
                        ch.link(tt(heads(t(1)), heads(A[:, 1:3, :].rearrange("p a n -> p (a n)")), per_head(ecs, c, 1), ALU.mult))
                        ch.link(tt(yb, yb, t(1), ALU.add))
                    at("yd_done", 2 * TT, 2 * c + 2)
                    tt(yb, gg, yb, ALU.add).then_inc(S["y_ready"], 1)
                    for g in range(GROUPS):
                        at("yt_done", 2 * TT, 2 * c + g + 1)
                        zv = arena[:, Z + 4 * g:Z + 4 * g + 4, c * P:(c + 1) * P]
                        stt(zv, G[:, g, :].rearrange("p (k n) -> p k n", k=4), 0.5, zv, ALU.mult, ALU.mult).then_inc(S["yt_out"], 1)
                norm_dve(4, "attn", 0, Q, Q)
                norm_dve(4, "ssd", 0, Z, Z)
                norm_dve(4, "ssd", 4, Z + 4, Z + 4)
                at("x_back", 16, 16)
                norm_dve(KD, "mix_post", 0, H, H, (RAW, RAW))
                norm_dve(KD, "ffn_pre", 0, RAW, H)
                at("x1_saved", 16, 16)
                for p in range(FK):
                    cv, gt = t(4), lambda i: t(2, T, i)
                    w = lambda i: prm[:, PC["fconv_w"] + 3 * p + i:PC["fconv_w"] + 3 * p + i + 1]
                    at("gate_copied", FK, p + 1)
                    at("gelu_done", FK, p)
                    ch.link(ts(cv, gt(0), w(0), prm[:, PC["fconv_b"] + p:PC["fconv_b"] + p + 1], ALU.mult, ALU.add))
                    ch.link(stt(cv, gt(1), w(1), cv, ALU.mult, ALU.add))
                    stt(cv, gt(2), w(2), cv, ALU.mult, ALU.add).then_inc(S["gate_conv"], 1)
                    at("gelu_done", FK, p + 1)
                    at("weights_used", UNITS_W, uend(41 + 2 * p))
                    tt(arena[:, FFN + p, :], rs, t(6), ALU.mult).then_inc(S["f_ready"], 1)
                at("x1_back", 16, 16)
                norm_dve(KD, "ffn_post", 0, H, H, (RAW, H))
                assert ch.n == DVE_LINKS, ch.n

        @block.gpsimd
        def _(pool):
            n = [0]

            def const(ins):
                n[0] += 1
                ins.then_inc(S["const"], 1)
                pool.wait_ge(S["const"], n[0])

            sel = nc.gpsimd.affine_select
            for name in STARTED:
                pool.sem_inc(S[name], 1)
                pool.sem_inc(S["started"], 1)
            const(nc.gpsimd.memset(ones[:, :], 1.0))
            const(nc.gpsimd.memset(qb[:, :, :], 0.0))
            const(nc.gpsimd.memset(epsc[:, :], EPS))
            const(nc.gpsimd.memset(t(0), 0.0))
            const(nc.gpsimd.memset(ident[:, :], 0.0))
            const(sel(out=ident[:, :], in_=ident[:, :], compare_op=ALU.not_equal, fill=1.0, base=0, pattern=[[-1, P]], channel_multiplier=1))
            const(sel(out=upper[:, :], in_=ones[:, :], compare_op=ALU.is_ge, fill=0.0, base=0, pattern=[[1, P]], channel_multiplier=-1))
            const(sel(out=lower[:, :], in_=ones[:, :], compare_op=ALU.is_ge, fill=0.0, base=0, pattern=[[-1, P]], channel_multiplier=1))
            pool.dma_start(pad_dram, t(0, 127)[0:HEADS * 15]).then_inc(S["rpb_pad"], 16)
            pool.dma_start(skp[:, :], bass.AP(skip.tensor, 0, [[0, P], [1, SH]])).then_inc(S["rpb_pad"], 16)
            pool.wait_ge(S["rpb_pad"], 32)
            pool.dma_start(pad_dram[:, 48:79], rpb).then_inc(S["rpb_pad"], 16)
            pool.wait_ge(S["rpb_pad"], 48)
            for h in range(HEADS):
                pool.dma_start(bass.AP(bias_dram.tensor, h * 64 * 960, [[64, 15], [960, 64], [1, 64]]),
                               bass.AP(pad_dram.tensor, h * 15 * 127 + 63, [[127, 15], [-1, 64], [1, 64]])).then_inc(S["table_read"], 16)
            pool.wait_ge(S["table_read"], 16 * HEADS)
            pool.dma_start(arena[:, 0:PAIRS, 0:960], bias_dram.rearrange("a p n -> p a n")).then_inc(S["table_read"], 16)
            pool.wait_ge(S["table_read"], 16 * HEADS + 16)
            for h in range(HEADS):
                v = arena[(h % 2) * 64:(h % 2) * 64 + 64, h // 2, 0:960].rearrange("p (a n) -> p a n", a=15)
                sel(out=v[:, :, 0:48], in_=v[:, :, 0:48], compare_op=ALU.is_ge, fill=MASKED, base=WIN_COLS // 2,
                    pattern=[[0, 15], [1, 48]], channel_multiplier=-1).then_inc(S["table_masked"], 1)
                pool.wait_ge(S["table_masked"], 2 * h + 1)
                sel(out=v[:, :, 16:64], in_=v[:, :, 16:64], compare_op=ALU.is_ge, fill=MASKED, base=WIN_COLS // 2 - 1 - 16,
                    pattern=[[0, 15], [-1, 48]], channel_multiplier=1).then_inc(S["table_masked"], 1)
                pool.wait_ge(S["table_masked"], 2 * h + 2)
            pool.dma_start(bias_dram.rearrange("a p n -> p a n"), arena[:, 0:PAIRS, 0:960]).then_inc(S["table_saved"], 16)
            pool.wait_ge(S["table_saved"], 16)
            while n[0] < CONSTS:
                const(nc.gpsimd.memset(mx[:, :], 0.0))
            with pool.Fori(0, SEQS) as s:
                def at(name, per, k):
                    pool.wait_ge(S[name], s * per + k + start(name, k))

                def settled():
                    pool.sem_inc(S["settled"], 1)

                at("xt_out", 16, 16)
                settled()
                pool.dma_start(x_dram, arena[:, RAW:RAW + KD, :]).then_inc(S["raw_saved"], 16)
                at("rs_done", 7, 1)
                settled()
                for i in (2, 3):
                    nc.gpsimd.memset(t(i, 2), 0.0)
                    m = nc.gpsimd.memset(t(i, 2, 1026), 0.0)
                m.then_inc(S["pads"], 1)
                at("v_out", TT, TT)
                at("o_done", UNITS, 0)
                settled()
                pool.dma_start(v_dram.rearrange("(i p) n -> p i n", p=P),
                               arena[:, VK:VK + 4, :].rearrange("p a (b n) -> p (a b) n", b=2)).then_inc(S["v_saved"], 16)
                at("v_saved", 16, 16)
                at("rows_ready", 1, 1)

                def load_v(hp):
                    cols = slice(hp * P, (hp + 1) * P)
                    settled()
                    pool.dma_start(v_even, v_dram[:, cols].rearrange("(i p) n -> p i n", p=P)).then_inc(S["v_in"], 16)
                    settled()
                    pool.dma_start(v_odd, v_dram[64:64 + 7 * P, cols].rearrange("(i p) n -> p i n", p=P)).then_inc(S["v_in"], 16)

                def load_table(hp):
                    settled()
                    pool.dma_start(table, bias_dram[hp]).then_inc(S["tb_in"], 16)

                load_v(0)
                load_table(0)
                pool.dma_start(cs_dram[0], rows[32:64, :]).then_inc(S["rows_saved"], 16)
                pool.dma_start(cs_dram[1], rows[64:96, :]).then_inc(S["rows_saved"], 16)
                for st in range(UNITS):
                    hp, r = divmod(st, ROWS)
                    if hp and r == 1:
                        at("s_biased", UNITS, st - 1)
                        load_table(hp)
                    if hp and r == 2:
                        at("o_done", UNITS, st - 2)
                        load_v(hp)
                    at("s_done", UNITS, max(0, st - 1))
                    if st == 0:
                        at("pads", 2, 1)
                    settled()
                    for hh in range(2):
                        m = nc.gpsimd.tensor_copy(qb[hh * 64:(hh + 1) * 64, st % 2, hh * 64:(hh + 1) * 64],
                                                  arena[hh * 64:(hh + 1) * 64, Q + hp, r * 64:(r + 1) * 64])
                    m.then_inc(S["q_ready"], 1)
                at("coef_out", 1, 1)

                def weighted(c, d):
                    nc.gpsimd.tensor_tensor(arena[:, XW, :].rearrange("p (h n) -> p h n", h=SH),
                                            arena[:, H + c, :].rearrange("p (h n) -> p h n", h=SH),
                                            wst[:, c, d * SH:(d + 1) * SH].unsqueeze(2).broadcast_to([P, SH, SP_]),
                                            ALU.mult).then_inc(S["xw_ready"], 1)

                for i, c in enumerate(range(TT - 1, 0, -1)):
                    at("st_done", 21, i)
                    weighted(c, 1)
                for c in range(TT):
                    if c < TT - 1:
                        at("st_done", 21, 7 + 2 * c)
                        weighted(c, 0)
                    at("yt_done", 2 * TT, 2 * c)
                    nc.gpsimd.tensor_tensor(arena[:, YBUF, :].rearrange("p (h n) -> p h n", h=SH),
                                            arena[:, H + c, :].rearrange("p (h n) -> p h n", h=SH),
                                            skp[:, :].unsqueeze(2).broadcast_to([P, SH, SP_]), ALU.mult).then_inc(S["xd_ready"], 1)
                at("yt_out", 2 * TT, 2 * TT)
                settled()
                pool.dma_start(arena[:, RAW:RAW + KD, :], x_dram).then_inc(S["x_back"], 16)
                at("norm_applied", NSQ, 28)
                settled()
                pool.dma_start(x1_dram, arena[:, RAW:RAW + KD, :]).then_inc(S["x1_saved"], 16)
                at("rs_done", 7, 6)
                settled()
                nc.gpsimd.memset(t(2, 1), 0.0)
                nc.gpsimd.memset(t(2, 1, 1025), 0.0).then_inc(S["pads"], 1)
                at("weights_used", UNITS_W, UNITS_W)
                settled()
                pool.dma_start(arena[:, RAW:RAW + KD, :], x1_dram).then_inc(S["x1_back"], 16)
                for i in range(TT):
                    at("yo_copied", 16, 2 * i + 2)
                    settled()
                    pool.dma_start(y[bass.ds(s, 1), i * P:(i + 1) * P, :].rearrange("a p n -> (a p) n"),
                                   arena[:, Z + i, :]).then_inc(S["y_saved"], 16)
                at("y_saved", 16 * TT, 16 * TT)
                pool.sem_inc(S["sequence_saved"], 1)
            pool.wait_ge(S["x1_saved"], 16 * SEQS)


def tiled(w):
    k, n = w.shape
    return w.reshape(k // P, P, n // P, P).transpose(2, 1, 0, 3).reshape(n // P, P, k)


def by_channel(a):
    a = a.reshape(-1, a.shape[-1] // P, P)
    return a.transpose(2, 1, 0).reshape(P, -1)


def kernel(**inputs):
    import numpy as np
    import concourse.bacc as bacc
    from concourse.bass_utils import run_bass_kernel_spmd

    a = {k: np.asarray(v) for k, v in inputs.items()}
    w_in = a["w_in"][0]
    blocks = tiled(w_in[:, :IN_BLOCKS * P])
    order = list(range(16))
    for i in range(4):
        order += [20 + 3 * i, 21 + 3 * i, 22 + 3 * i, 16 + i]
    pad = np.zeros(P - 32, np.float32)
    prm = np.concatenate([
        by_channel(a["norm_mix_pre"][0]), by_channel(a["norm_mix_post"][0]), by_channel(a["attn_out_norm"][0]),
        by_channel(a["ssd_norm"][0]), by_channel(a["norm_ffn_pre"][0]), by_channel(a["norm_ffn_post"][0]),
        by_channel(a["ssd_conv_w"][0]), by_channel(a["ssd_conv_b"][0]), by_channel(a["ffn_conv_w"][0]),
        by_channel(a["ffn_conv_b"][0]),
        np.concatenate([a["ssd_dt_bias"][0].reshape(-1), pad])[:, None],
        np.concatenate([a["ssd_a_log"][0].reshape(-1), pad])[:, None]], axis=1)
    gate, up = tiled(a["w_gate"][0]), tiled(a["w_up"][0])
    arrays = {
        "x": np.concatenate([a["x_prompt"], a["x_sample"]]),
        "w_in_tiles": blocks[order],
        "w_dt_tiles": w_in[:, IN_BLOCKS * P:].reshape(KD, P, 32).transpose(1, 0, 2).reshape(P, KD * 32),
        "w_out_tiles": tiled(a["w_out"][0]),
        "w_gu_tiles": np.stack([gate, up], axis=1).reshape(GU_BLOCKS, P, D),
        "w_down_tiles": tiled(a["w_down"][0]),
        "params": prm,
        "skip": a["ssd_d"][0],
        "rpb": a["attn_rpb"][0].reshape(HEADS * 15, 31),
    }
    arrays = {k: np.ascontiguousarray(v) for k, v in arrays.items()}
    nc = bacc.Bacc("TRN2", target_bir_lowering=False, num_devices=1)
    args = [nc.dram_tensor(k, v.shape, mybir.dt.from_np(v.dtype), kind="ExternalInput").ap() for k, v in arrays.items()]
    out = nc.dram_tensor("y", (SEQS, T, D), mybir.dt.float32, kind="ExternalOutput").ap()
    encoder(nc, *args, out)
    r = run_bass_kernel_spmd(nc, [arrays], core_ids=[0])
    y = r.results[0]["y"]
    return y[0:1], y[1:2]
```

```python
import concourse.bass as bass
from concourse import mybir
from contextlib import ExitStack

P = 128
SEQS = 2
T = 1024
D = 1024
KD = D // P
TT = T // P
HALF = 512
GRID_W, ROWS, KR, WIN_COLS = 64, 16, 8, 16
HEADS, DH = 8, 64
PAIRS = HEADS // 2
UNITS = PAIRS * ROWS
KEYS = KR * GRID_W
SH, SP_, GROUPS = 16, 64, 2
GH = SH // GROUPS
FF = 2816
FK = FF // P
EPS = 1e-6
MASKED = -1e30

PC = {}
_c = 0
for _name, _n in (("mix_pre", KD), ("mix_post", KD), ("attn", 4), ("ssd", KD), ("ffn_pre", KD), ("ffn_post", KD),
                  ("conv_w", 12 * 5), ("conv_b", 12), ("fconv_w", FK * 3), ("fconv_b", FK), ("dt_bias", 1), ("a_log", 1)):
    PC[_name] = _c
    _c += _n
NPARAM = _c

IN_BLOCKS, OUT_BLOCKS, GU_BLOCKS, DOWN_BLOCKS = 33, 8, 2 * FK, 2 * KD
DT_BLOCK = 12
B_OUT, B_GU, B_DOWN = IN_BLOCKS, IN_BLOCKS + OUT_BLOCKS, IN_BLOCKS + OUT_BLOCKS + GU_BLOCKS
BLOCKS = B_DOWN + DOWN_BLOCKS
UC = 4


def chunks_of(b):
    return 12 if B_OUT <= b < B_GU else FK if b >= B_DOWN else KD


UNIT_CHUNKS, UNITS_TO = [], [0]
for _b in range(BLOCKS):
    UNIT_CHUNKS += [min(UC, chunks_of(_b) - _k) for _k in range(0, chunks_of(_b), UC)]
    UNITS_TO.append(len(UNIT_CHUNKS))
UNITS_W = len(UNIT_CHUNKS)
RAW_SLOTS, SPLIT_SLOTS = 2, 3
LOADS = UNITS_W // RAW_SLOTS


def uend(block):
    return UNITS_TO[block + 1]


STARTED = ('diag_done', 'f_ready', 'gate_conv', 'gate_copied', 'gelu_done', 'in_copied', 'lo_split', 'norm_applied', 'o_done', 'pt_done', 'rs_done', 's_done', 'sequence_saved', 'silu_done', 'sq_used', 'st_done', 'weights_used', 'yd_done', 'yo_copied', 'yo_t', 'yt_done')
H, XBC, Z, Q, K = 0, 8, 20, 28, 32
VT, VK = 16, 12
RAW = 8
B_T, C_T = XBC + 8, XBC + 10
BTOK, YBUF, SF = K, K + 2, K + 3
SB, XW = XBC, XBC + 7
FFN = XBC
REGIONS = (8, 12, 8, 8)

H_LO = Z
MIX_HI = [k for k in range(12)]
MIX_LO = [12 + k for k in range(8)] + [Q + k for k in range(4)]
FHI = [0, 1, 2, 3, 4, 5, 6, 7, Z, Z + 1, Z + 2]
F_CHUNKS = [XBC + k for k in range(12)] + [Q + k for k in range(8)]

NORMS = (8, 4, 4, 4, 8, 8, 8)
NSQ = sum(NORMS)
NSPLIT = 8 + 12 + 8
Z_SAVES = (2, 6)
DVE_LINKS = 347

PER = {"bc_in0": 32 * TT, "bc_in1": 32 * TT, "cb_done": TT, "cb_out": TT, "coef_exp": 1, "coef_in": 1, "coef_out": 1,
       "conv_done": 12, "diag_done": len(NORMS), "dve_step": DVE_LINKS, "e_exp": 2 * TT, "e_ready": 2 * TT,
       "exp_dt": 1, "exp_dt_out": 1, "f_ready": FK, "fhi_done": 2 * FK, "flo_done": 2 * FK, "full_ready": NSPLIT,
       "gate_conv": FK, "gate_copied": FK, "gelu_done": FK, "hi_done": NSPLIT, "hi_split": UNITS_W,
       "in_copied": IN_BLOCKS, "lo_split": UNITS_W, "m_ready": 2 * TT, "norm_applied": NSQ, "o2_copied": DOWN_BLOCKS,
       "o_done": UNITS, "o_out": UNITS, "out_copied": OUT_BLOCKS, "p_exp": UNITS, "p_scaled": UNITS, "pads": 2,
       "pt_done": UNITS, "pt_out": UNITS, "q_ready": UNITS, "raw_saved": 16, "rows_ready": 1, "rows_saved": 32,
       "rs_done": len(NORMS), "s_biased": UNITS, "s_done": UNITS, "sequence_saved": 1, "silu_done": 20,
       "sq_done": NSQ, "sq_used": NSQ, "srt_done": len(NORMS), "st_done": 21, "st_read": 21, "tanh_done": 20,
       "tb_in": 16 * PAIRS, "tot_done": 1, "v_in": 32 * PAIRS, "v_out": TT, "v_saved": 16, "vt_done": TT,
       "weights_used": UNITS_W, "x1_back": 32 * KD, "x1_saved": 16, "x_back": 32, "x_in": 16 * TT, "xd_ready": TT,
       "xt_done": 16, "xt_out": 16, "xtok_done": 3 * TT, "xtok_out": 3 * TT, "xw_ready": 14, "y_ready": TT,
       "y_saved": 16 * TT, "yd_done": 2 * TT, "yo_copied": 16, "yo_done": TT, "yo_t": 16, "yt_done": 2 * TT,
       "yt_out": 2 * TT, "z_back": 16, "z_saved0": 16 * Z_SAVES[0], "z_saved1": 16 * Z_SAVES[1]}


def down_ahead(half, k):
    b = B_DOWN + half * KD
    return UNITS_TO[b - 1] + k // UC + 4 if half else UNITS_TO[b] + max(3, k // UC + 2)


def encoder(nc, x, w_in, w_out, w_gu, w_down, params, skip, rpb, y):
    F = mybir.dt.float32
    ALU, ACT = mybir.AluOpType, mybir.ActivationFunctionType
    ctx = ExitStack()
    with ctx:
        def sb(name, shape):
            return ctx.enter_context(nc.sbuf_tensor(name, shape, F))

        def sem(name):
            return ctx.enter_context(nc.semaphore(name))

        R = mybir.dt.float32r

        def twin(name, width):
            at = -(-nc.sbuf_base // 32) * 32
            full = sb(name, [P, width])
            rounded = nc.alloc_sbuf_tensor_at(name + "_rounded", [P, width], R, offset=at)
            assert nc.sbuf_base == at + 4 * width
            return full, rounded

        regions = [twin(f"arena{i}", n * T) for i, n in enumerate(REGIONS)]

        class Arena:
            def __init__(self, tensors):
                self.views = [t[:, :].rearrange("p (k n) -> p k n", k=n) for t, n in zip(tensors, REGIONS)]

            def __getitem__(self, index):
                p, k, n = index
                lo, hi = (k.start, k.stop) if isinstance(k, slice) else (k, k + 1)
                i = max(i for i in range(len(REGIONS)) if sum(REGIONS[:i]) <= lo)
                base = sum(REGIONS[:i])
                assert hi <= base + REGIONS[i]
                return self.views[i][p, slice(lo - base, hi - base) if isinstance(k, slice) else k - base, n]

        arena, arena_r = Arena([f for f, _ in regions]), Arena([r for _, r in regions])
        tmp, tmp_r = twin("small", 8 * 1028)
        raw = sb("raw", [P, RAW_SLOTS, UC * P])
        whi = ctx.enter_context(nc.sbuf_tensor("whi", [P, SPLIT_SLOTS, UC * P], R))
        wlo = ctx.enter_context(nc.sbuf_tensor("wlo", [P, SPLIT_SLOTS, UC * P], R))
        rows = sb("rows", [P, T])
        scal = sb("scal", [P, TT, 96])
        wst = sb("wst", [P, TT, 32])
        ecs = sb("ecs", [P, TT, 32])
        dtot = sb("dtot", [P, TT, 32])
        ident = sb("ident", [P, P])
        ones = sb("ones", [P, P])
        upper = sb("upper", [P, P])
        lower = sb("lower", [P, P])
        last = ident[:, P - 1:P].broadcast_to([P, P])
        first = ident[:, 0:1].broadcast_to([P, P])
        prm = sb("prm", [P, NPARAM])
        hconv = sb("hconv", [P, 72])
        skp = sb("skp", [P, SH])
        acol = sb("acol", [P, 1])
        epsc = sb("epsc", [P, 1])
        srt = sb("srt", [P, 8])
        rst = sb("rst", [P, 8])
        mx = sb("mx", [P, 2])
        nmx = sb("nmx", [P, 2])
        rsum = sb("rsum", [P, 2])
        rinv = sb("rinv", [P, 2])
        G = ctx.enter_context(nc.psum_tensor("G", [P, 4, HALF], F))
        A = ctx.enter_context(nc.psum_tensor("A", [P, 4, HALF], F))

        qb = sb("qb", [P, 2, P])

        def t(i, n=T, o=0):
            return tmp[:, i * 1028 + o:i * 1028 + o + n]

        pbuf = t(0).rearrange("p (a n) -> p a n", a=2)
        ptbuf = t(1).rearrange("p (a n) -> p a n", a=2)
        v_even = t(6).rearrange("p (a n) -> p a n", a=8)
        v_odd = t(7, 7 * P).rearrange("p (a n) -> p a n", a=7)

        def bc(g, d):
            o = 4 * 1028 + (2 * g + d) * T
            return tmp[:, o:o + T].rearrange("p (h n) -> p h n", h=GH)

        def f_full(k, cs=slice(0, T), of=None):
            if k < len(F_CHUNKS):
                return (arena if of is None else of[0])[:, F_CHUNKS[k], cs]
            o = (5 + k - len(F_CHUNKS)) * 1028
            return (tmp if of is None else of[1])[:, o:o + T][:, cs]

        def f_r(k, cs):
            return f_full(k, cs, (arena_r, tmp_r))

        def fhi(k):
            return arena_r[:, FHI[k // 2], (k % 2) * HALF:(k % 2 + 1) * HALF]

        def o_chunk(j):
            return arena[:, Z + 3 + j, :] if j < 5 else t({5: 3, 6: 7, 7: 4}[j])

        def x1_part(k, h):
            return f_full(2 * k + h)[:, 0:HALF]

        def x_back(k):
            return arena[:, K + k, :] if k < 4 else t(k - 1)

        table = t(5, 960)

        x_dram = nc.dram_tensor("x_by_channel", (P, KD, T), F, kind="Internal").ap()
        z_dram = nc.dram_tensor("gate_by_channel", (P, KD, T), F, kind="Internal").ap()
        x1_dram = nc.dram_tensor("x1_by_channel", (P, KD, T), F, kind="Internal").ap()
        v_dram = nc.dram_tensor("v_by_token", (T, PAIRS * P), F, kind="Internal").ap()
        cs_dram = nc.dram_tensor("running_sums", (2, 32, T), F, kind="Internal").ap()
        pad_dram = nc.dram_tensor("padded_bias", (HEADS * 15, 127), F, kind="Internal").ap()
        bias_dram = nc.dram_tensor("bias_tables", (PAIRS, P, 960), F, kind="Internal").ap()

        names = """params_in w_in0 w_in1 hi_split lo_split weights_used full_ready hi_done z_saved0 z_saved1 z_back fhi_done flo_done x_in xt_done xt_out
            raw_saved h_ready sq_done sq_used srt_done diag_done rs_done norm_applied
            in_copied vt_done v_out v_saved v_in tb_in conv_done z_raw tanh_done silu_done
            dt_done dt_read exp_dt exp_dt_out rows_ready rows_saved q_ready s_done s_biased p_exp p_scaled
            pt_done pt_out o_done o_out qb_free xtok_done xtok_out scal_done scal_out tot_done tot_out
            coef_in coef_exp coef_out xw_ready st_done st_read sb_ready cb_done cb_out bc_in0 bc_in1 settled sp_settled e_ready e_exp m_ready yd_done yo_done
            y_ready yt_done yt_out sf_ready xd_ready out_copied x1_part x_back x1_ready x1_saved
            pads gate_copied gate_tap gate_conv gelu_done f_ready o2_copied x1_back y_norm yo_t yo_copied y_saved sequence_saved
            const started dve_step scratch rpb_pad table_read table_masked table_saved"""
        S = {n: sem(n) for n in names.split()}
        w_in_sem = [S[f"w_in{i}"] for i in range(RAW_SLOTS)]
        CONSTS = 14

        def start(name, k):
            assert k > 0 or name in STARTED, name
            return int(name in STARTED)

        block = ctx.enter_context(nc.Block())

        @block.sync
        def _(sp):
            sp.dma_start(prm[:, :], params).then_inc(S["params_in"], 16)
            sp.wait_ge(S["started"], len(STARTED))
            with sp.Fori(0, SEQS) as s:
                def nth(name, k):
                    return s * PER[name] + k + start(name, k)

                def load(b, src):
                    for j, u in enumerate(range(UNITS_TO[b], UNITS_TO[b + 1])):
                        n = UNIT_CHUNKS[u]
                        sp.wait_ge(S["lo_split"], nth("lo_split", max(0, u - RAW_SLOTS + 1)))
                        sp.dma_start(raw[:, u % RAW_SLOTS, 0:n * P], src[:, j * UC * P:(j * UC + n) * P]
                                     ).then_inc(w_in_sem[u % RAW_SLOTS], 16)

                sp.wait_ge(S["sequence_saved"], nth("sequence_saved", 0))
                sp.sem_inc(S["sp_settled"], 1)
                for i in range(TT):
                    sp.dma_start(arena[:, Z + i, :], x[bass.ds(s, 1), i * P:(i + 1) * P, :].rearrange("a p n -> (a p) n")
                                 ).then_inc(S["x_in"], 16)
                for b in range(IN_BLOCKS):
                    load(b, w_in[b])
                for b in range(OUT_BLOCKS):
                    load(B_OUT + b, w_out[b])
                for b in range(GU_BLOCKS):
                    load(B_GU + b, w_gu[b])
                for b in range(DOWN_BLOCKS):
                    load(B_DOWN + b, w_down[b % KD])

        @block.tensor
        def _(pe):
            pe.wait_ge(S["const"], CONSTS)
            pe.wait_ge(S["params_in"], 16)
            with pe.Fori(0, SEQS) as s:
                def nth(name, k):
                    return s * PER[name] + k + start(name, k)

                def product(out, u, kk, hi, lo, first, last):
                    w = slice(kk * P, (kk + 1) * P)
                    nc.tensor.matmul(out, whi[:, u % SPLIT_SLOTS, w], hi, start=first, stop=False)
                    nc.tensor.matmul(out, whi[:, u % SPLIT_SLOTS, w], lo, start=False, stop=False)
                    return nc.tensor.matmul(out, wlo[:, u % SPLIT_SLOTS, w], hi, start=False, stop=last)

                def gemm_unit(b, j, bank, hi, lo, ready=None):
                    u, kc = UNITS_TO[b] + j, j * UC
                    pe.wait_ge(S["lo_split"], nth("lo_split", u + 1))
                    for kk in range(UNIT_CHUNKS[u]):
                        if ready:
                            ready(kc + kk)
                        for h in range(2):
                            cs = slice(h * HALF, (h + 1) * HALF)
                            m = product(G[:, 2 * bank + h, :], u, kk, arena_r[:, hi[kc + kk], cs], arena_r[:, lo[kc + kk], cs],
                                        kc + kk == 0, kc + kk == chunks_of(b) - 1)
                    m.then_inc(S["weights_used"], 1)

                def gemm(b, bank, hi, lo, ready=None):
                    for j in range(UNITS_TO[b + 1] - UNITS_TO[b]):
                        gemm_unit(b, j, bank, hi, lo, ready)

                h_hi, h_lo = [H + k for k in range(KD)], [H_LO + k for k in range(KD)]

                nsq = [0]
                nn = [0]

                def sums(k, last):
                    if k == 0:
                        pe.wait_ge(S["norm_applied"], nth("norm_applied", nsq[0]))
                    nsq[0] += 1
                    pe.wait_ge(S["sq_done"], nth("sq_done", nsq[0]))
                    for i in range(TT):
                        m = nc.tensor.matmul(A[:, 3, i:i + 1], t(nsq[0] % 2, P, i * P), ones[:, 0:1],
                                             start=(k == 0 and i == 0), stop=last, skip_group_check=True)
                    m.then_inc(S["sq_used"], 1)

                def spread():
                    nn[0] += 1
                    pe.wait_ge(S["diag_done"], nth("diag_done", nn[0]))
                    for i in range(TT):
                        m = nc.tensor.matmul(G[:, 2 + i // 4, (i % 4) * P:(i % 4 + 1) * P], ones[:, :], t(2, P, i * P),
                                             start=True, stop=True)
                    m.then_inc(S["rs_done"], 1)

                def norm_pe(chunks):
                    for k in range(chunks):
                        sums(k, k == chunks - 1)
                    spread()

                pe.wait_ge(S["x_in"], nth("x_in", 16 * TT))
                pe.wait_ge(S["yo_copied"], nth("yo_copied", 0))
                for i in range(16):
                    k, h = divmod(i, 2)
                    if i >= 3:
                        pe.wait_ge(S["xt_out"], nth("xt_out", i - 2))
                    for j in range(4):
                        m = nc.tensor.transpose(A[:, i % 3, j * P:(j + 1) * P], arena[:, Z + 4 * h + j, k * P:(k + 1) * P], ident[:, :])
                    m.then_inc(S["xt_done"], 1)
                norm_pe(KD)
                for b in range(13):
                    pe.wait_ge(S["in_copied"], nth("in_copied", max(0, b - 1)))
                    gemm(b, b % 2, h_hi, h_lo, (lambda k: pe.wait_ge(S["norm_applied"], nth("norm_applied", k + 1))) if b == 0 else None)
                pe.wait_ge(S["in_copied"], nth("in_copied", 12))
                for i in range(TT):
                    if i >= 2:
                        pe.wait_ge(S["v_out"], nth("v_out", i - 1))
                    for j in range(4):
                        m = nc.tensor.transpose(A[:, 2 + i % 2, j * P:(j + 1) * P], arena[:, VT + j, i * P:(i + 1) * P], ident[:, :])
                    m.then_inc(S["vt_done"], 1)
                for b in range(13, 17):
                    pe.wait_ge(S["in_copied"], nth("in_copied", b - 1))
                    gemm(b, b % 2, h_hi, h_lo)
                pe.wait_ge(S["v_out"], nth("v_out", TT))
                for st in range(UNITS + 2):
                    if st < UNITS:
                        rs = min(max(st % ROWS - KR // 2, 0), ROWS - KR)
                        pe.wait_ge(S["q_ready"], nth("q_ready", st + 1))
                        if st >= 2:
                            pe.wait_ge(S["s_biased"], nth("s_biased", st - 1))
                        nc.tensor.matmul(A[:, st % 2, :], qb[:, st % 2, :],
                                         arena[:, K + st // ROWS, rs * GRID_W:rs * GRID_W + KEYS],
                                         start=True, stop=True).then_inc(S["s_done"], 1)
                        b = 17 + st // 4
                        if st % 4 == 0:
                            pe.wait_ge(S["in_copied"], nth("in_copied", b - 1))
                        if st % 2 == 0:
                            gemm_unit(b, st % 4 // 2, b % 2, h_hi, h_lo)
                    if 1 <= st <= UNITS:
                        u = st - 1
                        pe.wait_ge(S["p_scaled"], nth("p_scaled", u + 1))
                        if u >= 1:
                            pe.wait_ge(S["pt_out"], nth("pt_out", u))
                        for j in range(4):
                            m = nc.tensor.transpose(A[:, 2, j * P:(j + 1) * P], pbuf[:, u % 2, j * P:(j + 1) * P], ident[:, :])
                        m.then_inc(S["pt_done"], 1)
                    if st >= 2:
                        u = st - 2
                        rs = min(max(u % ROWS - KR // 2, 0), ROWS - KR)
                        pe.wait_ge(S["pt_out"], nth("pt_out", u + 1))
                        pe.wait_ge(S["v_in"], nth("v_in", 32 * (u // ROWS + 1)))
                        if u >= 1:
                            pe.wait_ge(S["o_out"], nth("o_out", u))
                        for j in range(4):
                            vv = (v_even if rs % 2 == 0 else v_odd)[:, rs // 2 + j, :]
                            m = nc.tensor.matmul(A[:, 3, 0:P], vv, ptbuf[:, u % 2, j * P:(j + 1) * P], start=(j == 0), stop=(j == 3))
                        m.then_inc(S["o_done"], 1)
                pe.wait_ge(S["silu_done"], nth("silu_done", 20))
                pe.wait_ge(S["rows_ready"], nth("rows_ready", 1))
                pe.wait_ge(S["in_copied"], nth("in_copied", IN_BLOCKS))
                pe.wait_ge(S["o_out"], nth("o_out", UNITS))
                for c in range(TT):
                    for part in range(3):
                        i = 3 * c + part
                        if i >= 4:
                            pe.wait_ge(S["xtok_out"], nth("xtok_out", i - 3))
                        n = 4 if part < 2 else 2
                        for j in range(n):
                            m = nc.tensor.transpose(A[:, i % 4, j * P:(j + 1) * P],
                                                    arena[:, XBC + 4 * part + j, c * P:(c + 1) * P], ident[:, :])
                        if part == 2:
                            m = nc.tensor.transpose(A[:, i % 4, 2 * P:2 * P + 96], rows[0:96, c * P:(c + 1) * P], ident[0:96, 0:96])
                        m.then_inc(S["xtok_done"], 1)
                pe.wait_ge(S["xtok_out"], nth("xtok_out", 3 * TT))
                nc.tensor.matmul(G[:, 0, 0:TT * 32], last, scal[:, :, 32:64], start=True, stop=True)
                nc.tensor.matmul(G[:, 1, 0:TT * 32], first, scal[:, :, 64:96], start=True, stop=True).then_inc(S["tot_done"], 1)
                for i, c in enumerate(range(TT - 1, 0, -1)):
                    pe.wait_ge(S["xw_ready"], nth("xw_ready", i + 1))
                    pe.wait_ge(S["coef_out"], nth("coef_out", 1))
                    if i:
                        pe.wait_ge(S["st_read"], nth("st_read", i))
                    for g in range(GROUPS):
                        m = nc.tensor.matmul(G[:, g, :], arena[:, BTOK + c // 4, (c % 4) * 256 + g * P:(c % 4) * 256 + (g + 1) * P],
                                             arena[:, XW, g * HALF:(g + 1) * HALF], start=True, stop=True)
                    m.then_inc(S["st_done"], 1)
                for c in range(TT):
                    if c == 0:
                        pe.wait_ge(S["st_read"], nth("st_read", 7))
                    if c:
                        pe.wait_ge(S["cb_out"], nth("cb_out", c))
                        pe.wait_ge(S["st_read"], nth("st_read", 7 + 2 * c))
                    for g in range(GROUPS):
                        m = nc.tensor.matmul(A[:, 0, g * P:(g + 1) * P], arena[:, B_T + g, c * P:(c + 1) * P],
                                             arena[:, C_T + g, c * P:(c + 1) * P], start=True, stop=True)
                    m.then_inc(S["cb_done"], 1)
                    if c:
                        pe.wait_ge(S["y_ready"], nth("y_ready", c))
                    if c < TT - 1:
                        pe.wait_ge(S["st_read"], nth("st_read", 7))
                        for g in range(GROUPS):
                            m = nc.tensor.matmul(A[:, 1 + g, :], arena[:, C_T + g, c * P:(c + 1) * P],
                                                 arena[:, SB + c, g * HALF:(g + 1) * HALF], start=True, stop=True)
                    if c:
                        pe.wait_ge(S["st_read"], nth("st_read", 7 + 2 * c))
                        for g in range(GROUPS):
                            m = nc.tensor.matmul(G[:, 2 + g, :], arena[:, C_T + g, c * P:(c + 1) * P],
                                                 arena[:, SF, g * HALF:(g + 1) * HALF], start=True, stop=True)
                    m.then_inc(S["yo_done"], 1)
                    if c < TT - 1:
                        pe.wait_ge(S["xw_ready"], nth("xw_ready", 7 + c + 1))
                        for g in range(GROUPS):
                            if g:
                                pe.wait_ge(S["st_read"], nth("st_read", 7 + 2 * c + 1))
                            nc.tensor.matmul(A[:, 3, :], arena[:, BTOK + c // 4, (c % 4) * 256 + g * P:(c % 4) * 256 + (g + 1) * P],
                                             arena[:, XW, g * HALF:(g + 1) * HALF], start=True, stop=True).then_inc(S["st_done"], 1)
                    if c:
                        pe.wait_ge(S["yt_out"], nth("yt_out", 2 * c))
                    for g in range(GROUPS):
                        pe.wait_ge(S["m_ready"], nth("m_ready", 2 * c + g + 1))
                        for hd in range(GH):
                            m = nc.tensor.matmul(G[:, g, hd * SP_:(hd + 1) * SP_], t(2 * g, P, hd * P),
                                                 arena[:, H + c, g * HALF + hd * SP_:g * HALF + (hd + 1) * SP_],
                                                 start=True, stop=True)
                        m.then_inc(S["yd_done"], 1)
                    pe.wait_ge(S["y_ready"], nth("y_ready", c + 1))
                    for g in range(GROUPS):
                        for j in range(4):
                            m = nc.tensor.transpose(G[:, g, j * P:(j + 1) * P],
                                                    arena[:, YBUF, (4 * g + j) * P:(4 * g + j + 1) * P], ident[:, :])
                        m.then_inc(S["yt_done"], 1)
                pe.wait_ge(S["yt_out"], nth("yt_out", 2 * TT))
                norm_pe(4)
                norm_pe(4)
                norm_pe(4)
                for b in range(OUT_BLOCKS):
                    if b == 0:
                        pe.wait_ge(S["norm_applied"], nth("norm_applied", 20))
                    if b >= 2:
                        pe.wait_ge(S["out_copied"], nth("out_copied", b - 1))
                    gemm(B_OUT + b, b % 2, MIX_HI, MIX_LO)
                    if b:
                        sums(b - 1, False)
                sums(KD - 1, True)
                pe.wait_ge(S["out_copied"], nth("out_copied", OUT_BLOCKS))
                spread()
                norm_pe(KD)
                for p in range(FK):
                    pe.wait_ge(S["gate_copied"], nth("gate_copied", p))
                    gemm(B_GU + 2 * p, 0, h_hi, h_lo, (lambda k: pe.wait_ge(S["norm_applied"], nth("norm_applied", 28 + k + 1))) if p == 0 else None)
                    pe.wait_ge(S["f_ready"], nth("f_ready", p))
                    gemm(B_GU + 2 * p + 1, 1, h_hi, h_lo)
                for i in range(DOWN_BLOCKS):
                    half, j = divmod(i, KD)
                    if i == 0:
                        pe.wait_ge(S["gate_copied"], nth("gate_copied", FK))
                        pe.wait_ge(S["f_ready"], nth("f_ready", FK))
                    if i >= 2:
                        pe.wait_ge(S["o2_copied"], nth("o2_copied", i - 1))
                    b = B_DOWN + i
                    cs = slice(half * HALF, (half + 1) * HALF)
                    for u in range(UNITS_TO[b], UNITS_TO[b + 1]):
                        pe.wait_ge(S["lo_split"], nth("lo_split", u + 1))
                        for kk in range(UNIT_CHUNKS[u]):
                            k = (u - UNITS_TO[b]) * UC + kk
                            if j == 0:
                                pe.wait_ge(S["flo_done"], nth("flo_done", half * FK + k + 1))
                            m = product(G[:, 2 * (i % 2), :], u, kk, fhi(k), f_r(k, cs), k == 0, k == FK - 1)
                        m.then_inc(S["weights_used"], 1)
                    if i > KD:
                        sums(j - 1, False)
                sums(KD - 1, True)
                pe.wait_ge(S["o2_copied"], nth("o2_copied", DOWN_BLOCKS))
                spread()
                for i in range(16):
                    tile, g = divmod(i, 2)
                    if i == 0:
                        pe.wait_ge(S["norm_applied"], nth("norm_applied", NSQ))
                    if i >= 3:
                        pe.wait_ge(S["yo_copied"], nth("yo_copied", i - 2))
                    for j in range(4):
                        m = nc.tensor.transpose(A[:, i % 3, j * P:(j + 1) * P],
                                                o_chunk(4 * g + j)[:, tile * P:(tile + 1) * P], ident[:, :])
                    m.then_inc(S["yo_t"], 1)


        @block.scalar
        def _(act):
            act.wait_ge(S["const"], CONSTS)
            act.wait_ge(S["params_in"], 16)
            nc.scalar.mul(hconv[:, :], prm[:, PC["conv_w"]:PC["conv_w"] + 72], 0.5)
            nc.scalar.activation(acol[0:32, :], prm[0:32, PC["a_log"]:PC["a_log"] + 1], ACT.Exp).then_inc(S["scratch"], 1)
            act.wait_ge(S["scratch"], 1)
            nc.scalar.mul(acol[0:32, :], acol[0:32, :], -1.0).then_inc(S["scratch"], 1)
            with act.Fori(0, SEQS) as s:
                def nth(name, k):
                    return s * PER[name] + k + start(name, k)

                nsq = [0]
                nn = [0]
                units = [0]
                his = [0]

                def split_to(n):
                    while units[0] < min(n, UNITS_W):
                        u = units[0]
                        act.wait_ge(w_in_sem[u % RAW_SLOTS], (s * LOADS + u // RAW_SLOTS + 1) * 16)
                        act.wait_ge(S["weights_used"], nth("weights_used", max(0, u - SPLIT_SLOTS + 1)))
                        w = slice(0, UNIT_CHUNKS[u] * P)
                        nc.scalar.copy(whi[:, u % SPLIT_SLOTS, w], raw[:, u % RAW_SLOTS, w]).then_inc(S["hi_split"], 1)
                        units[0] += 1

                def first_parts(to):
                    for c in to:
                        his[0] += 1
                        act.wait_ge(S["full_ready"], nth("full_ready", his[0]))
                        nc.scalar.copy(arena_r[:, c, :], t(5 + his[0] % 2)).then_inc(S["hi_done"], 1)

                def square(src):
                    nsq[0] += 1
                    act.wait_ge(S["sq_used"], nth("sq_used", max(0, nsq[0] - 2)))
                    nc.scalar.activation(t(nsq[0] % 2), src, ACT.Square).then_inc(S["sq_done"], 1)

                def norm_act(sources, width, ready=None):
                    for i, c in enumerate(sources):
                        if ready:
                            ready(i)
                        square(arena[:, c, :])
                    root(width)

                def root(width):
                    act.wait_ge(S["sq_used"], nth("sq_used", nsq[0]))
                    act.wait_ge(S["diag_done"], nth("diag_done", nn[0]))
                    nn[0] += 1
                    nc.scalar.activation(srt[:, :], A[:, 3, 0:8], ACT.Sqrt, bias=epsc[:, :], scale=1.0 / width).then_inc(S["srt_done"], 1)

                act.wait_ge(S["norm_applied"], nth("norm_applied", 0))
                for i in range(16):
                    k, h = divmod(i, 2)
                    act.wait_ge(S["xt_done"], nth("xt_done", i + 1))
                    nc.scalar.copy(arena[:, RAW + k, h * HALF:(h + 1) * HALF], A[:, i % 3, :]).then_inc(S["xt_out"], 1)
                split_to(3)
                norm_act(range(RAW, RAW + KD), D, lambda i: act.wait_ge(S["xt_out"], nth("xt_out", 2 * i + 2)))
                first_parts(range(H, H + KD))

                def used(b):
                    split_to(uend(b) + 2)
                    act.wait_ge(S["weights_used"], nth("weights_used", uend(b)))

                def psum(b):
                    return G[:, 2 * (b % 2):2 * (b % 2) + 2, :].rearrange("p a n -> p (a n)")

                for b in range(12):
                    used(b)
                    to = (Q, K, VT)[b // 4] + b % 4
                    if b < 4:
                        nc.scalar.mul(arena[:, to, :], psum(b), DH ** -0.5).then_inc(S["in_copied"], 1)
                    else:
                        nc.scalar.copy(arena[:, to, :], psum(b)).then_inc(S["in_copied"], 1)
                used(DT_BLOCK)
                nc.scalar.activation(t(0)[0:32], psum(DT_BLOCK)[0:32], ACT.Identity,
                                     bias=prm[0:32, PC["dt_bias"]:PC["dt_bias"] + 1]).then_inc(S["in_copied"], 1)
                act.wait_ge(S["pads"], nth("pads", 1))

                def z_saved(m, k):
                    act.wait_ge(S[f"z_saved{m % 2}"], nth(f"z_saved{m % 2}", 16 * k))

                def copy_z(i, m):
                    used(13 + i if i < 4 else 17 + m)
                    nc.scalar.mul(t(2 + m % 2, T, 2), psum(13 + i if i < 4 else 17 + m), 0.5).then_inc(S["in_copied"], 1)

                def tanh_half(i, src):
                    act.wait_ge(S["silu_done"], nth("silu_done", i))
                    nc.scalar.activation(t(4), src, ACT.Tanh).then_inc(S["tanh_done"], 1)

                for i in range(4):
                    if i >= 2:
                        z_saved(i, 1)
                    copy_z(i, i)
                    if i == 0:
                        act.wait_ge(S["exp_dt"], nth("exp_dt", 1))
                        nc.scalar.activation(t(1)[0:32], t(1)[0:32], ACT.Exp, scale=-1.0).then_inc(S["exp_dt_out"], 1)
                    act.wait_ge(S["in_copied"], nth("in_copied", 14 + i))
                    tanh_half(i, t(2 + i % 2, T, 2))
                for st in range(UNITS + 10):
                    split_to(UNITS_TO[17] + min(st // 2, 31) + 2)
                    if st < UNITS:
                        act.wait_ge(S["s_biased"], nth("s_biased", st + 1))
                        nc.scalar.activation(pbuf[:, st % 2, :], pbuf[:, st % 2, :], ACT.Exp, bias=nmx[:, st % 2:st % 2 + 1],
                                             accum_out=rsum[:, st % 2:st % 2 + 1]).then_inc(S["p_exp"], 1)
                    if 1 <= st <= UNITS:
                        u = st - 1
                        act.wait_ge(S["pt_done"], nth("pt_done", u + 1))
                        act.wait_ge(S["o_done"], nth("o_done", max(0, u - 1)))
                        nc.scalar.copy(ptbuf[:, u % 2, :], A[:, 2, :]).then_inc(S["pt_out"], 1)
                    if 2 <= st < UNITS + 2:
                        u = st - 2
                        act.wait_ge(S["o_done"], nth("o_done", u + 1))
                        r = u % ROWS
                        for hh in range(2):
                            o = nc.scalar.copy(arena[hh * 64:(hh + 1) * 64, Q + u // ROWS, r * 64:(r + 1) * 64],
                                               A[hh * 64:(hh + 1) * 64, 3, hh * 64:(hh + 1) * 64])
                        o.then_inc(S["o_out"], 1)
                    if st % 4 == 0 and 4 <= st <= UNITS:
                        m = st // 4 - 1
                        if m < 2:
                            z_saved(m, 2)
                        elif m % 4 == 1:
                            z_saved(m, 2 + m // 4)
                        else:
                            act.wait_ge(S["conv_done"], nth("conv_done", 3 * ((m - 2) // 4) + (m - 2) % 4 + 1))
                        if m % 4 < 3:
                            act.wait_ge(S["weights_used"], nth("weights_used", uend(17 + m)))
                            nc.scalar.copy(t(2 + m % 2, T, 2), psum(17 + m)).then_inc(S["in_copied"], 1)
                        else:
                            act.wait_ge(S["weights_used"], nth("weights_used", uend(17 + m)))
                            nc.scalar.mul(t(2 + m % 2, T, 2), psum(17 + m), 0.5).then_inc(S["in_copied"], 1)
                    if st % 4 == 0 and 8 <= st and (st // 4 - 2) % 4 < 3 and st // 4 - 2 < 16:
                        m = st // 4 - 2
                        j = 3 * (m // 4) + m % 4
                        act.wait_ge(S["conv_done"], nth("conv_done", j + 1))
                        tanh_half(4 + m, arena[:, XBC + j, :])
                    if st % 4 == 1 and 4 < st and (st // 4 - 1) % 4 == 3 and st // 4 - 1 < 16:
                        m = st // 4 - 1
                        act.wait_ge(S["in_copied"], nth("in_copied", 18 + m))
                        tanh_half(4 + m, t(2 + m % 2, T, 2))

                def broadcast_sums(c, g):
                    for d in range(2):
                        src = bass.AP(cs_dram.tensor, (d * 32 + d * SH + g * GH) * T + c * P, [[0, P], [T, GH], [1, P]])
                        act.dma_start(bc(g, d), src).then_inc(S[f"bc_in{g}"], 16)

                act.wait_ge(S["silu_done"], nth("silu_done", 20))
                act.wait_ge(S["o_done"], nth("o_done", UNITS))
                act.wait_ge(S["rows_saved"], nth("rows_saved", 32))
                for g in range(GROUPS):
                    broadcast_sums(0, g)
                for i in range(3 * TT):
                    c, part = divmod(i, 3)
                    act.wait_ge(S["xtok_done"], nth("xtok_done", i + 1))
                    if part < 2:
                        nc.scalar.copy(arena[:, H + c, part * HALF:(part + 1) * HALF], A[:, i % 4, :]).then_inc(S["xtok_out"], 1)
                    else:
                        nc.scalar.copy(arena[:, BTOK + c // 4, (c % 4) * 256:(c % 4 + 1) * 256], A[:, i % 4, 0:256])
                        nc.scalar.copy(scal[:, c, :], A[:, i % 4, 256:352]).then_inc(S["xtok_out"], 1)
                act.wait_ge(S["coef_in"], nth("coef_in", 1))
                for d in range(2):
                    hs = slice(d * SH, (d + 1) * SH)
                    tot = G[:, d, 0:TT * 32].rearrange("p (c n) -> p c n", c=TT)[:, :, hs]
                    nc.scalar.activation(dtot[:, :, hs], tot, ACT.Exp)
                    nc.scalar.activation(ecs[:, :, hs], scal[:, :, 32 + d * 48:48 + d * 48], ACT.Exp)
                nc.scalar.activation(wst[:, :, :], wst[:, :, :], ACT.Exp).then_inc(S["coef_exp"], 1)
                for c in range(TT):
                    for g in range(GROUPS):
                        act.wait_ge(S["e_ready"], nth("e_ready", 2 * c + g + 1))
                        if c < TT - 1:
                            broadcast_sums(c + 1, g)
                        nc.scalar.activation(t(2 * g), t(2 * g), ACT.Exp).then_inc(S["e_exp"], 1)
                act.wait_ge(S["yt_out"], nth("yt_out", 2 * TT))
                split_to(UNITS_TO[B_OUT] + 3)
                norm_act(range(Q, Q + 4), 512)
                first_parts(MIX_HI[0:4])
                norm_act(range(Z, Z + 4), 512)
                first_parts(MIX_HI[4:8])
                norm_act(range(Z + 4, Z + 8), 512)
                first_parts(MIX_HI[8:12])
                for j in range(OUT_BLOCKS):
                    used(B_OUT + j)
                    nc.scalar.copy(arena[:, Z + j, :], psum(j)).then_inc(S["out_copied"], 1)
                    act.wait_ge(S["out_copied"], nth("out_copied", j + 1))
                    square(arena[:, Z + j, :])
                root(D)
                split_to(UNITS_TO[B_GU] + 3)
                norm_act(range(RAW, RAW + KD), D, lambda i: act.wait_ge(S["norm_applied"], nth("norm_applied", 21 + i)))
                first_parts(range(H, H + KD))
                act.wait_ge(S["pads"], nth("pads", 2))
                for p in range(FK):
                    used(B_GU + 2 * p)
                    act.wait_ge(S["gate_conv"], nth("gate_conv", p))
                    nc.scalar.copy(t(2, T, 1), psum(0)).then_inc(S["gate_copied"], 1)
                    split_to(uend(B_GU + 2 * p) + 3)
                    act.wait_ge(S["gate_conv"], nth("gate_conv", p + 1))
                    act.wait_ge(S["f_ready"], nth("f_ready", p))
                    nc.scalar.activation(t(1), t(4), ACT.Gelu_apprx_tanh).then_inc(S["gelu_done"], 1)
                    split_to(uend(B_GU + 2 * p) + 4)
                def copy_o(i):
                    half, j = divmod(i, KD)
                    used(B_DOWN + i)
                    nc.scalar.copy(o_chunk(j)[:, half * HALF:(half + 1) * HALF], G[:, 2 * (i % 2), :]).then_inc(S["o2_copied"], 1)
                    if half:
                        act.wait_ge(S["o2_copied"], nth("o2_copied", i + 1))
                        square(o_chunk(j))

                for i in range(DOWN_BLOCKS):
                    half, j = divmod(i, KD)
                    if j == 0:
                        for k in range(FK):
                            split_to(down_ahead(half, k))
                            if half:
                                act.wait_ge(S["weights_used"], nth("weights_used", UNITS_TO[B_DOWN + i - 1] + k // UC + 1))
                            elif k == 0:
                                act.wait_ge(S["weights_used"], nth("weights_used", UNITS_TO[B_DOWN]))
                            act.wait_ge(S["f_ready"], nth("f_ready", k + 1))
                            nc.scalar.copy(fhi(k), f_full(k, slice(half * HALF, (half + 1) * HALF))).then_inc(S["fhi_done"], 1)
                        if half:
                            copy_o(KD - 1)
                    if i != KD - 1:
                        copy_o(i)
                root(D)
                for i in range(16):
                    tile, g = divmod(i, 2)
                    act.wait_ge(S["yo_t"], nth("yo_t", i + 1))
                    nc.scalar.copy(arena[:, H + tile, g * HALF:(g + 1) * HALF], A[:, i % 3, :]).then_inc(S["yo_copied"], 1)

        @block.vector
        def _(dve):
            dve.wait_ge(S["const"], CONSTS)
            dve.wait_ge(S["params_in"], 16)
            dve.wait_ge(S["scratch"], 2)
            with dve.Fori(0, SEQS) as s:
                def nth(name, k):
                    return s * PER[name] + k + start(name, k)

                links = [0]

                def step():
                    links[0] += 1
                    return links[0]

                tt, ts, stt = nc.vector.tensor_tensor, nc.vector.tensor_scalar, nc.vector.scalar_tensor_tensor
                nn = [0]
                applied = [0]
                rs = G[:, 2:4, :].rearrange("p a n -> p (a n)")

                def col(name, k):
                    return prm[:, PC[name] + k:PC[name] + k + 1]

                units, fulls = [0], [0]

                def split_to(n):
                    while units[0] < min(n, UNITS_W):
                        u = units[0]
                        dve.wait_ge(S["hi_split"], nth("hi_split", u + 1))
                        w = slice(0, UNIT_CHUNKS[u] * P)
                        tt(wlo[:, u % SPLIT_SLOTS, w], raw[:, u % RAW_SLOTS, w], whi[:, u % SPLIT_SLOTS, w].bitcast(F),
                           ALU.subtract).then_inc(S["lo_split"], 1)
                        units[0] += 1

                def norm_root():
                    nn[0] += 1
                    dve.wait_ge(S["srt_done"], nth("srt_done", nn[0]))
                    dve.wait_ge(S["rs_done"], nth("rs_done", nn[0] - 1))
                    nc.vector.reciprocal(rst[:, :], srt[:, :]).then_inc(S["dve_step"], 1)
                    dve.wait_ge(S["dve_step"], nth("dve_step", step()))
                    for i in range(TT):
                        m = ts(t(2, P, i * P), ident[:, :], rst[:, i:i + 1], None, ALU.mult)
                    m.then_inc(S["diag_done"], 1)
                    dve.wait_ge(S["rs_done"], nth("rs_done", nn[0]))

                def norm_split(chunks, gain, g0, src, hi, lo):
                    norm_root()
                    dve.wait_ge(S["norm_applied"], nth("norm_applied", applied[0]))

                    def second(k, n):
                        dve.wait_ge(S["hi_done"], nth("hi_done", n))
                        tt(arena_r[:, lo[k], :], t(5 + n % 2), arena_r[:, hi[k], :].bitcast(F), ALU.subtract).then_inc(S["norm_applied"], 1)
                        applied[0] += 1

                    for k in range(chunks):
                        fulls[0] += 1
                        if k >= 2:
                            dve.wait_ge(S["norm_applied"], nth("norm_applied", applied[0]))
                        stt(t(5 + fulls[0] % 2), arena[:, src + k, :], col(gain, g0 + k), rs, ALU.mult, ALU.mult
                            ).then_inc(S["full_ready"], 1)
                        if k:
                            second(k - 1, fulls[0] - 1)
                    second(chunks - 1, fulls[0])

                h_hi, h_lo = [H + k for k in range(KD)], [H_LO + k for k in range(KD)]
                split_to(3)
                dve.wait_ge(S["yo_t"], nth("yo_t", 0))
                norm_split(KD, "mix_pre", 0, RAW, h_hi, h_lo)
                split_to(UNITS_TO[DT_BLOCK + 1] + 2)
                dve.wait_ge(S["raw_saved"], nth("raw_saved", 16))
                for i in range(TT):
                    dve.wait_ge(S["vt_done"], nth("vt_done", i + 1))
                    nc.vector.tensor_copy(arena[:, VK + i // 2, (i % 2) * HALF:(i % 2 + 1) * HALF], A[:, 2 + i % 2, :]).then_inc(S["v_out"], 1)
                def silu(i, c):
                    dve.wait_ge(S["tanh_done"], nth("tanh_done", i + 1))
                    stt(c, t(4), 1.0, c, ALU.add, ALU.mult).then_inc(S["silu_done"], 1)

                x_, u_, z_, z2 = (t(i)[0:32] for i in (0, 1, 5, 6))
                dve.wait_ge(S["in_copied"], nth("in_copied", DT_BLOCK + 1))
                stt(u_, x_, -1.0, x_, ALU.mult, ALU.max).then_inc(S["exp_dt"], 1)
                dve.wait_ge(S["exp_dt_out"], nth("exp_dt_out", 1))
                ts(z_, u_, 2.0, None, ALU.add).then_inc(S["dve_step"], 1)
                dve.wait_ge(S["dve_step"], nth("dve_step", step()))
                nc.vector.reciprocal(z_, z_).then_inc(S["dve_step"], 1)
                dve.wait_ge(S["dve_step"], nth("dve_step", step()))
                split_to(UNITS_TO[14] + 2)
                tt(z_, z_, u_, ALU.mult).then_inc(S["dve_step"], 1)
                dve.wait_ge(S["dve_step"], nth("dve_step", step()))
                tt(z2, z_, z_, ALU.mult).then_inc(S["dve_step"], 1)
                dve.wait_ge(S["dve_step"], nth("dve_step", step()))
                ts(u_, z2, 1.0 / 17, None, ALU.mult).then_inc(S["dve_step"], 1)
                dve.wait_ge(S["dve_step"], nth("dve_step", step()))
                silu(0, t(2, T, 2))
                for n in range(7, 0, -1):
                    if n == 4:
                        split_to(UNITS_TO[15])
                    stt(u_, u_, 1.0 / (2 * n + 1), z2, ALU.add, ALU.mult).then_inc(S["dve_step"], 1)
                    dve.wait_ge(S["dve_step"], nth("dve_step", step()))
                split_to(UNITS_TO[15] + 1)
                silu(1, t(3, T, 2))
                stt(z_, u_, 1.0, z_, ALU.add, ALU.mult).then_inc(S["dve_step"], 1)
                dve.wait_ge(S["dve_step"], nth("dve_step", step()))
                ts(x_, x_, 0.0, None, ALU.max).then_inc(S["dve_step"], 1)
                dve.wait_ge(S["dve_step"], nth("dve_step", step()))
                stt(rows[0:32, :], z_, 2.0, x_, ALU.mult, ALU.add).then_inc(S["dve_step"], 1)
                dve.wait_ge(S["dve_step"], nth("dve_step", step()))
                ts(x_, rows[0:32, :], acol[0:32, :], None, ALU.mult).then_inc(S["dve_step"], 1)
                dve.wait_ge(S["dve_step"], nth("dve_step", step()))
                split_to(UNITS_TO[15] + 2)
                for c in range(TT):
                    da = x_[:, c * P:(c + 1) * P]
                    nc.vector.tensor_tensor_scan(rows[32:64, c * P:(c + 1) * P], ones[0:32, :], da, 0.0, ALU.mult, ALU.add)
                    m = nc.vector.tensor_tensor_scan(rows[64:96, c * P:(c + 1) * P][:, ::-1], ones[0:32, :], da[:, ::-1], 0.0,
                                                     ALU.mult, ALU.add)
                m.then_inc(S["rows_ready"], 1)

                for i in (2, 3):
                    split_to(UNITS_TO[13 + i] + 2)
                    silu(i, t(2 + i % 2, T, 2))
                split_to(UNITS_TO[17] + 2)
                dve.wait_ge(S["v_saved"], nth("v_saved", 16))
                for st in range(UNITS + 10):
                    split_to(UNITS_TO[17] + min(st // 2, 31) + 2)
                    if st < UNITS:
                        dve.wait_ge(S["s_done"], nth("s_done", st + 1))
                        dve.wait_ge(S["tb_in"], nth("tb_in", 16 * (st // ROWS + 1)))
                        dve.wait_ge(S["pt_done"], nth("pt_done", max(0, st - 1)))
                        if st < 2:
                            dve.wait_ge(S["rows_ready"], nth("rows_ready", 1))
                        dve.sem_inc(S["settled"], 1)
                        rs0 = min(max(st % ROWS - KR // 2, 0), ROWS - KR)
                        ro = rs0 - st % ROWS + KR - 1
                        nc.vector.tensor_tensor_reduce(
                            out=pbuf[:, st % 2, :], in0=A[:, st % 2, :], in1=table[:, ro * 64:ro * 64 + KEYS], scale=1.0,
                            scalar=-3e38, op0=ALU.add, op1=ALU.max, accum_out=mx[:, st % 2:st % 2 + 1]).then_inc(S["dve_step"], 1)
                        dve.wait_ge(S["dve_step"], nth("dve_step", step()))
                        ts(nmx[:, st % 2:st % 2 + 1], mx[:, st % 2:st % 2 + 1], -1.0, None, ALU.mult).then_inc(S["s_biased"], 1)
                    m = st // 4 - 1
                    if 0 <= m < 16 and m % 4 < 3:
                        j = 3 * (m // 4) + m % 4
                        o, cv = arena[:, XBC + j, :], lambda i: t(2 + m % 2, T, i)
                        w = lambda i: hconv[:, 5 * j + i:5 * j + i + 1]
                        if st % 4 == 1:
                            dve.wait_ge(S["in_copied"], nth("in_copied", 18 + m))
                            ts(o, cv(0), w(0), hconv[:, 60 + j:61 + j], ALU.mult, ALU.add).then_inc(S["dve_step"], 1)
                            dve.wait_ge(S["dve_step"], nth("dve_step", step()))
                            stt(o, cv(1), w(1), o, ALU.mult, ALU.add).then_inc(S["dve_step"], 1)
                            dve.wait_ge(S["dve_step"], nth("dve_step", step()))
                        if st % 4 == 2:
                            stt(o, cv(2), w(2), o, ALU.mult, ALU.add).then_inc(S["dve_step"], 1)
                            dve.wait_ge(S["dve_step"], nth("dve_step", step()))
                            stt(o, cv(3), w(3), o, ALU.mult, ALU.add).then_inc(S["dve_step"], 1)
                            dve.wait_ge(S["dve_step"], nth("dve_step", step()))
                        if st % 4 == 3:
                            stt(o, cv(4), w(4), o, ALU.mult, ALU.add).then_inc(S["conv_done"], 1)
                    if 0 <= m < 16 and m % 4 == 3 and st % 4 == 2:
                        silu(4 + m, t(2 + m % 2, T, 2))
                    if st % 4 == 0 and 0 <= m - 1 < 16 and (m - 1) % 4 < 3:
                        silu(4 + m - 1, arena[:, XBC + 3 * ((m - 1) // 4) + (m - 1) % 4, :])
                    if st < UNITS:
                        dve.wait_ge(S["p_exp"], nth("p_exp", st + 1))
                        nc.vector.reciprocal(rinv[:, st % 2:st % 2 + 1], rsum[:, st % 2:st % 2 + 1]).then_inc(S["dve_step"], 1)
                        dve.wait_ge(S["dve_step"], nth("dve_step", step()))
                        ts(pbuf[:, st % 2, :], pbuf[:, st % 2, :], rinv[:, st % 2:st % 2 + 1], None, ALU.mult).then_inc(S["p_scaled"], 1)
                dve.wait_ge(S["tot_done"], nth("tot_done", 1))
                for d in range(2):
                    hs = slice(d * SH, (d + 1) * SH)
                    m = tt(wst[:, :, hs], G[:, d, 0:TT * 32].rearrange("p (c n) -> p c n", c=TT)[:, :, hs],
                           scal[:, :, 32 + d * 48:48 + d * 48], ALU.subtract)
                m.then_inc(S["coef_in"], 1)
                dve.wait_ge(S["coef_exp"], nth("coef_exp", 1))
                tt(wst[:, :, :], wst[:, :, :], scal[:, :, 0:32], ALU.mult).then_inc(S["coef_out"], 1)

                def per_head(coef, c, d):
                    return coef[:, c, d * SH:(d + 1) * SH].unsqueeze(2).broadcast_to([P, SH, SP_])

                def heads(ap):
                    return ap.rearrange("p (h n) -> p h n", h=SH)

                gg = G[:, 0:2, :].rearrange("p a n -> p (a n)")
                for i, c in enumerate(range(TT - 1, 0, -1)):
                    to = arena[:, SB + c - 1, :]
                    if i:
                        tt(heads(to), heads(arena[:, SB + c, :]), per_head(dtot, c, 1), ALU.mult).then_inc(S["dve_step"], 1)
                        dve.wait_ge(S["dve_step"], nth("dve_step", step()))
                    dve.wait_ge(S["st_done"], nth("st_done", i + 1))
                    if i:
                        m = tt(to, gg, to, ALU.add)
                    else:
                        m = nc.vector.tensor_copy(to, gg)
                    m.then_inc(S["st_read"], 1)
                    dve.wait_ge(S["st_read"], nth("st_read", i + 1))
                dve.wait_ge(S["rows_saved"], nth("rows_saved", 32))
                dve.wait_ge(S["z_back"], nth("z_back", 16))
                yb = arena[:, YBUF, :]
                for c in range(TT):
                    dve.wait_ge(S["cb_done"], nth("cb_done", c + 1))
                    cbv = A[:, 0, 0:2 * P].rearrange("p (g n) -> p g n", g=2)
                    up, lo = rows[:, 0:256], rows[:, 256:512]
                    tt(up.rearrange("p (g n) -> p g n", g=2), cbv, upper[:, :].unsqueeze(1).broadcast_to([P, 2, P]), ALU.mult)
                    m = tt(lo.rearrange("p (g n) -> p g n", g=2), cbv, lower[:, :].unsqueeze(1).broadcast_to([P, 2, P]), ALU.mult)
                    m.then_inc(S["cb_out"], 1)
                    dve.wait_ge(S["cb_out"], nth("cb_out", c + 1))
                    if c < TT - 1:
                        if c:
                            dve.wait_ge(S["yo_done"], nth("yo_done", c + 1))
                            tt(heads(arena[:, SF, :]), heads(arena[:, SF, :]), per_head(dtot, c, 0), ALU.mult).then_inc(S["dve_step"], 1)
                            dve.wait_ge(S["dve_step"], nth("dve_step", step()))
                        for g in range(GROUPS):
                            sf = arena[:, SF, g * HALF:(g + 1) * HALF]
                            dve.wait_ge(S["st_done"], nth("st_done", 7 + 2 * c + g + 1))
                            if c:
                                m = tt(sf, A[:, 3, :], sf, ALU.add)
                            else:
                                m = nc.vector.tensor_copy(sf, A[:, 3, :])
                            m.then_inc(S["st_read"], 1)
                    for g in range(GROUPS):
                        dve.wait_ge(S[f"bc_in{g}"], nth(f"bc_in{g}", 32 * (c + 1)))
                        dve.wait_ge(S["yd_done"], nth("yd_done", max(0, 2 * c + g - 1)))
                        E, W = t(2 * g), t(2 * g + 1)
                        for h in range(GH):
                            n = g * GH + h
                            m = ts(E[:, h * P:(h + 1) * P], bc(g, 0)[:, h, :], scal[:, c, 32 + n:33 + n], None, ALU.subtract)
                        m.then_inc(S["dve_step"], 1)
                        dve.wait_ge(S["dve_step"], nth("dve_step", step()))
                        for h in range(GH):
                            n = g * GH + h
                            eh = E[:, h * P:(h + 1) * P]
                            m = stt(eh, bc(g, 1)[:, h, :], scal[:, c, 80 + n:81 + n], eh, ALU.subtract, ALU.min)
                        m.then_inc(S["e_ready"], 1)
                        for h in range(GH):
                            n = g * GH + h
                            m = ts(W[:, h * P:(h + 1) * P], lo[:, g * P:(g + 1) * P], scal[:, c, 16 + n:17 + n], None, ALU.mult)
                        m.then_inc(S["dve_step"], 1)
                        dve.wait_ge(S["dve_step"], nth("dve_step", step()))
                        for h in range(GH):
                            n = g * GH + h
                            wh = W[:, h * P:(h + 1) * P]
                            m = stt(wh, up[:, g * P:(g + 1) * P], scal[:, c, n:n + 1], wh, ALU.mult, ALU.add)
                        m.then_inc(S["dve_step"], 1)
                        dve.wait_ge(S["dve_step"], nth("dve_step", step()))
                    for g in range(GROUPS):
                        dve.wait_ge(S["e_exp"], nth("e_exp", 2 * c + g + 1))
                        tt(t(2 * g), t(2 * g), t(2 * g + 1), ALU.mult).then_inc(S["m_ready"], 1)
                    dve.wait_ge(S["m_ready"], nth("m_ready", 2 * c + 2))
                    dve.wait_ge(S["xd_ready"], nth("xd_ready", c + 1))
                    dve.wait_ge(S["yo_done"], nth("yo_done", c + 1))
                    if c:
                        tt(heads(t(1)), heads(G[:, 2:4, :].rearrange("p a n -> p (a n)")), per_head(ecs, c, 0), ALU.mult).then_inc(S["dve_step"], 1)
                        dve.wait_ge(S["dve_step"], nth("dve_step", step()))
                        tt(yb, yb, t(1), ALU.add).then_inc(S["dve_step"], 1)
                        dve.wait_ge(S["dve_step"], nth("dve_step", step()))
                    if c < TT - 1:
                        tt(heads(t(1)), heads(A[:, 1:3, :].rearrange("p a n -> p (a n)")), per_head(ecs, c, 1), ALU.mult).then_inc(S["dve_step"], 1)
                        dve.wait_ge(S["dve_step"], nth("dve_step", step()))
                        tt(yb, yb, t(1), ALU.add).then_inc(S["dve_step"], 1)
                        dve.wait_ge(S["dve_step"], nth("dve_step", step()))
                    dve.wait_ge(S["yd_done"], nth("yd_done", 2 * c + 2))
                    tt(yb, gg, yb, ALU.add).then_inc(S["y_ready"], 1)
                    for g in range(GROUPS):
                        dve.wait_ge(S["yt_done"], nth("yt_done", 2 * c + g + 1))
                        zv = arena[:, Z + 4 * g:Z + 4 * g + 4, c * P:(c + 1) * P]
                        tt(zv, G[:, g, :].rearrange("p (k n) -> p k n", k=4), zv, ALU.mult).then_inc(S["yt_out"], 1)
                split_to(UNITS_TO[B_OUT] + 3)
                norm_split(4, "attn", 0, Q, MIX_HI[0:4], MIX_LO[0:4])
                norm_split(4, "ssd", 0, Z, MIX_HI[4:8], MIX_LO[4:8])
                norm_split(4, "ssd", 4, Z + 4, MIX_HI[8:12], MIX_LO[8:12])
                split_to(UNITS_TO[B_GU] + 3 - 3)
                norm_root()
                dve.wait_ge(S["x_back"], nth("x_back", 32))
                for k in range(KD):
                    stt(arena[:, Z + k, :], arena[:, Z + k, :], col("mix_post", k), rs, ALU.mult, ALU.mult).then_inc(S["dve_step"], 1)
                    dve.wait_ge(S["dve_step"], nth("dve_step", step()))
                    tt(arena[:, RAW + k, :], x_back(k), arena[:, Z + k, :], ALU.add).then_inc(S["norm_applied"], 1)
                    applied[0] += 1
                split_to(UNITS_TO[B_GU] + 3)
                norm_split(KD, "ffn_pre", 0, RAW, h_hi, h_lo)
                dve.wait_ge(S["x1_saved"], nth("x1_saved", 16))
                for p in range(FK):
                    cv, gt = t(4), lambda i: t(2, T, i)
                    w = lambda i: prm[:, PC["fconv_w"] + 3 * p + i:PC["fconv_w"] + 3 * p + i + 1]
                    split_to(uend(B_GU + 2 * p) + 2)
                    dve.wait_ge(S["gate_copied"], nth("gate_copied", p + 1))
                    dve.wait_ge(S["gelu_done"], nth("gelu_done", p))
                    ts(cv, gt(0), w(0), prm[:, PC["fconv_b"] + p:PC["fconv_b"] + p + 1], ALU.mult, ALU.add).then_inc(S["dve_step"], 1)
                    dve.wait_ge(S["dve_step"], nth("dve_step", step()))
                    stt(cv, gt(1), w(1), cv, ALU.mult, ALU.add).then_inc(S["dve_step"], 1)
                    dve.wait_ge(S["dve_step"], nth("dve_step", step()))
                    stt(cv, gt(2), w(2), cv, ALU.mult, ALU.add).then_inc(S["gate_conv"], 1)
                    split_to(uend(B_GU + 2 * p) + 3)
                    dve.wait_ge(S["gelu_done"], nth("gelu_done", p + 1))
                    split_to(uend(B_GU + 2 * p) + 4)
                    dve.wait_ge(S["weights_used"], nth("weights_used", uend(B_GU + 2 * p + 1)))
                    tt(f_full(p), rs, t(1), ALU.mult).then_inc(S["f_ready"], 1)
                for half in range(2):
                    for k in range(FK):
                        split_to(down_ahead(half, k))
                        dve.wait_ge(S["fhi_done"], nth("fhi_done", half * FK + k + 1))
                        cs = slice(half * HALF, (half + 1) * HALF)
                        tt(f_r(k, cs), f_full(k, cs), fhi(k).bitcast(F),
                           ALU.subtract).then_inc(S["flo_done"], 1)
                    if half == 0:
                        split_to(UNITS_TO[B_DOWN + KD])
                split_to(UNITS_W)
                norm_root()
                dve.wait_ge(S["x1_back"], nth("x1_back", 32 * KD))
                for k in range(KD):
                    o = o_chunk(k)
                    stt(o, o, col("ffn_post", k), rs, ALU.mult, ALU.mult).then_inc(S["dve_step"], 1)
                    dve.wait_ge(S["dve_step"], nth("dve_step", step()))
                    for h in range(2):
                        m = tt(o[:, h * HALF:(h + 1) * HALF], o[:, h * HALF:(h + 1) * HALF], x1_part(k, h), ALU.add)
                    m.then_inc(S["norm_applied"], 1)
                    applied[0] += 1
                assert links[0] == DVE_LINKS, links[0]

        @block.gpsimd
        def _(pool):
            n = [0]

            def const(ins):
                n[0] += 1
                ins.then_inc(S["const"], 1)
                pool.wait_ge(S["const"], n[0])

            sel = nc.gpsimd.affine_select
            for name in STARTED:
                pool.sem_inc(S[name], 1)
                pool.sem_inc(S["started"], 1)
            const(nc.gpsimd.memset(ones[:, :], 1.0))
            const(nc.gpsimd.memset(qb[:, :, :], 0.0))
            const(nc.gpsimd.memset(epsc[:, :], EPS))
            const(nc.gpsimd.memset(t(0), 0.0))
            const(nc.gpsimd.memset(ident[:, :], 0.0))
            const(sel(out=ident[:, :], in_=ident[:, :], compare_op=ALU.not_equal, fill=1.0, base=0, pattern=[[-1, P]], channel_multiplier=1))
            const(sel(out=upper[:, :], in_=ones[:, :], compare_op=ALU.is_ge, fill=0.0, base=0, pattern=[[1, P]], channel_multiplier=-1))
            const(sel(out=lower[:, :], in_=ones[:, :], compare_op=ALU.is_ge, fill=0.0, base=0, pattern=[[-1, P]], channel_multiplier=1))
            pool.dma_start(pad_dram, t(0, 127)[0:HEADS * 15]).then_inc(S["rpb_pad"], 16)
            pool.dma_start(skp[:, :], bass.AP(skip.tensor, 0, [[0, P], [1, SH]])).then_inc(S["rpb_pad"], 16)
            pool.wait_ge(S["rpb_pad"], 32)
            pool.dma_start(pad_dram[:, 48:79], rpb).then_inc(S["rpb_pad"], 16)
            pool.wait_ge(S["rpb_pad"], 48)
            for h in range(HEADS):
                pool.dma_start(bass.AP(bias_dram.tensor, h * 64 * 960, [[64, 15], [960, 64], [1, 64]]),
                               bass.AP(pad_dram.tensor, h * 15 * 127 + 63, [[127, 15], [-1, 64], [1, 64]])).then_inc(S["table_read"], 16)
            pool.wait_ge(S["table_read"], 16 * HEADS)
            pool.dma_start(arena[:, 0:PAIRS, 0:960], bias_dram.rearrange("a p n -> p a n")).then_inc(S["table_read"], 16)
            pool.wait_ge(S["table_read"], 16 * HEADS + 16)
            for h in range(HEADS):
                v = arena[(h % 2) * 64:(h % 2) * 64 + 64, h // 2, 0:960].rearrange("p (a n) -> p a n", a=15)
                sel(out=v[:, :, 0:48], in_=v[:, :, 0:48], compare_op=ALU.is_ge, fill=MASKED, base=WIN_COLS // 2,
                    pattern=[[0, 15], [1, 48]], channel_multiplier=-1).then_inc(S["table_masked"], 1)
                pool.wait_ge(S["table_masked"], 2 * h + 1)
                sel(out=v[:, :, 16:64], in_=v[:, :, 16:64], compare_op=ALU.is_ge, fill=MASKED, base=WIN_COLS // 2 - 1 - 16,
                    pattern=[[0, 15], [-1, 48]], channel_multiplier=1).then_inc(S["table_masked"], 1)
                pool.wait_ge(S["table_masked"], 2 * h + 2)
            pool.dma_start(bias_dram.rearrange("a p n -> p a n"), arena[:, 0:PAIRS, 0:960]).then_inc(S["table_saved"], 16)
            pool.wait_ge(S["table_saved"], 16)
            while n[0] < CONSTS:
                const(nc.gpsimd.memset(mx[:, :], 0.0))
            with pool.Fori(0, SEQS) as s:
                def nth(name, k):
                    return s * PER[name] + k + start(name, k)

                def settled():
                    pool.sem_inc(S["settled"], 1)

                pool.wait_ge(S["xt_out"], nth("xt_out", 16))
                settled()
                pool.dma_start(x_dram, arena[:, RAW:RAW + KD, :]).then_inc(S["raw_saved"], 16)
                pool.wait_ge(S["rs_done"], nth("rs_done", 1))
                settled()
                for i in (2, 3):
                    nc.gpsimd.memset(t(i, 2), 0.0)
                    m = nc.gpsimd.memset(t(i, 2, 1026), 0.0)
                m.then_inc(S["pads"], 1)
                pool.wait_ge(S["v_out"], nth("v_out", TT))
                pool.wait_ge(S["o_done"], nth("o_done", 0))
                settled()
                pool.dma_start(v_dram.rearrange("(i p) n -> p i n", p=P),
                               arena[:, VK:VK + 4, :].rearrange("p a (b n) -> p (a b) n", b=2)).then_inc(S["v_saved"], 16)

                def save_z(k, m, i):
                    pool.wait_ge(S["silu_done"], nth("silu_done", i + 1))
                    settled()
                    pool.dma_start(z_dram[:, k, :], t(2 + m % 2, T, 2)).then_inc(S[f"z_saved{m % 2}"], 16)

                for i in range(4):
                    save_z(i, i, i)
                pool.wait_ge(S["v_saved"], nth("v_saved", 16))
                pool.wait_ge(S["rows_ready"], nth("rows_ready", 1))

                def load_v(hp):
                    cols = slice(hp * P, (hp + 1) * P)
                    settled()
                    pool.dma_start(v_even, v_dram[:, cols].rearrange("(i p) n -> p i n", p=P)).then_inc(S["v_in"], 16)
                    settled()
                    pool.dma_start(v_odd, v_dram[64:64 + 7 * P, cols].rearrange("(i p) n -> p i n", p=P)).then_inc(S["v_in"], 16)

                def load_table(hp):
                    settled()
                    pool.dma_start(table, bias_dram[hp]).then_inc(S["tb_in"], 16)

                load_v(0)
                load_table(0)
                pool.dma_start(cs_dram[0], rows[32:64, :]).then_inc(S["rows_saved"], 16)
                pool.dma_start(cs_dram[1], rows[64:96, :]).then_inc(S["rows_saved"], 16)
                for st in range(UNITS):
                    hp, r = divmod(st, ROWS)
                    if hp and r == 1:
                        pool.wait_ge(S["s_biased"], nth("s_biased", st - 1))
                        load_table(hp)
                    if hp and r == 2:
                        pool.wait_ge(S["o_done"], nth("o_done", st - 2))
                        load_v(hp)
                    pool.wait_ge(S["s_done"], nth("s_done", max(0, st - 1)))
                    if st == 0:
                        pool.wait_ge(S["pads"], nth("pads", 1))
                    settled()
                    for hh in range(2):
                        m = nc.gpsimd.tensor_copy(qb[hh * 64:(hh + 1) * 64, st % 2, hh * 64:(hh + 1) * 64],
                                                  arena[hh * 64:(hh + 1) * 64, Q + hp, r * 64:(r + 1) * 64])
                    m.then_inc(S["q_ready"], 1)
                    if st % 16 == 5 and st > 16:
                        save_z(3 + st // 16, 3, 4 * (st // 16) + 3)
                save_z(7, 3, 19)
                pool.wait_ge(S["in_copied"], nth("in_copied", IN_BLOCKS))
                for i in range(2):
                    pool.wait_ge(S[f"z_saved{i}"], nth(f"z_saved{i}", 16 * Z_SAVES[i]))
                settled()
                pool.dma_start(arena[:, Z:Z + KD, :], z_dram).then_inc(S["z_back"], 16)
                pool.wait_ge(S["coef_out"], nth("coef_out", 1))

                def weighted(c, d):
                    nc.gpsimd.tensor_tensor(arena[:, XW, :].rearrange("p (h n) -> p h n", h=SH),
                                            arena[:, H + c, :].rearrange("p (h n) -> p h n", h=SH),
                                            wst[:, c, d * SH:(d + 1) * SH].unsqueeze(2).broadcast_to([P, SH, SP_]),
                                            ALU.mult).then_inc(S["xw_ready"], 1)

                for i, c in enumerate(range(TT - 1, 0, -1)):
                    pool.wait_ge(S["st_done"], nth("st_done", i))
                    weighted(c, 1)
                for c in range(TT):
                    if c < TT - 1:
                        pool.wait_ge(S["st_done"], nth("st_done", 7 + 2 * c))
                        weighted(c, 0)
                    pool.wait_ge(S["yt_done"], nth("yt_done", 2 * c))
                    nc.gpsimd.tensor_tensor(arena[:, YBUF, :].rearrange("p (h n) -> p h n", h=SH),
                                            arena[:, H + c, :].rearrange("p (h n) -> p h n", h=SH),
                                            skp[:, :].unsqueeze(2).broadcast_to([P, SH, SP_]), ALU.mult).then_inc(S["xd_ready"], 1)
                pool.wait_ge(S["norm_applied"], nth("norm_applied", 20))
                settled()
                pool.dma_start(arena[:, K:K + 4, :], x_dram[:, 0:4, :]).then_inc(S["x_back"], 16)
                pool.dma_start(tmp[:, 3 * 1028:7 * 1028].rearrange("p (k n) -> p k n", k=4)[:, :, 0:T], x_dram[:, 4:8, :]
                               ).then_inc(S["x_back"], 16)
                pool.wait_ge(S["norm_applied"], nth("norm_applied", 28))
                settled()
                pool.dma_start(x1_dram, arena[:, RAW:RAW + KD, :]).then_inc(S["x1_saved"], 16)
                pool.wait_ge(S["rs_done"], nth("rs_done", 6))
                settled()
                nc.gpsimd.memset(t(2, 1), 0.0)
                nc.gpsimd.memset(t(2, 1, 1025), 0.0).then_inc(S["pads"], 1)
                pool.wait_ge(S["weights_used"], nth("weights_used", UNITS_TO[B_DOWN + KD]))
                settled()
                for k in range(KD):
                    for h in range(2):
                        pool.dma_start(x1_part(k, h), x1_dram[:, k, h * HALF:(h + 1) * HALF]).then_inc(S["x1_back"], 16)
                for i in range(TT):
                    pool.wait_ge(S["yo_copied"], nth("yo_copied", 2 * i + 2))
                    settled()
                    pool.dma_start(y[bass.ds(s, 1), i * P:(i + 1) * P, :].rearrange("a p n -> (a p) n"),
                                   arena[:, H + i, :]).then_inc(S["y_saved"], 16)
                pool.wait_ge(S["y_saved"], nth("y_saved", 16 * TT))
                pool.sem_inc(S["sequence_saved"], 1)
            pool.wait_ge(S["x1_saved"], 16 * SEQS)


def tiled(w):
    k, n = w.shape
    return w.reshape(k // P, P, n // P, P).transpose(2, 1, 0, 3).reshape(n // P, P, k)


def by_channel(a):
    a = a.reshape(-1, a.shape[-1] // P, P)
    return a.transpose(2, 1, 0).reshape(P, -1)


def kernel(**inputs):
    import numpy as np
    import concourse.bacc as bacc
    from concourse.bass_utils import run_bass_kernel_spmd

    a = {k: np.asarray(v) for k, v in inputs.items()}
    w_in = a["w_in"][0]
    blocks = tiled(np.pad(w_in, ((0, 0), (0, P - 32))))
    order = list(range(12)) + [32] + list(range(12, 16))
    for i in range(4):
        order += [20 + 3 * i, 21 + 3 * i, 22 + 3 * i, 16 + i]
    pad = np.zeros(P - 32, np.float32)
    prm = np.concatenate([
        by_channel(a["norm_mix_pre"][0]), by_channel(a["norm_mix_post"][0]), by_channel(a["attn_out_norm"][0]),
        by_channel(a["ssd_norm"][0]), by_channel(a["norm_ffn_pre"][0]), by_channel(a["norm_ffn_post"][0]),
        by_channel(a["ssd_conv_w"][0]), by_channel(a["ssd_conv_b"][0]), by_channel(a["ffn_conv_w"][0]),
        by_channel(a["ffn_conv_b"][0]),
        np.concatenate([a["ssd_dt_bias"][0].reshape(-1), pad])[:, None],
        np.concatenate([a["ssd_a_log"][0].reshape(-1), pad])[:, None]], axis=1)
    gate, up = tiled(a["w_gate"][0]), tiled(a["w_up"][0])
    arrays = {
        "x": np.concatenate([a["x_prompt"], a["x_sample"]]),
        "w_in_tiles": blocks[order],
        "w_out_tiles": tiled(a["w_out"][0]),
        "w_gu_tiles": np.stack([gate, up], axis=1).reshape(GU_BLOCKS, P, D),
        "w_down_tiles": tiled(a["w_down"][0]),
        "params": prm,
        "skip": a["ssd_d"][0],
        "rpb": a["attn_rpb"][0].reshape(HEADS * 15, 31),
    }
    arrays = {k: np.ascontiguousarray(v) for k, v in arrays.items()}
    nc = bacc.Bacc("TRN2", target_bir_lowering=False, num_devices=1)
    nc.disable_value_cache = True
    args = [nc.dram_tensor(k, v.shape, mybir.dt.from_np(v.dtype), kind="ExternalInput").ap() for k, v in arrays.items()]
    out = nc.dram_tensor("y", (SEQS, T, D), mybir.dt.float32, kind="ExternalOutput").ap()
    encoder(nc, *args, out)
    r = run_bass_kernel_spmd(nc, [arrays], core_ids=[0])
    y = r.results[0]["y"]
    return y[0:1], y[1:2]
```

```python
import concourse.bass as bass
from concourse import mybir
from contextlib import ExitStack

P = 128
SEQS = 2
T = 1024
D = 1024
KD = D // P
TT = T // P
HALF = 512
GRID_W, ROWS, KR, WIN_COLS = 64, 16, 8, 16
HEADS, DH = 8, 64
PAIRS = HEADS // 2
UNITS = PAIRS * ROWS
KEYS = KR * GRID_W
SH, SP_, GROUPS = 16, 64, 2
GH = SH // GROUPS
FF = 2816
FK = FF // P
EPS = 1e-6
MASKED = -1e30

PC = {}
_c = 0
for _name, _n in (("mix_pre", KD), ("mix_post", KD), ("attn", 4), ("ssd", KD), ("ffn_pre", KD), ("ffn_post", KD),
                  ("conv_w", 12 * 5), ("conv_b", 12), ("fconv_w", FK * 3), ("fconv_b", FK), ("dt_bias", 1), ("a_log", 1)):
    PC[_name] = _c
    _c += _n
NPARAM = _c

IN_BLOCKS, OUT_BLOCKS, GU_BLOCKS, DOWN_BLOCKS = 33, 8, 2 * FK, 2 * KD
DT_BLOCK = 12
B_OUT, B_GU, B_DOWN = IN_BLOCKS, IN_BLOCKS + OUT_BLOCKS, IN_BLOCKS + OUT_BLOCKS + GU_BLOCKS
BLOCKS = B_DOWN + DOWN_BLOCKS
UC = 4


def chunks_of(b):
    return 12 if B_OUT <= b < B_GU else FK if b >= B_DOWN else KD


UNIT_CHUNKS, UNITS_TO = [], [0]
for _b in range(BLOCKS):
    UNIT_CHUNKS += [min(UC, chunks_of(_b) - _k) for _k in range(0, chunks_of(_b), UC)]
    UNITS_TO.append(len(UNIT_CHUNKS))
UNITS_W = len(UNIT_CHUNKS)
RAW_SLOTS, SPLIT_SLOTS = 4, 3
LOADS = [len(range(i, UNITS_W, RAW_SLOTS)) for i in range(RAW_SLOTS)]


def uend(block):
    return UNITS_TO[block + 1]


STARTED = ('f_ready', 'gate_conv', 'gate_copied', 'gelu_done', 'in_copied', 'lo_split', 'norm_applied', 'o_done', 'pt_done', 's_done', 'sequence_saved', 'silu_done', 'sq_used', 'srt_done', 'weights_used', 'yo_copied', 'yo_t')
H, XBC, Z, Q, K = 0, 8, 20, 28, 32
VT, VK = 16, 12
RAW = 8
B_T, C_T = XBC + 8, XBC + 10
BTOK, YBUF, SF = K, K + 2, K + 3
SB, XW = XBC, XBC + 7
FFN = XBC
REGIONS = (8, 12, 8, 8)

H_LO = Z
MIX_HI = [k for k in range(12)]
MIX_LO = [12 + k for k in range(8)] + [Q + k for k in range(4)]
FHI = [0, 1, 2, 3, 4, 5, 6, 7, Z, Z + 1, Z + 2]
F_CHUNKS = [XBC + k for k in range(12)] + [Q + k for k in range(8)]

NORMS = 6
NAPPLIED = 5 * KD + 12
NSQ = 5 * KD + 4
NSPLIT = 8 + 12 + 8
Z_SAVES = (2, 6)
DVE_LINKS = 291

PER = {"bc_in0": 32 * TT, "bc_in1": 32 * TT, "cb_done": TT, "cb_out": TT, "coef_exp": 1, "coef_in": 1, "coef_out": 1,
       "conv_done": 12, "diag_done": 1, "dve_step": DVE_LINKS, "e_exp": 2 * TT, "e_ready": 2 * TT, "exp_dt": 1,
       "exp_dt_out": 1, "f_read": TT - 1, "f_ready": FK, "fb_ready": TT, "fhi_done": 2 * FK, "flo_done": 2 * FK,
       "full_ready": NSPLIT, "gate_conv": FK, "gate_copied": FK, "gelu_done": FK, "hi_done": NSPLIT,
       "hi_split": UNITS_W, "in_copied": IN_BLOCKS, "lo_split": UNITS_W, "m_ready": 2 * TT, "mix_sums": 1,
       "norm_applied": NAPPLIED, "o2_copied": DOWN_BLOCKS, "o_done": UNITS, "o_out": UNITS, "out_copied": OUT_BLOCKS,
       "p_exp": UNITS, "p_scaled": UNITS, "pads": 2, "pre_e": 2 * TT, "pre_w": 2 * TT, "pt_done": UNITS,
       "pt_out": UNITS, "q_ready": UNITS, "raw_saved": 16, "rows_ready": 1, "rows_saved": 32, "rs_done": 1,
       "s_biased": UNITS, "s_done": UNITS, "sequence_saved": 1, "sf_scaled": TT - 2, "silu_done": 20, "sq_done": NSQ,
       "sq_used": NSQ, "sqc_done": TT, "srt_done": NORMS, "st_done": 14, "st_read": 14, "tanh_done": 20,
       "tb_in": 16 * PAIRS, "tot_done": 1, "v_in": 32 * PAIRS, "v_out": TT, "v_saved": 16, "vt_done": TT,
       "weights_used": UNITS_W, "x1_back": 32 * KD, "x1_saved": 16, "x_back": 32, "x_in": 16 * TT, "xd_ready": TT,
       "xt_done": 16, "xt_out": 16, "xtok_done": 3 * TT, "xtok_out": 3 * TT, "xw_ready": 14, "y_ready": TT,
       "y_saved": 16 * 16, "yd_done": 2 * TT, "yo_copied": 16, "yo_t": 16, "yob_done": TT - 1, "yof_done": TT - 1,
       "yt_done": TT, "yt_out": TT, "z_back": 16, "z_saved0": 16 * Z_SAVES[0], "z_saved1": 16 * Z_SAVES[1]}


def down_ahead(half, k):
    b = B_DOWN + half * KD
    return UNITS_TO[b - 1] + k // UC + 4 if half else UNITS_TO[b] + max(3, k // UC + 2)


def encoder(nc, x, w_in, w_out, w_gu, w_down, params, skip, rpb, y):
    F = mybir.dt.float32
    ALU, ACT = mybir.AluOpType, mybir.ActivationFunctionType
    ctx = ExitStack()
    with ctx:
        def sb(name, shape):
            return ctx.enter_context(nc.sbuf_tensor(name, shape, F))

        def sem(name):
            return ctx.enter_context(nc.semaphore(name))

        R = mybir.dt.float32r

        def twin(name, width):
            at = -(-nc.sbuf_base // 32) * 32
            full = sb(name, [P, width])
            rounded = nc.alloc_sbuf_tensor_at(name + "_rounded", [P, width], R, offset=at)
            assert nc.sbuf_base == at + 4 * width
            return full, rounded

        regions = [twin(f"arena{i}", n * T) for i, n in enumerate(REGIONS)]

        class Arena:
            def __init__(self, tensors):
                self.views = [t[:, :].rearrange("p (k n) -> p k n", k=n) for t, n in zip(tensors, REGIONS)]

            def __getitem__(self, index):
                p, k, n = index
                lo, hi = (k.start, k.stop) if isinstance(k, slice) else (k, k + 1)
                i = max(i for i in range(len(REGIONS)) if sum(REGIONS[:i]) <= lo)
                base = sum(REGIONS[:i])
                assert hi <= base + REGIONS[i]
                return self.views[i][p, slice(lo - base, hi - base) if isinstance(k, slice) else k - base, n]

        arena, arena_r = Arena([f for f, _ in regions]), Arena([r for _, r in regions])
        tmp, tmp_r = twin("small", 8 * 1028)
        raw = sb("raw", [P, RAW_SLOTS, UC * P])
        whi = ctx.enter_context(nc.sbuf_tensor("whi", [P, SPLIT_SLOTS, UC * P], R))
        wlo = ctx.enter_context(nc.sbuf_tensor("wlo", [P, SPLIT_SLOTS, UC * P], R))
        rows = sb("rows", [P, T])
        scal = sb("scal", [P, TT, 96])
        shared = raw[:, 2:4, :].rearrange("p a n -> p (a n)")
        wst, ecs, dtot = (shared[:, i * TT * 32:(i + 1) * TT * 32].rearrange("p (c n) -> p c n", c=TT) for i in range(3))
        nscal = shared[:, 3 * TT * 32:3 * TT * 32 + TT * SH].rearrange("p (c n) -> p c n", c=TT)
        ident = sb("ident", [P, P])
        ones = sb("ones", [P, P])
        upper = sb("upper", [P, P])
        lower = sb("lower", [P, P])
        last = ident[:, P - 1:P].broadcast_to([P, P])
        first = ident[:, 0:1].broadcast_to([P, P])
        prm = sb("prm", [P, NPARAM])
        hconv = sb("hconv", [P, 72])
        skp = sb("skp", [P, SH])
        acol = sb("acol", [P, 1])
        epsc = sb("epsc", [P, 1])
        srt = sb("srt", [P, 24])
        rst = sb("rst", [P, 24])
        mx = sb("mx", [P, 2])
        nmx = sb("nmx", [P, 2])
        rsum = sb("rsum", [P, 2])
        rinv = sb("rinv", [P, 2])
        G = ctx.enter_context(nc.psum_tensor("G", [P, 4, HALF], F))
        A = ctx.enter_context(nc.psum_tensor("A", [P, 4, HALF], F))

        qb = sb("qb", [P, 2, P])

        def t(i, n=T, o=0):
            return tmp[:, i * 1028 + o:i * 1028 + o + n]

        pbuf = t(0).rearrange("p (a n) -> p a n", a=2)
        ptbuf = t(1).rearrange("p (a n) -> p a n", a=2)
        v_even = t(6).rearrange("p (a n) -> p a n", a=8)
        v_odd = t(7, 7 * P).rearrange("p (a n) -> p a n", a=7)

        def bc(g, d):
            o = 4 * 1028 + (2 * g + d) * T
            return tmp[:, o:o + T].rearrange("p (h n) -> p h n", h=GH)

        def f_full(k, cs=slice(0, T), of=None):
            if k < len(F_CHUNKS):
                return (arena if of is None else of[0])[:, F_CHUNKS[k], cs]
            o = (5 + k - len(F_CHUNKS)) * 1028
            return (tmp if of is None else of[1])[:, o:o + T][:, cs]

        def f_r(k, cs):
            return f_full(k, cs, (arena_r, tmp_r))

        def fhi(k):
            return arena_r[:, FHI[k // 2], (k % 2) * HALF:(k % 2 + 1) * HALF]

        def o_chunk(j):
            return arena[:, Z + 3 + j, :] if j < 5 else t({5: 3, 6: 7, 7: 4}[j])

        def x1_part(k, h):
            return f_full(2 * k + h)[:, 0:HALF]

        LAST_TURN = 2 * KD - 2

        def y_bank(n):
            return (A[:, 0, :], A[:, 1, :], G[:, 1, :], G[:, 3, :])[n % 4]

        def y_part(n):
            return x1_part(n % 8, n // 8)

        def x_back(k):
            return arena[:, K + k, :] if k < 4 else t(k - 1)

        table = t(5, 960)

        x_dram = nc.dram_tensor("x_by_channel", (P, KD, T), F, kind="Internal").ap()
        z_dram = nc.dram_tensor("gate_by_channel", (P, KD, T), F, kind="Internal").ap()
        x1_dram = nc.dram_tensor("x1_by_channel", (P, KD, T), F, kind="Internal").ap()
        v_dram = nc.dram_tensor("v_by_token", (T, PAIRS * P), F, kind="Internal").ap()
        cs_dram = nc.dram_tensor("running_sums", (2, 32, T), F, kind="Internal").ap()
        pad_dram = nc.dram_tensor("padded_bias", (HEADS * 15, 127), F, kind="Internal").ap()
        bias_dram = nc.dram_tensor("bias_tables", (PAIRS, P, 960), F, kind="Internal").ap()

        names = """params_in w_in0 w_in1 w_in2 w_in3 hi_split lo_split weights_used full_ready hi_done z_saved0
            z_saved1 z_back fhi_done flo_done x_in xt_done xt_out raw_saved sq_done sq_used srt_done diag_done
            rs_done norm_applied in_copied vt_done v_out v_saved v_in tb_in conv_done tanh_done silu_done exp_dt
            exp_dt_out rows_ready rows_saved q_ready s_done s_biased p_exp p_scaled pt_done pt_out o_done o_out
            xtok_done xtok_out tot_done coef_in coef_exp coef_out xw_ready st_done st_read cb_done cb_out bc_in0
            bc_in1 settled sp_settled e_ready e_exp m_ready yd_done yof_done yob_done f_read fb_ready pre_e
            pre_w sqc_done mix_sums y_ready yt_done yt_out sf_scaled xd_ready out_copied x_back x1_saved pads
            gate_copied gate_conv gelu_done f_ready o2_copied x1_back yo_t yo_copied y_saved sequence_saved
            const started dve_step scratch rpb_pad table_read table_masked table_saved"""
        S = {n: sem(n) for n in names.split()}
        w_in_sem = [S[f"w_in{i}"] for i in range(RAW_SLOTS)]
        CONSTS = 8

        def start(name, k):
            assert k > 0 or name in STARTED, name
            return int(name in STARTED)

        block = ctx.enter_context(nc.Block())

        @block.sync
        def _(sp):
            sp.dma_start(prm[:, :], params).then_inc(S["params_in"], 16)
            sp.wait_ge(S["started"], len(STARTED))
            with sp.Fori(0, SEQS) as s:
                def nth(name, k):
                    return s * PER[name] + k + start(name, k)

                def load(b, src):
                    for j, u in enumerate(range(UNITS_TO[b], UNITS_TO[b + 1])):
                        n = UNIT_CHUNKS[u]
                        sp.wait_ge(S["lo_split"], nth("lo_split", max(0, u - RAW_SLOTS + 1)))
                        sp.dma_start(raw[:, u % RAW_SLOTS, 0:n * P], src[:, j * UC * P:(j * UC + n) * P]
                                     ).then_inc(w_in_sem[u % RAW_SLOTS], 16)

                load(0, w_in[0])
                sp.wait_ge(S["weights_used"], nth("weights_used", 0))
                sp.sem_inc(S["sp_settled"], 1)
                for i in range(TT):
                    sp.dma_start(arena[:, H + i, :], x[bass.ds(s, 1), i * P:(i + 1) * P, :].rearrange("a p n -> (a p) n")
                                 ).then_inc(S["x_in"], 16)
                for b in range(1, IN_BLOCKS):
                    load(b, w_in[b])
                sp.wait_ge(S["yt_out"], nth("yt_out", TT))
                for b in range(OUT_BLOCKS):
                    load(B_OUT + b, w_out[b])
                for b in range(GU_BLOCKS):
                    load(B_GU + b, w_gu[b])
                for b in range(DOWN_BLOCKS):
                    load(B_DOWN + b, w_down[b % KD])

        @block.tensor
        def _(pe):
            pe.wait_ge(S["const"], CONSTS)
            pe.wait_ge(S["params_in"], 16)
            with pe.Fori(0, SEQS) as s:
                def nth(name, k):
                    return s * PER[name] + k + start(name, k)

                def product(out, u, kk, hi, lo, first, last):
                    w = slice(kk * P, (kk + 1) * P)
                    nc.tensor.matmul(out, whi[:, u % SPLIT_SLOTS, w], hi, start=first, stop=False)
                    nc.tensor.matmul(out, whi[:, u % SPLIT_SLOTS, w], lo, start=False, stop=False)
                    return nc.tensor.matmul(out, wlo[:, u % SPLIT_SLOTS, w], hi, start=False, stop=last)

                def gemm_unit(b, j, bank, hi, lo, ready=None, part=None):
                    u, kc = UNITS_TO[b] + j, j * UC
                    pe.wait_ge(S["lo_split"], nth("lo_split", u + 1))
                    for kk in range(UNIT_CHUNKS[u]) if part is None else range(part * UC // 2, (part + 1) * UC // 2):
                        if ready:
                            ready(kc + kk)
                        for h in range(2):
                            cs = slice(h * HALF, (h + 1) * HALF)
                            m = product(G[:, 2 * bank + h, :], u, kk, arena_r[:, hi[kc + kk], cs], arena_r[:, lo[kc + kk], cs],
                                        kc + kk == 0, kc + kk == chunks_of(b) - 1)
                    if part != 0:
                        m.then_inc(S["weights_used"], 1)

                def gemm(b, bank, hi, lo, ready=None):
                    for j in range(UNITS_TO[b + 1] - UNITS_TO[b]):
                        gemm_unit(b, j, bank, hi, lo, ready)

                h_hi, h_lo = [H + k for k in range(KD)], [H_LO + k for k in range(KD)]

                nsq = [0]
                nn = [0]

                def sums(k, last):
                    if k == 0:
                        pe.wait_ge(S["srt_done"], nth("srt_done", nn[0]))
                    nsq[0] += 1
                    pe.wait_ge(S["sq_done"], nth("sq_done", nsq[0]))
                    for i in range(TT):
                        m = nc.tensor.matmul(A[:, 3, i:i + 1], t(k, P, i * P), ones[:, 0:1],
                                             start=(k == 0 and i == 0), stop=last, skip_group_check=True)
                    m.then_inc(S["sq_used"], 1)

                def added_sums():
                    pe.wait_ge(S["srt_done"], nth("srt_done", nn[0]))
                    nsq[0] += KD - 1
                    pe.wait_ge(S["sq_used"], nth("sq_used", nsq[0]))
                    for h in range(2):
                        nc.tensor.matmul(A[:, 2 + h, :], ones[:, :], t(2, HALF, h * HALF), start=True, stop=False, skip_group_check=True)

                def all_sums(k):
                    if k == 0:
                        pe.wait_ge(S["srt_done"], nth("srt_done", nn[0]))
                    nsq[0] += 1
                    pe.wait_ge(S["sq_done"], nth("sq_done", nsq[0]))
                    for h in range(2):
                        m = nc.tensor.matmul(A[:, 2 + h, :], ones[:, :], t(nsq[0] % 2, HALF, h * HALF),
                                             start=(k == 0), stop=(k == KD - 1), skip_group_check=True)
                    m.then_inc(S["sq_used"], 1)
                    if k == KD - 1:
                        nn[0] += 1

                def spread(to):
                    nn[0] += 1
                    pe.wait_ge(S["diag_done"], nth("diag_done", 1))
                    for n, banks in enumerate(to):
                        for i in range(TT):
                            m = nc.tensor.matmul(banks[:, i // 4, (i % 4) * P:(i % 4 + 1) * P], ones[:, :], t(2 + n, P, i * P),
                                                 start=True, stop=True)
                    m.then_inc(S["rs_done"], 1)

                pe.wait_ge(S["x_in"], nth("x_in", 16 * TT))
                pe.wait_ge(S["yo_copied"], nth("yo_copied", 0))
                for i in range(16):
                    k, h = divmod(i, 2)
                    if i >= 4:
                        pe.wait_ge(S["xt_out"], nth("xt_out", i - 3))
                    for j in range(4):
                        m = nc.tensor.transpose(G[:, i % 4, j * P:(j + 1) * P], arena[:, H + 4 * h + j, k * P:(k + 1) * P], ident[:, :])
                    m.then_inc(S["xt_done"], 1)
                    if h and k:
                        all_sums(k - 1)
                all_sums(KD - 1)
                pe.wait_ge(S["xt_out"], nth("xt_out", 16))
                for b in range(13):
                    pe.wait_ge(S["in_copied"], nth("in_copied", max(0, b - 1)))
                    gemm(b, b % 2, h_hi, h_lo, (lambda k: pe.wait_ge(S["norm_applied"], nth("norm_applied", k + 1))) if b == 0 else None)
                pe.wait_ge(S["in_copied"], nth("in_copied", 12))
                for i in range(TT):
                    if i >= 2:
                        pe.wait_ge(S["v_out"], nth("v_out", i - 1))
                    for j in range(4):
                        m = nc.tensor.transpose(A[:, 2 + i % 2, j * P:(j + 1) * P], arena[:, VT + j, i * P:(i + 1) * P], ident[:, :])
                    m.then_inc(S["vt_done"], 1)
                for b in range(13, 17):
                    pe.wait_ge(S["in_copied"], nth("in_copied", b - 1))
                    gemm(b, b % 2, h_hi, h_lo)
                pe.wait_ge(S["v_out"], nth("v_out", TT))
                for st in range(UNITS + 2):
                    if st < UNITS:
                        rs = min(max(st % ROWS - KR // 2, 0), ROWS - KR)
                        pe.wait_ge(S["q_ready"], nth("q_ready", st + 1))
                        if st >= 2:
                            pe.wait_ge(S["s_biased"], nth("s_biased", st - 1))
                        nc.tensor.matmul(A[:, st % 2, :], qb[:, st % 2, :],
                                         arena[:, K + st // ROWS, rs * GRID_W:rs * GRID_W + KEYS],
                                         start=True, stop=True).then_inc(S["s_done"], 1)
                        b = 17 + st // 4
                        if st % 4 == 0:
                            pe.wait_ge(S["in_copied"], nth("in_copied", b - 1))
                        gemm_unit(b, st % 4 // 2, b % 2, h_hi, h_lo, part=st % 2)
                    if 1 <= st <= UNITS:
                        u = st - 1
                        pe.wait_ge(S["p_scaled"], nth("p_scaled", u + 1))
                        if u >= 1:
                            pe.wait_ge(S["pt_out"], nth("pt_out", u))
                        for j in range(4):
                            m = nc.tensor.transpose(A[:, 2, j * P:(j + 1) * P], pbuf[:, u % 2, j * P:(j + 1) * P], ident[:, :])
                        m.then_inc(S["pt_done"], 1)
                    if st >= 2:
                        u = st - 2
                        rs = min(max(u % ROWS - KR // 2, 0), ROWS - KR)
                        pe.wait_ge(S["pt_out"], nth("pt_out", u + 1))
                        pe.wait_ge(S["v_in"], nth("v_in", 32 * (u // ROWS + 1)))
                        if u >= 1:
                            pe.wait_ge(S["o_out"], nth("o_out", u))
                        for j in range(4):
                            vv = (v_even if rs % 2 == 0 else v_odd)[:, rs // 2 + j, :]
                            m = nc.tensor.matmul(A[:, 3, 0:P], vv, ptbuf[:, u % 2, j * P:(j + 1) * P], start=(j == 0), stop=(j == 3))
                        m.then_inc(S["o_done"], 1)
                pe.wait_ge(S["o_out"], nth("o_out", UNITS))
                pe.wait_ge(S["silu_done"], nth("silu_done", 20))
                pe.wait_ge(S["rows_ready"], nth("rows_ready", 1))
                pe.wait_ge(S["in_copied"], nth("in_copied", IN_BLOCKS))
                for c in range(TT):
                    for part in range(3):
                        i = 3 * c + part
                        if i >= 3:
                            pe.wait_ge(S["xtok_out"], nth("xtok_out", i - 2))
                        n = 4 if part < 2 else 2
                        for j in range(n):
                            m = nc.tensor.transpose(A[:, i % 3, j * P:(j + 1) * P],
                                                    arena[:, XBC + 4 * part + j, c * P:(c + 1) * P], ident[:, :])
                        if part == 2:
                            m = nc.tensor.transpose(A[:, i % 3, 2 * P:2 * P + 96], rows[0:96, c * P:(c + 1) * P], ident[0:96, 0:96])
                        m.then_inc(S["xtok_done"], 1)
                pe.wait_ge(S["xtok_out"], nth("xtok_out", 3 * TT))
                nc.tensor.matmul(G[:, 0, 0:TT * 32], last, scal[:, :, 32:64], start=True, stop=True)
                nc.tensor.matmul(G[:, 1, 0:TT * 32], first, scal[:, :, 64:96], start=True, stop=True).then_inc(S["tot_done"], 1)

                def state(c, x_at, banks):
                    for g in range(GROUPS):
                        m = nc.tensor.matmul(G[:, banks + g, :], arena[:, BTOK + c // 4, (c % 4) * 256 + g * P:(c % 4) * 256 + (g + 1) * P],
                                             arena[:, x_at, g * HALF:(g + 1) * HALF], start=True, stop=True)
                    m.then_inc(S["st_done"], 1)

                def incoming(c, state_at, to, done):
                    for g in range(GROUPS):
                        m = nc.tensor.matmul(to[:, g, :], arena[:, C_T + g, c * P:(c + 1) * P],
                                             arena[:, state_at, g * HALF:(g + 1) * HALF], start=True, stop=True)
                    m.then_inc(S[done], 1)

                def inner(c):
                    for g in range(GROUPS):
                        m = nc.tensor.matmul(A[:, 0, (c % 2) * 256 + g * P:(c % 2) * 256 + (g + 1) * P], arena[:, B_T + g, c * P:(c + 1) * P],
                                             arena[:, C_T + g, c * P:(c + 1) * P], start=True, stop=True)
                    m.then_inc(S["cb_done"], 1)

                def from_states(c, g, first):
                    parts = ([SB + c - 1] if c else []) + ([SB + c] if c < TT - 1 else [])
                    for n, at_ in enumerate(parts):
                        nc.tensor.matmul(G[:, g, :], ident[:, :], arena[:, at_, g * HALF:(g + 1) * HALF],
                                         start=first and n == 0, stop=False, skip_group_check=True)

                def within(c, g, first):
                    pe.wait_ge(S["m_ready"], nth("m_ready", 2 * c + g + 1))
                    for hd in range(GH):
                        m = nc.tensor.matmul(G[:, g, hd * SP_:(hd + 1) * SP_], t(2 * g, P, hd * P),
                                             arena[:, H + c, g * HALF + hd * SP_:g * HALF + (hd + 1) * SP_],
                                             start=first and hd == 0, stop=True, skip_group_check=True)
                    m.then_inc(S["yd_done"], 1)

                def turn(c):
                    pe.wait_ge(S["y_ready"], nth("y_ready", c + 1))
                    for i in range(8):
                        m = nc.tensor.transpose(A[:, 1 + i // 4, i % 4 * P:(i % 4 + 1) * P], arena[:, YBUF, i * P:(i + 1) * P], ident[:, :])
                    m.then_inc(S["yt_done"], 1)

                def tile_sums(c):
                    pe.wait_ge(S["sqc_done"], nth("sqc_done", c + 1))
                    for i in range(8):
                        m = nc.tensor.matmul(A[:, 3, 8 + (i // 4) * TT + c:9 + (i // 4) * TT + c], arena[:, H + c, i * P:(i + 1) * P],
                                             ones[:, 0:1], start=(i % 4 == 0), stop=(i % 4 == 3), skip_group_check=True)
                    if c == TT - 1:
                        m.then_inc(S["mix_sums"], 1)

                pe.wait_ge(S["coef_out"], nth("coef_out", 1))
                for i, c in enumerate(range(TT - 1, 0, -1)):
                    pe.wait_ge(S["xw_ready"], nth("xw_ready", i + 1))
                    if i >= 2:
                        pe.wait_ge(S["st_read"], nth("st_read", i - 1))
                    state(c, (XW, YBUF)[i % 2], 2 * (i % 2))
                    if i < 4:
                        sums(i, i == 3)
                pe.wait_ge(S["st_read"], nth("st_read", 7))
                inner(0)
                for c in range(TT):
                    if c:
                        pe.wait_ge(S["st_read"], nth("st_read", 7 + c))
                        incoming(c, SF, G[:, 2:4, :], "yof_done")
                    if c < TT - 1:
                        pe.wait_ge(S["cb_out"], nth("cb_out", c + 1))
                        inner(c + 1)
                    if c:
                        pe.wait_ge(S["fb_ready"], nth("fb_ready", c))
                        turn(c - 1)
                    within(c, 0, True)
                    if c:
                        pe.wait_ge(S["yt_out"], nth("yt_out", c))
                    if c < TT - 1:
                        incoming(c, SB + c, A[:, 1:3, :], "yob_done")
                        pe.wait_ge(S["xw_ready"], nth("xw_ready", 7 + c + 1))
                        if c:
                            pe.wait_ge(S["f_read"], nth("f_read", c))
                        state(c, XW, 2)
                    if c >= 2:
                        tile_sums(c - 2)
                    pe.wait_ge(S["fb_ready"], nth("fb_ready", c + 1))
                    for g in range(GROUPS):
                        from_states(c, g, g == 1)
                    within(c, 1, False)
                turn(TT - 1)
                tile_sums(TT - 2)
                tile_sums(TT - 1)
                spread([G[:, 2:4, :], A[:, 0:2, :], A[:, 2:4, :]])
                for b in range(OUT_BLOCKS):
                    if b >= 2:
                        pe.wait_ge(S["out_copied"], nth("out_copied", b - 1))
                    if b == 1:
                        pe.wait_ge(S["norm_applied"], nth("norm_applied", 20))
                    gemm(B_OUT + b, b % 2, MIX_HI, MIX_LO,
                         (lambda k: pe.wait_ge(S["norm_applied"], nth("norm_applied", 8 + k + 1))) if b == 0 else None)
                added_sums()
                all_sums(KD - 1)
                pe.wait_ge(S["out_copied"], nth("out_copied", OUT_BLOCKS))
                for k in range(KD):
                    all_sums(k)
                for p in range(FK):
                    pe.wait_ge(S["gate_copied"], nth("gate_copied", p))
                    gemm(B_GU + 2 * p, 0, h_hi, h_lo, (lambda k: pe.wait_ge(S["norm_applied"], nth("norm_applied", 28 + k + 1))) if p == 0 else None)
                    pe.wait_ge(S["f_ready"], nth("f_ready", p))
                    gemm(B_GU + 2 * p + 1, 1, h_hi, h_lo)

                def half_sums(half):
                    if half == 0:
                        pe.wait_ge(S["srt_done"], nth("srt_done", nn[0]))
                    nsq[0] += KD - 1
                    pe.wait_ge(S["sq_used"], nth("sq_used", nsq[0]))
                    nc.tensor.matmul(A[:, 2 + half, :], ones[:, :], t(1, HALF, half * HALF), start=True, stop=False, skip_group_check=True)
                    nsq[0] += 1
                    pe.wait_ge(S["sq_done"], nth("sq_done", nsq[0]))
                    nc.tensor.matmul(A[:, 2 + half, :], ones[:, :], t(0, HALF, nsq[0] % 2 * HALF), start=False, stop=True,
                                     skip_group_check=True).then_inc(S["sq_used"], 1)

                def turn_half(half):
                    for i in range(8):
                        g, tile = divmod(i, 4)
                        if tile == 0:
                            pe.wait_ge(S["norm_applied"], nth("norm_applied", NAPPLIED - 16 + 8 * half + 4 * g + 4))
                        n = 8 * half + i
                        if n >= 4:
                            pe.wait_ge(S["yo_copied"], nth("yo_copied", n - 3))
                        for j in range(4):
                            m = nc.tensor.transpose(y_bank(n)[:, j * P:(j + 1) * P],
                                                    o_chunk(4 * g + j)[:, half * HALF + tile * P:half * HALF + (tile + 1) * P], ident[:, :])
                        m.then_inc(S["yo_t"], 1)

                for i in range(DOWN_BLOCKS):
                    half, j = divmod(i, KD)
                    if i == 0:
                        pe.wait_ge(S["gate_copied"], nth("gate_copied", FK))
                        pe.wait_ge(S["f_ready"], nth("f_ready", FK))
                    if i >= 2:
                        pe.wait_ge(S["o2_copied"], nth("o2_copied", i - 1))
                    b = B_DOWN + i
                    cs = slice(half * HALF, (half + 1) * HALF)
                    for u in range(UNITS_TO[b], UNITS_TO[b + 1]):
                        pe.wait_ge(S["lo_split"], nth("lo_split", u + 1))
                        for kk in range(UNIT_CHUNKS[u]):
                            k = (u - UNITS_TO[b]) * UC + kk
                            if j == 0:
                                pe.wait_ge(S["flo_done"], nth("flo_done", half * FK + k + 1))
                            m = product(G[:, 2 * (i % 2), :], u, kk, fhi(k), f_r(k, cs), k == 0, k == FK - 1)
                        m.then_inc(S["weights_used"], 1)
                    if i == KD:
                        half_sums(0)
                    if i == LAST_TURN:
                        turn_half(0)
                half_sums(1)
                turn_half(1)

        @block.scalar
        def _(act):
            act.wait_ge(S["const"], CONSTS)
            act.wait_ge(S["params_in"], 16)
            nc.scalar.mul(hconv[:, :], prm[:, PC["conv_w"]:PC["conv_w"] + 72], 0.5)
            nc.scalar.activation(acol[0:32, :], prm[0:32, PC["a_log"]:PC["a_log"] + 1], ACT.Exp).then_inc(S["scratch"], 1)
            act.wait_ge(S["scratch"], 1)
            nc.scalar.mul(acol[0:32, :], acol[0:32, :], -1.0).then_inc(S["scratch"], 1)
            with act.Fori(0, SEQS) as s:
                def nth(name, k):
                    return s * PER[name] + k + start(name, k)

                nsq = [0]
                nn = [0]
                units = [0]
                his = [0]

                def split_to(n):
                    while units[0] < min(n, UNITS_W):
                        u = units[0]
                        act.wait_ge(w_in_sem[u % RAW_SLOTS], (s * LOADS[u % RAW_SLOTS] + u // RAW_SLOTS + 1) * 16)
                        act.wait_ge(S["weights_used"], nth("weights_used", max(0, u - SPLIT_SLOTS + 1)))
                        w = slice(0, UNIT_CHUNKS[u] * P)
                        nc.scalar.copy(whi[:, u % SPLIT_SLOTS, w], raw[:, u % RAW_SLOTS, w]).then_inc(S["hi_split"], 1)
                        units[0] += 1

                def first_parts(to):
                    for c in to:
                        his[0] += 1
                        act.wait_ge(S["full_ready"], nth("full_ready", his[0]))
                        nc.scalar.copy(arena_r[:, c, :], t(5 + his[0] % 2)).then_inc(S["hi_done"], 1)

                def square(src, to=None):
                    nsq[0] += 1
                    act.wait_ge(S["sq_used"], nth("sq_used", max(0, nsq[0] - 2)))
                    nc.scalar.activation(t(nsq[0] % 2) if to is None else to, src, ACT.Square).then_inc(S["sq_done"], 1)

                def half_square(src, to=None):
                    nsq[0] += 1
                    act.wait_ge(S["sq_used"], nth("sq_used", nsq[0] - 2))
                    nc.scalar.activation(t(0, HALF, nsq[0] % 2 * HALF) if to is None else to, src, ACT.Square).then_inc(S["sq_done"], 1)

                def root(to):
                    act.wait_ge(S["sq_used"], nth("sq_used", nsq[0]))
                    nc.scalar.activation(to, A[:, 2:4, :].rearrange("p a n -> p (a n)"), ACT.Sqrt, bias=epsc[:, :], scale=1.0 / D
                                         ).then_inc(S["srt_done"], 1)

                act.wait_ge(S["norm_applied"], nth("norm_applied", 0))
                act.wait_ge(S["sequence_saved"], nth("sequence_saved", 0))
                for i in range(16):
                    k, h = divmod(i, 2)
                    act.wait_ge(S["xt_done"], nth("xt_done", i + 1))
                    nc.scalar.copy(arena[:, RAW + k, h * HALF:(h + 1) * HALF], G[:, i % 4, :]).then_inc(S["xt_out"], 1)
                    if h:
                        act.wait_ge(S["xt_out"], nth("xt_out", i + 1))
                        square(arena[:, RAW + k, :])
                split_to(3)
                root(t(7))
                first_parts(range(H, H + KD))

                def used(b):
                    split_to(uend(b) + 2)
                    act.wait_ge(S["weights_used"], nth("weights_used", uend(b)))

                def psum(b):
                    return G[:, 2 * (b % 2):2 * (b % 2) + 2, :].rearrange("p a n -> p (a n)")

                act.wait_ge(S["table_saved"], 16)
                for b in range(12):
                    used(b)
                    to = (Q, K, VT)[b // 4] + b % 4
                    if b < 4:
                        nc.scalar.mul(arena[:, to, :], psum(b), DH ** -0.5).then_inc(S["in_copied"], 1)
                    else:
                        nc.scalar.copy(arena[:, to, :], psum(b)).then_inc(S["in_copied"], 1)
                used(DT_BLOCK)
                nc.scalar.activation(t(0)[0:32], psum(DT_BLOCK)[0:32], ACT.Identity,
                                     bias=prm[0:32, PC["dt_bias"]:PC["dt_bias"] + 1]).then_inc(S["in_copied"], 1)
                act.wait_ge(S["pads"], nth("pads", 1))

                def z_saved(m, k):
                    act.wait_ge(S[f"z_saved{m % 2}"], nth(f"z_saved{m % 2}", 16 * k))

                def copy_z(i, m):
                    used(13 + i if i < 4 else 17 + m)
                    nc.scalar.mul(t(2 + m % 2, T, 2), psum(13 + i if i < 4 else 17 + m), 0.5).then_inc(S["in_copied"], 1)

                def tanh_half(i, src):
                    act.wait_ge(S["silu_done"], nth("silu_done", i))
                    nc.scalar.activation(t(4), src, ACT.Tanh).then_inc(S["tanh_done"], 1)

                for i in range(4):
                    if i >= 2:
                        z_saved(i, 1)
                    copy_z(i, i)
                    if i == 0:
                        act.wait_ge(S["exp_dt"], nth("exp_dt", 1))
                        nc.scalar.activation(t(1)[0:32], t(1)[0:32], ACT.Exp, scale=-1.0).then_inc(S["exp_dt_out"], 1)
                    act.wait_ge(S["in_copied"], nth("in_copied", 14 + i))
                    tanh_half(i, t(2 + i % 2, T, 2))
                for st in range(UNITS + 10):
                    split_to(min(UNITS_TO[17] + st // 2 + 2, UNITS_TO[B_OUT]))
                    if st < UNITS:
                        act.wait_ge(S["s_biased"], nth("s_biased", st + 1))
                        nc.scalar.activation(pbuf[:, st % 2, :], pbuf[:, st % 2, :], ACT.Exp, bias=nmx[:, st % 2:st % 2 + 1],
                                             accum_out=rsum[:, st % 2:st % 2 + 1]).then_inc(S["p_exp"], 1)
                    if 1 <= st <= UNITS:
                        u = st - 1
                        act.wait_ge(S["pt_done"], nth("pt_done", u + 1))
                        act.wait_ge(S["o_done"], nth("o_done", max(0, u - 1)))
                        nc.scalar.copy(ptbuf[:, u % 2, :], A[:, 2, :]).then_inc(S["pt_out"], 1)
                    if 2 <= st < UNITS + 2:
                        u = st - 2
                        act.wait_ge(S["o_done"], nth("o_done", u + 1))
                        r = u % ROWS
                        for hh in range(2):
                            o = nc.scalar.copy(arena[hh * 64:(hh + 1) * 64, Q + u // ROWS, r * 64:(r + 1) * 64],
                                               A[hh * 64:(hh + 1) * 64, 3, hh * 64:(hh + 1) * 64])
                        o.then_inc(S["o_out"], 1)
                    if st % 4 == 0 and 4 <= st <= UNITS:
                        m = st // 4 - 1
                        if m < 2:
                            z_saved(m, 2)
                        elif m % 4 == 1:
                            z_saved(m, 2 + m // 4)
                        else:
                            act.wait_ge(S["conv_done"], nth("conv_done", 3 * ((m - 2) // 4) + (m - 2) % 4 + 1))
                        if m % 4 < 3:
                            act.wait_ge(S["weights_used"], nth("weights_used", uend(17 + m)))
                            nc.scalar.copy(t(2 + m % 2, T, 2), psum(17 + m)).then_inc(S["in_copied"], 1)
                        else:
                            act.wait_ge(S["weights_used"], nth("weights_used", uend(17 + m)))
                            nc.scalar.mul(t(2 + m % 2, T, 2), psum(17 + m), 0.5).then_inc(S["in_copied"], 1)
                    if st % 4 == 0 and 8 <= st and (st // 4 - 2) % 4 < 3 and st // 4 - 2 < 16:
                        m = st // 4 - 2
                        j = 3 * (m // 4) + m % 4
                        act.wait_ge(S["conv_done"], nth("conv_done", j + 1))
                        tanh_half(4 + m, arena[:, XBC + j, :])
                    if st % 4 == 1 and 4 < st and (st // 4 - 1) % 4 == 3 and st // 4 - 1 < 16:
                        m = st // 4 - 1
                        act.wait_ge(S["in_copied"], nth("in_copied", 18 + m))
                        tanh_half(4 + m, t(2 + m % 2, T, 2))

                act.wait_ge(S["o_out"], nth("o_out", UNITS))
                act.wait_ge(S["silu_done"], nth("silu_done", 20))
                act.wait_ge(S["z_saved1"], nth("z_saved1", 16 * Z_SAVES[1]))
                for k in range(4):
                    nsq[0] += 1
                    nc.scalar.activation(t(k), arena[:, Q + k, :], ACT.Square).then_inc(S["sq_done"], 1)

                def broadcast_sums(c, g):
                    for d in range(2):
                        src = bass.AP(cs_dram.tensor, (d * 32 + d * SH + g * GH) * T + c * P, [[0, P], [T, GH], [1, P]])
                        act.dma_start(bc(g, d), src).then_inc(S[f"bc_in{g}"], 16)

                act.wait_ge(S["silu_done"], nth("silu_done", 20))
                act.wait_ge(S["o_done"], nth("o_done", UNITS))
                act.wait_ge(S["rows_saved"], nth("rows_saved", 32))
                for g in range(GROUPS):
                    broadcast_sums(0, g)
                for i in range(3 * TT):
                    c, part = divmod(i, 3)
                    act.wait_ge(S["xtok_done"], nth("xtok_done", i + 1))
                    if part < 2:
                        nc.scalar.copy(arena[:, H + c, part * HALF:(part + 1) * HALF], A[:, i % 3, :]).then_inc(S["xtok_out"], 1)
                    else:
                        nc.scalar.copy(arena[:, BTOK + c // 4, (c % 4) * 256:(c % 4 + 1) * 256], A[:, i % 3, 0:256])
                        nc.scalar.mul(nscal[:, c, :], A[:, i % 3, 288:304], -1.0)
                        nc.scalar.copy(scal[:, c, :], A[:, i % 3, 256:352]).then_inc(S["xtok_out"], 1)
                act.wait_ge(S["coef_in"], nth("coef_in", 1))
                for d in range(2):
                    hs = slice(d * SH, (d + 1) * SH)
                    tot = G[:, d, 0:TT * 32].rearrange("p (c n) -> p c n", c=TT)[:, :, hs]
                    nc.scalar.activation(dtot[:, :, hs], tot, ACT.Exp)
                    nc.scalar.activation(ecs[:, :, hs], scal[:, :, 32 + d * 48:48 + d * 48], ACT.Exp)
                nc.scalar.activation(wst[:, :, :], wst[:, :, :], ACT.Exp).then_inc(S["coef_exp"], 1)

                def prepare(i):
                    c, g = divmod(i, 2)
                    act.wait_ge(S[f"bc_in{g}"], nth(f"bc_in{g}", 32 * (c + 1)))
                    if i >= 2:
                        act.wait_ge(S["yd_done"], nth("yd_done", i - 1))
                    for h in range(GH):
                        n = g * GH + h
                        m = nc.scalar.activation(t(2 * g, P, h * P), bc(g, 0)[:, h, :], ACT.Identity, bias=nscal[:, c, n:n + 1])
                    m.then_inc(S["pre_e"], 1)
                    act.wait_ge(S["cb_out"], nth("cb_out", c + 1))
                    for h in range(GH):
                        n = g * GH + h
                        lo = (c % 2) * HALF + 256 + g * P
                        m = nc.scalar.mul(t(2 * g + 1, P, h * P), rows[:, lo:lo + P], scal[:, c, 16 + n:17 + n])
                    m.then_inc(S["pre_w"], 1)

                def tile_squares(c):
                    act.wait_ge(S["yt_out"], nth("yt_out", c + 1))
                    nc.scalar.activation(arena[:, H + c, :].rearrange("p (k n) -> p k n", k=KD), arena[:, Z:Z + KD, c * P:(c + 1) * P],
                                         ACT.Square).then_inc(S["sqc_done"], 1)

                act.wait_ge(S["sq_used"], nth("sq_used", nsq[0]))
                act.wait_ge(S["xtok_out"], nth("xtok_out", 3 * TT))
                prepare(0)
                for i in range(2 * TT):
                    c, g = divmod(i, 2)
                    act.wait_ge(S["e_ready"], nth("e_ready", i + 1))
                    nc.scalar.activation(t(2 * g), t(2 * g), ACT.Exp).then_inc(S["e_exp"], 1)
                    if c < TT - 1:
                        broadcast_sums(c + 1, g)
                    if i + 1 < 2 * TT:
                        prepare(i + 1)
                    if g == 0 and c >= 2:
                        tile_squares(c - 2)
                tile_squares(TT - 2)
                tile_squares(TT - 1)
                split_to(UNITS_TO[B_OUT] + 3)
                act.wait_ge(S["mix_sums"], nth("mix_sums", 1))
                nc.scalar.activation(srt[:, :], A[:, 3, 0:3 * TT], ACT.Sqrt, bias=epsc[:, :], scale=1.0 / 512).then_inc(S["srt_done"], 1)
                first_parts(MIX_HI)
                for j in range(OUT_BLOCKS):
                    used(B_OUT + j)
                    nc.scalar.copy(arena[:, Z + j, :], psum(j)).then_inc(S["out_copied"], 1)
                    act.wait_ge(S["out_copied"], nth("out_copied", j + 1))
                    square(arena[:, Z + j, :], None if j else t(2))
                root(t(7))
                split_to(UNITS_TO[B_GU] + 3)
                for k in range(KD):
                    act.wait_ge(S["norm_applied"], nth("norm_applied", 21 + k))
                    square(arena[:, RAW + k, :])
                root(t(7))
                first_parts(range(H, H + KD))
                act.wait_ge(S["pads"], nth("pads", 2))
                for p in range(FK):
                    used(B_GU + 2 * p)
                    act.wait_ge(S["gate_conv"], nth("gate_conv", p))
                    nc.scalar.copy(t(2, T, 1), psum(0)).then_inc(S["gate_copied"], 1)
                    split_to(uend(B_GU + 2 * p) + 3)
                    act.wait_ge(S["gate_conv"], nth("gate_conv", p + 1))
                    act.wait_ge(S["f_ready"], nth("f_ready", p))
                    nc.scalar.activation(t(1), t(4), ACT.Gelu_apprx_tanh).then_inc(S["gelu_done"], 1)
                    split_to(uend(B_GU + 2 * p) + 4)
                def copy_o(i):
                    half, j = divmod(i, KD)
                    used(B_DOWN + i)
                    nc.scalar.copy(o_chunk(j)[:, half * HALF:(half + 1) * HALF], G[:, 2 * (i % 2), :]).then_inc(S["o2_copied"], 1)
                    act.wait_ge(S["o2_copied"], nth("o2_copied", i + 1))
                    half_square(o_chunk(j)[:, half * HALF:(half + 1) * HALF], None if j else t(1, HALF, half * HALF))

                def half_root(half):
                    act.wait_ge(S["sq_used"], nth("sq_used", NSQ - 16 + 8 * half + 8))
                    nc.scalar.activation(t(2, HALF, half * HALF), A[:, 2 + half, :], ACT.Sqrt, bias=epsc[:, :], scale=1.0 / D
                                         ).then_inc(S["srt_done"], 1)

                def results(half):
                    for n in range(8 * half, 8 * half + 8):
                        act.wait_ge(S["yo_t"], nth("yo_t", n + 1))
                        nc.scalar.copy(y_part(n), y_bank(n)).then_inc(S["yo_copied"], 1)

                for i in range(DOWN_BLOCKS):
                    half, j = divmod(i, KD)
                    if j == 0:
                        for k in range(FK):
                            split_to(down_ahead(half, k))
                            if half:
                                act.wait_ge(S["weights_used"], nth("weights_used", UNITS_TO[B_DOWN + i - 1] + k // UC + 1))
                            elif k == 0:
                                act.wait_ge(S["weights_used"], nth("weights_used", UNITS_TO[B_DOWN]))
                            act.wait_ge(S["f_ready"], nth("f_ready", k + 1))
                            nc.scalar.copy(fhi(k), f_full(k, slice(half * HALF, (half + 1) * HALF))).then_inc(S["fhi_done"], 1)
                        if half:
                            copy_o(KD - 1)
                    if i != KD - 1:
                        copy_o(i)
                    if i == KD:
                        half_root(0)
                    if i == LAST_TURN:
                        results(0)
                half_root(1)
                results(1)

        @block.vector
        def _(dve):
            dve.wait_ge(S["const"], CONSTS)
            dve.wait_ge(S["params_in"], 16)
            dve.wait_ge(S["scratch"], 2)
            with dve.Fori(0, SEQS) as s:
                def nth(name, k):
                    return s * PER[name] + k + start(name, k)

                links = [0]

                def step():
                    links[0] += 1
                    return links[0]

                tt, ts, stt = nc.vector.tensor_tensor, nc.vector.tensor_scalar, nc.vector.scalar_tensor_tensor
                nn = [0]
                applied = [0]
                rs = G[:, 2:4, :].rearrange("p a n -> p (a n)")

                def col(name, k):
                    return prm[:, PC[name] + k:PC[name] + k + 1]

                units, fulls = [0], [0]

                def split_to(n):
                    while units[0] < min(n, UNITS_W):
                        u = units[0]
                        dve.wait_ge(S["hi_split"], nth("hi_split", u + 1))
                        w = slice(0, UNIT_CHUNKS[u] * P)
                        tt(wlo[:, u % SPLIT_SLOTS, w], raw[:, u % RAW_SLOTS, w], whi[:, u % SPLIT_SLOTS, w].bitcast(F),
                           ALU.subtract).then_inc(S["lo_split"], 1)
                        units[0] += 1

                def inverse_root(at):
                    nn[0] += 1
                    dve.wait_ge(S["srt_done"], nth("srt_done", nn[0]))
                    nc.vector.reciprocal(at, at).then_inc(S["dve_step"], 1)
                    dve.wait_ge(S["dve_step"], nth("dve_step", step()))
                    return at

                def norm_split(items, hi, lo):
                    dve.wait_ge(S["norm_applied"], nth("norm_applied", applied[0]))

                    def second(k, n):
                        dve.wait_ge(S["hi_done"], nth("hi_done", n))
                        tt(arena_r[:, lo[k], :], t(5 + n % 2), arena_r[:, hi[k], :].bitcast(F), ALU.subtract
                           ).then_inc(S["norm_applied"], 1)
                        applied[0] += 1

                    for k, (src, gain, inverse) in enumerate(items):
                        fulls[0] += 1
                        if k >= 2:
                            dve.wait_ge(S["norm_applied"], nth("norm_applied", applied[0]))
                        stt(t(5 + fulls[0] % 2), arena[:, src, :], gain, inverse, ALU.mult, ALU.mult).then_inc(S["full_ready"], 1)
                        if k:
                            second(k - 1, fulls[0] - 1)
                    second(len(items) - 1, fulls[0])

                h_hi, h_lo = [H + k for k in range(KD)], [H_LO + k for k in range(KD)]
                dve.wait_ge(S["yo_t"], nth("yo_t", 0))
                split_to(3)
                inverse = inverse_root(t(7))
                norm_split([(RAW + k, col("mix_pre", k), inverse) for k in range(KD)], h_hi, h_lo)
                split_to(UNITS_TO[DT_BLOCK + 1] + 2)
                dve.wait_ge(S["raw_saved"], nth("raw_saved", 16))
                for i in range(TT):
                    dve.wait_ge(S["vt_done"], nth("vt_done", i + 1))
                    nc.vector.tensor_copy(arena[:, VK + i // 2, (i % 2) * HALF:(i % 2 + 1) * HALF], A[:, 2 + i % 2, :]).then_inc(S["v_out"], 1)
                def silu(i, c):
                    dve.wait_ge(S["tanh_done"], nth("tanh_done", i + 1))
                    stt(c, t(4), 1.0, c, ALU.add, ALU.mult).then_inc(S["silu_done"], 1)

                x_, u_, z_, z2 = (t(i)[0:32] for i in (0, 1, 5, 6))
                dve.wait_ge(S["in_copied"], nth("in_copied", DT_BLOCK + 1))
                stt(u_, x_, -1.0, x_, ALU.mult, ALU.max).then_inc(S["exp_dt"], 1)
                dve.wait_ge(S["exp_dt_out"], nth("exp_dt_out", 1))
                ts(z_, u_, 2.0, None, ALU.add).then_inc(S["dve_step"], 1)
                dve.wait_ge(S["dve_step"], nth("dve_step", step()))
                for n in range(4):
                    part = z_[:, n * 256:(n + 1) * 256]
                    nc.vector.reciprocal(part, part).then_inc(S["dve_step"], 1)
                    dve.wait_ge(S["dve_step"], nth("dve_step", step()))
                    if n % 2:
                        split_to(UNITS_TO[14] + 1 + n // 2)
                tt(z_, z_, u_, ALU.mult).then_inc(S["dve_step"], 1)
                dve.wait_ge(S["dve_step"], nth("dve_step", step()))
                tt(z2, z_, z_, ALU.mult).then_inc(S["dve_step"], 1)
                dve.wait_ge(S["dve_step"], nth("dve_step", step()))
                ts(u_, z2, 1.0 / 17, None, ALU.mult).then_inc(S["dve_step"], 1)
                dve.wait_ge(S["dve_step"], nth("dve_step", step()))
                silu(0, t(2, T, 2))
                for n in range(7, 0, -1):
                    if n == 4:
                        split_to(UNITS_TO[15])
                    stt(u_, u_, 1.0 / (2 * n + 1), z2, ALU.add, ALU.mult).then_inc(S["dve_step"], 1)
                    dve.wait_ge(S["dve_step"], nth("dve_step", step()))
                split_to(UNITS_TO[15] + 2)
                silu(1, t(3, T, 2))
                stt(z_, u_, 1.0, z_, ALU.add, ALU.mult).then_inc(S["dve_step"], 1)
                dve.wait_ge(S["dve_step"], nth("dve_step", step()))
                ts(x_, x_, 0.0, None, ALU.max).then_inc(S["dve_step"], 1)
                dve.wait_ge(S["dve_step"], nth("dve_step", step()))
                stt(rows[0:32, :], z_, 2.0, x_, ALU.mult, ALU.add).then_inc(S["dve_step"], 1)
                dve.wait_ge(S["dve_step"], nth("dve_step", step()))
                ts(x_, rows[0:32, :], acol[0:32, :], None, ALU.mult).then_inc(S["dve_step"], 1)
                dve.wait_ge(S["dve_step"], nth("dve_step", step()))
                split_to(UNITS_TO[15] + 2)
                for c in range(TT):
                    da = x_[:, c * P:(c + 1) * P]
                    nc.vector.tensor_tensor_scan(rows[32:64, c * P:(c + 1) * P], ones[0:32, :], da, 0.0, ALU.mult, ALU.add)
                    m = nc.vector.tensor_tensor_scan(rows[64:96, c * P:(c + 1) * P][:, ::-1], ones[0:32, :], da[:, ::-1], 0.0,
                                                     ALU.mult, ALU.add)
                m.then_inc(S["rows_ready"], 1)

                for i in (2, 3):
                    split_to(UNITS_TO[13 + i] + 4)
                    silu(i, t(2 + i % 2, T, 2))
                split_to(UNITS_TO[17] + 2)
                dve.wait_ge(S["v_saved"], nth("v_saved", 16))
                for st in range(UNITS + 10):
                    split_to(min(UNITS_TO[17] + st // 2 + 2, UNITS_TO[B_OUT]))
                    if st < UNITS:
                        dve.wait_ge(S["s_done"], nth("s_done", st + 1))
                        dve.wait_ge(S["tb_in"], nth("tb_in", 16 * (st // ROWS + 1)))
                        dve.wait_ge(S["pt_done"], nth("pt_done", max(0, st - 1)))
                        if st < 2:
                            dve.wait_ge(S["rows_ready"], nth("rows_ready", 1))
                        dve.sem_inc(S["settled"], 1)
                        rs0 = min(max(st % ROWS - KR // 2, 0), ROWS - KR)
                        ro = rs0 - st % ROWS + KR - 1
                        nc.vector.tensor_tensor_reduce(
                            out=pbuf[:, st % 2, :], in0=A[:, st % 2, :], in1=table[:, ro * 64:ro * 64 + KEYS], scale=1.0,
                            scalar=-3e38, op0=ALU.add, op1=ALU.max, accum_out=mx[:, st % 2:st % 2 + 1]).then_inc(S["dve_step"], 1)
                        dve.wait_ge(S["dve_step"], nth("dve_step", step()))
                        ts(nmx[:, st % 2:st % 2 + 1], mx[:, st % 2:st % 2 + 1], -1.0, None, ALU.mult).then_inc(S["s_biased"], 1)
                    m = st // 4 - 1
                    if 0 <= m < 16 and m % 4 < 3:
                        j = 3 * (m // 4) + m % 4
                        o, cv = arena[:, XBC + j, :], lambda i: t(2 + m % 2, T, i)
                        w = lambda i: hconv[:, 5 * j + i:5 * j + i + 1]
                        if st % 4 == 1:
                            dve.wait_ge(S["in_copied"], nth("in_copied", 18 + m))
                            ts(o, cv(0), w(0), hconv[:, 60 + j:61 + j], ALU.mult, ALU.add).then_inc(S["dve_step"], 1)
                            dve.wait_ge(S["dve_step"], nth("dve_step", step()))
                            stt(o, cv(1), w(1), o, ALU.mult, ALU.add).then_inc(S["dve_step"], 1)
                            dve.wait_ge(S["dve_step"], nth("dve_step", step()))
                        if st % 4 == 2:
                            stt(o, cv(2), w(2), o, ALU.mult, ALU.add).then_inc(S["dve_step"], 1)
                            dve.wait_ge(S["dve_step"], nth("dve_step", step()))
                            stt(o, cv(3), w(3), o, ALU.mult, ALU.add).then_inc(S["dve_step"], 1)
                            dve.wait_ge(S["dve_step"], nth("dve_step", step()))
                        if st % 4 == 3:
                            stt(o, cv(4), w(4), o, ALU.mult, ALU.add).then_inc(S["conv_done"], 1)
                    if 0 <= m < 16 and m % 4 == 3 and st % 4 == 2:
                        silu(4 + m, t(2 + m % 2, T, 2))
                    if st < UNITS:
                        dve.wait_ge(S["p_exp"], nth("p_exp", st + 1))
                        nc.vector.reciprocal(rinv[:, st % 2:st % 2 + 1], rsum[:, st % 2:st % 2 + 1]).then_inc(S["dve_step"], 1)
                        dve.wait_ge(S["dve_step"], nth("dve_step", step()))
                        ts(pbuf[:, st % 2, :], pbuf[:, st % 2, :], rinv[:, st % 2:st % 2 + 1], None, ALU.mult).then_inc(S["p_scaled"], 1)
                    if st % 4 == 0 and 0 <= m - 1 < 16 and (m - 1) % 4 < 3:
                        silu(4 + m - 1, arena[:, XBC + 3 * ((m - 1) // 4) + (m - 1) % 4, :])
                dve.wait_ge(S["tot_done"], nth("tot_done", 1))
                for d in range(2):
                    hs = slice(d * SH, (d + 1) * SH)
                    m = tt(wst[:, :, hs], G[:, d, 0:TT * 32].rearrange("p (c n) -> p c n", c=TT)[:, :, hs],
                           scal[:, :, 32 + d * 48:48 + d * 48], ALU.subtract)
                m.then_inc(S["coef_in"], 1)
                dve.wait_ge(S["coef_exp"], nth("coef_exp", 1))
                tt(wst[:, :, :], wst[:, :, :], scal[:, :, 0:32], ALU.mult).then_inc(S["coef_out"], 1)

                def per_head(coef, c, d):
                    return coef[:, c, d * SH:(d + 1) * SH].unsqueeze(2).broadcast_to([P, SH, SP_])

                def heads(ap):
                    return ap.rearrange("p (h n) -> p h n", h=SH)

                gg = G[:, 0:2, :].rearrange("p a n -> p (a n)")
                g23 = G[:, 2:4, :].rearrange("p a n -> p (a n)")
                a12 = A[:, 1:3, :].rearrange("p a n -> p (a n)")
                for i, c in enumerate(range(TT - 1, 0, -1)):
                    to = arena[:, SB + c - 1, :]
                    if i:
                        tt(heads(to), heads(arena[:, SB + c, :]), per_head(dtot, c, 1), ALU.mult).then_inc(S["dve_step"], 1)
                        dve.wait_ge(S["dve_step"], nth("dve_step", step()))
                    dve.wait_ge(S["st_done"], nth("st_done", i + 1))
                    if i:
                        m = tt(to, (gg, g23)[i % 2], to, ALU.add)
                    else:
                        m = nc.vector.tensor_copy(to, gg)
                    m.then_inc(S["st_read"], 1)
                    dve.wait_ge(S["st_read"], nth("st_read", i + 1))
                dve.wait_ge(S["rows_saved"], nth("rows_saved", 32))
                dve.wait_ge(S["z_back"], nth("z_back", 16))
                yb = arena[:, YBUF, :]

                def masked(c):
                    dve.wait_ge(S["cb_done"], nth("cb_done", c + 1))
                    cbv = A[:, 0, (c % 2) * 256:(c % 2 + 1) * 256].rearrange("p (g n) -> p g n", g=2)
                    for n, mask in enumerate((upper, lower)):
                        at = (c % 2) * HALF + n * 256
                        m = tt(rows[:, at:at + 256].rearrange("p (g n) -> p g n", g=2), cbv,
                               mask[:, :].unsqueeze(1).broadcast_to([P, 2, P]), ALU.mult)
                    m.then_inc(S["cb_out"], 1)

                def gated(c):
                    dve.wait_ge(S["yt_done"], nth("yt_done", c + 1))
                    for g in range(GROUPS):
                        zv = arena[:, Z + 4 * g:Z + 4 * g + 4, c * P:(c + 1) * P]
                        m = tt(zv, A[:, 1 + g, :].rearrange("p (k n) -> p k n", k=4), zv, ALU.mult)
                    m.then_inc(S["yt_out"], 1)

                def with_skip(c):
                    dve.wait_ge(S["xd_ready"], nth("xd_ready", c + 1))
                    dve.wait_ge(S["yd_done"], nth("yd_done", 2 * c + 2))
                    tt(yb, gg, yb, ALU.add).then_inc(S["y_ready"], 1)

                masked(0)
                for i in range(2 * TT):
                    c, g = divmod(i, 2)
                    E, W = t(2 * g), t(2 * g + 1)
                    dve.wait_ge(S["pre_e"], nth("pre_e", i + 1))
                    for h in range(GH):
                        n = g * GH + h
                        eh = E[:, h * P:(h + 1) * P]
                        m = stt(eh, bc(g, 1)[:, h, :], scal[:, c, 80 + n:81 + n], eh, ALU.subtract, ALU.min)
                    m.then_inc(S["e_ready"], 1)
                    if g and c:
                        gated(c - 1)
                    dve.wait_ge(S["pre_w"], nth("pre_w", i + 1))
                    for h in range(GH):
                        n = g * GH + h
                        wh, up = W[:, h * P:(h + 1) * P], (c % 2) * HALF + g * P
                        m = stt(wh, rows[:, up:up + P], scal[:, c, n:n + 1], wh, ALU.mult, ALU.add)
                    m.then_inc(S["dve_step"], 1)
                    w_step = step()
                    if g == 0:
                        if c < TT - 1:
                            masked(c + 1)
                        if c:
                            with_skip(c - 1)
                    else:
                        if c:
                            dve.wait_ge(S["yof_done"], nth("yof_done", c))
                            m = tt(heads(arena[:, SB + c - 1, :]), heads(g23), per_head(ecs, c, 0), ALU.mult)
                            m.then_inc(S["f_read"], 1)
                        if c < TT - 1:
                            dve.wait_ge(S["yob_done"], nth("yob_done", c + 1))
                            m = tt(heads(arena[:, SB + c, :]), heads(a12), per_head(ecs, c, 1), ALU.mult)
                            m.then_inc(S["fb_ready"], 1)
                        else:
                            dve.wait_ge(S["f_read"], nth("f_read", c))
                            dve.sem_inc(S["fb_ready"], 1)
                        if c < TT - 1:
                            if c:
                                dve.wait_ge(S["sf_scaled"], nth("sf_scaled", c))
                            dve.wait_ge(S["st_done"], nth("st_done", 7 + c + 1))
                            if c:
                                m = tt(arena[:, SF, :], g23, arena[:, SF, :], ALU.add)
                            else:
                                m = nc.vector.tensor_copy(arena[:, SF, :], g23)
                            m.then_inc(S["st_read"], 1)
                            dve.wait_ge(S["st_read"], nth("st_read", 7 + c + 1))
                    dve.wait_ge(S["dve_step"], nth("dve_step", w_step))
                    dve.wait_ge(S["e_exp"], nth("e_exp", i + 1))
                    tt(E, E, W, ALU.mult).then_inc(S["m_ready"], 1)
                with_skip(TT - 1)
                gated(TT - 1)
                split_to(UNITS_TO[B_OUT] + 3)
                nn[0] += 1
                dve.wait_ge(S["srt_done"], nth("srt_done", nn[0]))
                nc.vector.reciprocal(rst[:, :], srt[:, :]).then_inc(S["dve_step"], 1)
                dve.wait_ge(S["dve_step"], nth("dve_step", step()))
                for i in range(3 * TT):
                    m = ts(t(2 + i // TT, P, i % TT * P), ident[:, :], rst[:, i:i + 1], None, ALU.mult)
                m.then_inc(S["diag_done"], 1)
                dve.wait_ge(S["rs_done"], nth("rs_done", 1))
                pair = lambda banks: banks.rearrange("p a n -> p (a n)")
                norm_split([(Q + k, col("attn", k), rs) for k in range(4)]
                           + [(Z + k, col("ssd", k), pair(A[:, 0:2, :] if k < 4 else A[:, 2:4, :])) for k in range(KD)],
                           MIX_HI, MIX_LO)
                nsq = [KD + 4]

                def add_squares(k, total, part):
                    nsq[0] += 1
                    dve.wait_ge(S["sq_done"], nth("sq_done", nsq[0]))
                    dve.wait_ge(S["sq_used"], nth("sq_used", nsq[0] - 1))
                    if k == 0:
                        dve.sem_inc(S["sq_used"], 1)
                    else:
                        tt(total, total, part(nsq[0] % 2), ALU.add).then_inc(S["sq_used"], 1)

                for j in range(OUT_BLOCKS):
                    split_to(uend(B_OUT + j) + 2)
                    if j < KD - 1:
                        add_squares(j, t(2), t)
                split_to(UNITS_TO[B_GU] + 3)
                inverse = inverse_root(t(7))
                dve.wait_ge(S["x_back"], nth("x_back", 32))
                for k in range(KD):
                    stt(arena[:, Z + k, :], arena[:, Z + k, :], col("mix_post", k), inverse, ALU.mult, ALU.mult).then_inc(S["dve_step"], 1)
                    dve.wait_ge(S["dve_step"], nth("dve_step", step()))
                    tt(arena[:, RAW + k, :], x_back(k), arena[:, Z + k, :], ALU.add).then_inc(S["norm_applied"], 1)
                    applied[0] += 1
                inverse = inverse_root(t(7))
                norm_split([(RAW + k, col("ffn_pre", k), inverse) for k in range(KD)], h_hi, h_lo)
                dve.wait_ge(S["x1_saved"], nth("x1_saved", 16))
                for p in range(FK):
                    cv, gt = t(4), lambda i: t(2, T, i)
                    w = lambda i: prm[:, PC["fconv_w"] + 3 * p + i:PC["fconv_w"] + 3 * p + i + 1]
                    split_to(uend(B_GU + 2 * p) + 2)
                    dve.wait_ge(S["gate_copied"], nth("gate_copied", p + 1))
                    dve.wait_ge(S["gelu_done"], nth("gelu_done", p))
                    ts(cv, gt(0), w(0), prm[:, PC["fconv_b"] + p:PC["fconv_b"] + p + 1], ALU.mult, ALU.add).then_inc(S["dve_step"], 1)
                    dve.wait_ge(S["dve_step"], nth("dve_step", step()))
                    stt(cv, gt(1), w(1), cv, ALU.mult, ALU.add).then_inc(S["dve_step"], 1)
                    dve.wait_ge(S["dve_step"], nth("dve_step", step()))
                    stt(cv, gt(2), w(2), cv, ALU.mult, ALU.add).then_inc(S["gate_conv"], 1)
                    split_to(uend(B_GU + 2 * p) + 3)
                    dve.wait_ge(S["gelu_done"], nth("gelu_done", p + 1))
                    split_to(uend(B_GU + 2 * p) + 4)
                    dve.wait_ge(S["weights_used"], nth("weights_used", uend(B_GU + 2 * p + 1)))
                    tt(f_full(p), rs, t(1), ALU.mult).then_inc(S["f_ready"], 1)
                for half in range(2):
                    for k in range(FK):
                        split_to(down_ahead(half, k))
                        dve.wait_ge(S["fhi_done"], nth("fhi_done", half * FK + k + 1))
                        cs = slice(half * HALF, (half + 1) * HALF)
                        tt(f_r(k, cs), f_full(k, cs), fhi(k).bitcast(F),
                           ALU.subtract).then_inc(S["flo_done"], 1)
                    if half == 0:
                        nsq[0] += 1 + KD
                        for j in range(KD - 1):
                            split_to(uend(B_DOWN + j) + 2)
                            add_squares(j, t(1, HALF), lambda i: t(0, HALF, i * HALF))
                        split_to(UNITS_TO[B_DOWN + KD])
                        nsq[0] += 1
                later = lambda j: add_squares(j, t(1, HALF, HALF), lambda i: t(0, HALF, i * HALF))
                for half in range(2):
                    if half:
                        for j in (5, 6):
                            split_to(uend(B_DOWN + KD + j) + 2)
                            later(j)
                    split_to(uend(B_DOWN + KD) + 2 if half == 0 else UNITS_W)
                    hs = slice(half * HALF, (half + 1) * HALF)
                    inverse = inverse_root(t(2, HALF, half * HALF))
                    dve.wait_ge(S["x1_back"], nth("x1_back", 32 * KD))
                    for k in range(KD):
                        o = o_chunk(k)[:, hs]
                        stt(o, o, col("ffn_post", k), inverse, ALU.mult, ALU.mult).then_inc(S["dve_step"], 1)
                        dve.wait_ge(S["dve_step"], nth("dve_step", step()))
                        tt(o, o, x1_part(k, half), ALU.add).then_inc(S["norm_applied"], 1)
                        if half == 0:
                            split_to(uend(B_DOWN + KD) + 2 + 3 * (k + 1))
                            if k == 0:
                                later(0)
                            elif k % 2:
                                later((k + 1) // 2)
                assert links[0] == DVE_LINKS, links[0]

        @block.gpsimd
        def _(pool):
            n = [0]

            def const(ins):
                n[0] += 1
                ins.then_inc(S["const"], 1)
                pool.wait_ge(S["const"], n[0])

            sel = nc.gpsimd.affine_select
            for name in STARTED:
                pool.sem_inc(S[name], 1)
                pool.sem_inc(S["started"], 1)
            const(nc.gpsimd.memset(ones[:, :], 1.0))
            const(nc.gpsimd.memset(qb[:, :, :], 0.0))
            const(nc.gpsimd.memset(epsc[:, :], EPS))
            const(nc.gpsimd.memset(t(4), 0.0))
            const(nc.gpsimd.memset(ident[:, :], 0.0))
            const(sel(out=ident[:, :], in_=ident[:, :], compare_op=ALU.not_equal, fill=1.0, base=0, pattern=[[-1, P]], channel_multiplier=1))
            const(sel(out=upper[:, :], in_=ones[:, :], compare_op=ALU.is_ge, fill=0.0, base=0, pattern=[[1, P]], channel_multiplier=-1))
            const(sel(out=lower[:, :], in_=ones[:, :], compare_op=ALU.is_ge, fill=0.0, base=0, pattern=[[-1, P]], channel_multiplier=1))
            pool.dma_start(pad_dram, t(4, 127)[0:HEADS * 15]).then_inc(S["rpb_pad"], 16)
            pool.dma_start(skp[:, :], bass.AP(skip.tensor, 0, [[0, P], [1, SH]])).then_inc(S["rpb_pad"], 16)
            pool.wait_ge(S["rpb_pad"], 32)
            pool.dma_start(pad_dram[:, 48:79], rpb).then_inc(S["rpb_pad"], 16)
            pool.wait_ge(S["rpb_pad"], 48)
            for h in range(HEADS):
                pool.dma_start(bass.AP(bias_dram.tensor, h * 64 * 960, [[64, 15], [960, 64], [1, 64]]),
                               bass.AP(pad_dram.tensor, h * 15 * 127 + 63, [[127, 15], [-1, 64], [1, 64]])).then_inc(S["table_read"], 16)
            pool.wait_ge(S["table_read"], 16 * HEADS)
            pool.dma_start(arena[:, K:K + PAIRS, 0:960], bias_dram.rearrange("a p n -> p a n")).then_inc(S["table_read"], 16)
            pool.wait_ge(S["table_read"], 16 * HEADS + 16)
            for h in range(HEADS):
                v = arena[(h % 2) * 64:(h % 2) * 64 + 64, K + h // 2, 0:960].rearrange("p (a n) -> p a n", a=15)
                sel(out=v[:, :, 0:48], in_=v[:, :, 0:48], compare_op=ALU.is_ge, fill=MASKED, base=WIN_COLS // 2,
                    pattern=[[0, 15], [1, 48]], channel_multiplier=-1).then_inc(S["table_masked"], 1)
                pool.wait_ge(S["table_masked"], 2 * h + 1)
                sel(out=v[:, :, 16:64], in_=v[:, :, 16:64], compare_op=ALU.is_ge, fill=MASKED, base=WIN_COLS // 2 - 1 - 16,
                    pattern=[[0, 15], [-1, 48]], channel_multiplier=1).then_inc(S["table_masked"], 1)
                pool.wait_ge(S["table_masked"], 2 * h + 2)
            pool.dma_start(bias_dram.rearrange("a p n -> p a n"), arena[:, K:K + PAIRS, 0:960]).then_inc(S["table_saved"], 16)
            pool.wait_ge(S["table_saved"], 16)
            assert n[0] == CONSTS
            with pool.Fori(0, SEQS) as s:
                def nth(name, k):
                    return s * PER[name] + k + start(name, k)

                def settled():
                    pool.sem_inc(S["settled"], 1)

                pool.wait_ge(S["xt_out"], nth("xt_out", 16))
                settled()
                pool.dma_start(x_dram, arena[:, RAW:RAW + KD, :]).then_inc(S["raw_saved"], 16)
                settled()
                for i in (2, 3):
                    nc.gpsimd.memset(t(i, 2), 0.0)
                    m = nc.gpsimd.memset(t(i, 2, 1026), 0.0)
                m.then_inc(S["pads"], 1)
                pool.wait_ge(S["v_out"], nth("v_out", TT))
                pool.wait_ge(S["o_done"], nth("o_done", 0))
                settled()
                pool.dma_start(v_dram.rearrange("(i p) n -> p i n", p=P),
                               arena[:, VK:VK + 4, :].rearrange("p a (b n) -> p (a b) n", b=2)).then_inc(S["v_saved"], 16)

                def save_z(k, m, i):
                    pool.wait_ge(S["silu_done"], nth("silu_done", i + 1))
                    settled()
                    pool.dma_start(z_dram[:, k, :], t(2 + m % 2, T, 2)).then_inc(S[f"z_saved{m % 2}"], 16)

                def load_v(hp):
                    cols = slice(hp * P, (hp + 1) * P)
                    settled()
                    pool.dma_start(v_even, v_dram[:, cols].rearrange("(i p) n -> p i n", p=P)).then_inc(S["v_in"], 16)
                    settled()
                    pool.dma_start(v_odd, v_dram[64:64 + 7 * P, cols].rearrange("(i p) n -> p i n", p=P)).then_inc(S["v_in"], 16)

                def load_table(hp):
                    settled()
                    pool.dma_start(table, bias_dram[hp]).then_inc(S["tb_in"], 16)

                for i in range(2):
                    save_z(i, i, i)
                pool.wait_ge(S["v_saved"], nth("v_saved", 16))
                pool.wait_ge(S["rows_ready"], nth("rows_ready", 1))
                load_v(0)
                load_table(0)
                pool.dma_start(cs_dram[0], rows[32:64, :]).then_inc(S["rows_saved"], 16)
                pool.dma_start(cs_dram[1], rows[64:96, :]).then_inc(S["rows_saved"], 16)
                save_z(2, 2, 2)
                for st in range(UNITS):
                    hp, r = divmod(st, ROWS)
                    if st == 2:
                        save_z(3, 3, 3)
                    if hp and r == 1:
                        pool.wait_ge(S["s_biased"], nth("s_biased", st - 1))
                        load_table(hp)
                    if hp and r == 2:
                        pool.wait_ge(S["o_done"], nth("o_done", st - 2))
                        load_v(hp)
                    pool.wait_ge(S["s_done"], nth("s_done", max(0, st - 1)))
                    if st == 0:
                        pool.wait_ge(S["pads"], nth("pads", 1))
                    settled()
                    for hh in range(2):
                        m = nc.gpsimd.tensor_copy(qb[hh * 64:(hh + 1) * 64, st % 2, hh * 64:(hh + 1) * 64],
                                                  arena[hh * 64:(hh + 1) * 64, Q + hp, r * 64:(r + 1) * 64])
                    m.then_inc(S["q_ready"], 1)
                    if st % 16 == 5 and st > 16:
                        save_z(3 + st // 16, 3, 4 * (st // 16) + 3)
                save_z(7, 3, 19)
                pool.wait_ge(S["in_copied"], nth("in_copied", IN_BLOCKS))
                for i in range(2):
                    pool.wait_ge(S[f"z_saved{i}"], nth(f"z_saved{i}", 16 * Z_SAVES[i]))
                settled()
                pool.dma_start(arena[:, Z:Z + KD, :], z_dram).then_inc(S["z_back"], 16)
                pool.wait_ge(S["coef_out"], nth("coef_out", 1))

                def weighted(c, d, to):
                    nc.gpsimd.tensor_tensor(arena[:, to, :].rearrange("p (h n) -> p h n", h=SH),
                                            arena[:, H + c, :].rearrange("p (h n) -> p h n", h=SH),
                                            wst[:, c, d * SH:(d + 1) * SH].unsqueeze(2).broadcast_to([P, SH, SP_]),
                                            ALU.mult).then_inc(S["xw_ready"], 1)

                for i, c in enumerate(range(TT - 1, 0, -1)):
                    if i >= 2:
                        pool.wait_ge(S["st_done"], nth("st_done", i - 1))
                    weighted(c, 1, (XW, YBUF)[i % 2])
                pool.wait_ge(S["st_done"], nth("st_done", 7))
                for c in range(TT):
                    if c < TT - 1:
                        if c:
                            pool.wait_ge(S["st_done"], nth("st_done", 7 + c))
                        weighted(c, 0, XW)
                    if c:
                        pool.wait_ge(S["yt_done"], nth("yt_done", c))
                    nc.gpsimd.tensor_tensor(arena[:, YBUF, :].rearrange("p (h n) -> p h n", h=SH),
                                            arena[:, H + c, :].rearrange("p (h n) -> p h n", h=SH),
                                            skp[:, :].unsqueeze(2).broadcast_to([P, SH, SP_]), ALU.mult).then_inc(S["xd_ready"], 1)
                    if 0 < c < TT - 1:
                        pool.wait_ge(S["yof_done"], nth("yof_done", c))
                        nc.gpsimd.tensor_tensor(arena[:, SF, :].rearrange("p (h n) -> p h n", h=SH),
                                                arena[:, SF, :].rearrange("p (h n) -> p h n", h=SH),
                                                dtot[:, c, 0:SH].unsqueeze(2).broadcast_to([P, SH, SP_]),
                                                ALU.mult).then_inc(S["sf_scaled"], 1)
                pool.wait_ge(S["norm_applied"], nth("norm_applied", 20))
                settled()
                pool.dma_start(arena[:, K:K + 4, :], x_dram[:, 0:4, :]).then_inc(S["x_back"], 16)
                pool.dma_start(tmp[:, 3 * 1028:7 * 1028].rearrange("p (k n) -> p k n", k=4)[:, :, 0:T], x_dram[:, 4:8, :]
                               ).then_inc(S["x_back"], 16)
                pool.wait_ge(S["norm_applied"], nth("norm_applied", 28))
                settled()
                pool.dma_start(x1_dram, arena[:, RAW:RAW + KD, :]).then_inc(S["x1_saved"], 16)
                nc.gpsimd.memset(t(2, 1), 0.0)
                nc.gpsimd.memset(t(2, 1, 1025), 0.0).then_inc(S["pads"], 1)
                pool.wait_ge(S["weights_used"], nth("weights_used", UNITS_TO[B_DOWN + KD]))
                settled()
                for k in range(KD):
                    for h in range(2):
                        pool.dma_start(x1_part(k, h), x1_dram[:, k, h * HALF:(h + 1) * HALF]).then_inc(S["x1_back"], 16)
                for n in range(16):
                    half, g, tile = n // 8, n // 4 % 2, n % 4
                    pool.wait_ge(S["yo_copied"], nth("yo_copied", n + 1))
                    settled()
                    rows_ = slice(half * HALF + tile * P, half * HALF + (tile + 1) * P)
                    pool.dma_start(y[bass.ds(s, 1), rows_, g * HALF:(g + 1) * HALF].rearrange("a p n -> (a p) n"),
                                   y_part(n)).then_inc(S["y_saved"], 16)
                pool.wait_ge(S["y_saved"], nth("y_saved", 16 * 16))
                pool.sem_inc(S["sequence_saved"], 1)
            pool.wait_ge(S["x1_saved"], 16 * SEQS)


def tiled(w):
    k, n = w.shape
    return w.reshape(k // P, P, n // P, P).transpose(2, 1, 0, 3).reshape(n // P, P, k)


def by_channel(a):
    a = a.reshape(-1, a.shape[-1] // P, P)
    return a.transpose(2, 1, 0).reshape(P, -1)


def kernel(**inputs):
    import numpy as np
    import concourse.bacc as bacc
    from concourse.bass_utils import run_bass_kernel_spmd

    a = {k: np.asarray(v) for k, v in inputs.items()}
    w_in = a["w_in"][0]
    blocks = tiled(np.pad(w_in, ((0, 0), (0, P - 32))))
    order = list(range(12)) + [32] + list(range(12, 16))
    for i in range(4):
        order += [20 + 3 * i, 21 + 3 * i, 22 + 3 * i, 16 + i]
    pad = np.zeros(P - 32, np.float32)
    prm = np.concatenate([
        by_channel(a["norm_mix_pre"][0]), by_channel(a["norm_mix_post"][0]), by_channel(a["attn_out_norm"][0]),
        by_channel(a["ssd_norm"][0]), by_channel(a["norm_ffn_pre"][0]), by_channel(a["norm_ffn_post"][0]),
        by_channel(a["ssd_conv_w"][0]), by_channel(a["ssd_conv_b"][0]), by_channel(a["ffn_conv_w"][0]),
        by_channel(a["ffn_conv_b"][0]),
        np.concatenate([a["ssd_dt_bias"][0].reshape(-1), pad])[:, None],
        np.concatenate([a["ssd_a_log"][0].reshape(-1), pad])[:, None]], axis=1)
    gate, up = tiled(a["w_gate"][0]), tiled(a["w_up"][0])
    arrays = {
        "x": np.concatenate([a["x_prompt"], a["x_sample"]]),
        "w_in_tiles": blocks[order],
        "w_out_tiles": tiled(a["w_out"][0]),
        "w_gu_tiles": np.stack([gate, up], axis=1).reshape(GU_BLOCKS, P, D),
        "w_down_tiles": tiled(a["w_down"][0]),
        "params": prm,
        "skip": a["ssd_d"][0],
        "rpb": a["attn_rpb"][0].reshape(HEADS * 15, 31),
    }
    arrays = {k: np.ascontiguousarray(v) for k, v in arrays.items()}
    nc = bacc.Bacc("TRN2", target_bir_lowering=False, num_devices=1)
    nc.disable_value_cache = True
    args = [nc.dram_tensor(k, v.shape, mybir.dt.from_np(v.dtype), kind="ExternalInput").ap() for k, v in arrays.items()]
    out = nc.dram_tensor("y", (SEQS, T, D), mybir.dt.float32, kind="ExternalOutput").ap()
    encoder(nc, *args, out)
    r = run_bass_kernel_spmd(nc, [arrays], core_ids=[0])
    y = r.results[0]["y"]
    return y[0:1], y[1:2]
```
